# Optimizing a Trainium2 kernel written in Bass

```python
import math
import jax, jax.numpy as jnp
from jax import lax
import numpy as np

D_MODEL = 2048
BATCH = 1
SEQ = 256
DEPTH = 1

CHUNK = 64
LEFT_CHUNKS = 8
BAND = LEFT_CHUNKS + 1
N_HEADS = 16
HEAD_DIM = 64
ATTN_WIDTH = N_HEADS * HEAD_DIM
MAX_REL = 128
POOL_WINDOWS = (2, 4, 8, 16)
N_POOL_GROUPS = len(POOL_WINDOWS)
POOL_WIDTH = D_MODEL // 2
POOL_GROUP = POOL_WIDTH // N_POOL_GROUPS
IN_WIDTH = 3 * ATTN_WIDTH + POOL_WIDTH + 2 * D_MODEL
D_FF = ((8 * D_MODEL + 3 * 256 - 1) // (3 * 256)) * 256
EPS = 1e-6
NEG_INF = -1e30


def rms_norm(x, g):
    xf = x.astype(jnp.float32)
    y = xf * lax.rsqrt(jnp.mean(xf * xf, axis=-1, keepdims=True) + EPS)
    return (y * g.astype(jnp.float32)).astype(x.dtype)

def chunked_rel_attention(q, k, v, rel_bias):
    B, S, _ = q.shape
    nc = S // CHUNK
    qc = q.reshape(B, nc, CHUNK, N_HEADS, HEAD_DIM)
    pad = ((0, 0), (LEFT_CHUNKS * CHUNK, 0), (0, 0))
    kp = jnp.pad(k, pad).reshape(B, nc + LEFT_CHUNKS, CHUNK, N_HEADS, HEAD_DIM)
    vp = jnp.pad(v, pad).reshape(B, nc + LEFT_CHUNKS, CHUNK, N_HEADS, HEAD_DIM)
    band_idx = jnp.arange(nc)[:, None] + jnp.arange(BAND)[None, :]
    kb = kp[:, band_idx].reshape(B, nc, BAND * CHUNK, N_HEADS, HEAD_DIM)
    vb = vp[:, band_idx].reshape(B, nc, BAND * CHUNK, N_HEADS, HEAD_DIM)
    scale = 1.0 / math.sqrt(HEAD_DIM)
    s = jnp.einsum('bnihd,bnjhd->bhnij', qc, kb).astype(jnp.float32) * scale
    i = jnp.arange(CHUNK)
    j = jnp.arange(BAND * CHUNK)
    dist = LEFT_CHUNKS * CHUNK + i[:, None] - j[None, :]
    rel_idx = jnp.clip(dist, -MAX_REL, MAX_REL) + MAX_REL
    bias = rel_bias.astype(jnp.float32)[:, rel_idx]
    key_pos = (jnp.arange(nc)[:, None] - LEFT_CHUNKS) * CHUNK + j[None, :]
    valid = key_pos >= 0
    s = s + bias[None, :, None]
    s = jnp.where(valid[None, None, :, None, :], s, NEG_INF)
    p = jax.nn.softmax(s, axis=-1).astype(v.dtype)
    o = jnp.einsum('bhnij,bnjhd->bnihd', p, vb)
    return o.reshape(B, S, ATTN_WIDTH)

def multiscale_pool(u, pool_w, pool_scale):
    B, S, _ = u.shape
    uf = u.astype(jnp.float32)
    cs = jnp.concatenate([jnp.zeros((B, 1, POOL_WIDTH), jnp.float32),
                          jnp.cumsum(uf, axis=1)], axis=1)
    t = jnp.arange(S)
    outs = []
    for g, w in enumerate(POOL_WINDOWS):
        sl = slice(g * POOL_GROUP, (g + 1) * POOL_GROUP)
        lo = jnp.maximum(t + 1 - w, 0)
        cnt = (t + 1 - lo).astype(jnp.float32)[None, :, None]
        mean = (cs[:, 1:, sl] - cs[:, lo, sl]) / cnt
        outs.append(mean - uf[..., sl])
    d = jnp.stack(outs, axis=2).astype(u.dtype)
    y = jnp.einsum('bsgc,gce->bsge', d, pool_w).reshape(B, S, POOL_WIDTH)
    return y * pool_scale

def swiglu(h, w_gate_up, w_down):
    gu = h @ w_gate_up
    gate, up = gu[..., :D_FF], gu[..., D_FF:]
    return (jax.nn.silu(gate) * up) @ w_down

def first_inputs(seed: int = 0) -> dict:
    key = jax.random.key(seed)
    ks = jax.random.split(key, 16)
    f32 = jnp.float32

    def nrm(k, shape, fan_in):
        return jax.random.normal(k, shape, f32) * (fan_in ** -0.5)

    def gain(k, shape):
        return 1.0 + 0.02 * jax.random.normal(k, shape, f32)

    return {
        "x": jax.random.normal(ks[0], (BATCH, SEQ, D_MODEL), f32),
        "norm_mix": gain(ks[1], (DEPTH, D_MODEL)),
        "w_in": nrm(ks[2], (DEPTH, D_MODEL, IN_WIDTH), D_MODEL),
        "rel_bias": 0.1 * jax.random.normal(ks[3], (DEPTH, N_HEADS, 2 * MAX_REL + 1), f32),
        "pool_w": nrm(ks[4], (DEPTH, N_POOL_GROUPS, POOL_GROUP, POOL_GROUP), POOL_GROUP),
        "pool_scale": gain(ks[5], (DEPTH, POOL_WIDTH)),
        "w_branch_a": nrm(ks[6], (DEPTH, ATTN_WIDTH, D_MODEL), ATTN_WIDTH),
        "w_branch_b": nrm(ks[7], (DEPTH, POOL_WIDTH, D_MODEL), POOL_WIDTH),
        "w_out": nrm(ks[8], (DEPTH, D_MODEL, D_MODEL), D_MODEL),
        "norm_ffn": gain(ks[9], (DEPTH, D_MODEL)),
        "w_gate_up": nrm(ks[10], (DEPTH, D_MODEL, 2 * D_FF), D_MODEL),
        "w_down": nrm(ks[11], (DEPTH, D_FF, D_MODEL), D_FF),
        "norm_final": gain(ks[12], (D_MODEL,)),
    }

def first_block(x, norm_mix, w_in, rel_bias, pool_w, pool_scale, w_branch_a, w_branch_b,
              w_out, norm_ffn, w_gate_up, w_down, norm_final):
    a0 = 3 * ATTN_WIDTH
    a1 = a0 + POOL_WIDTH
    a2 = a1 + D_MODEL
    for l in range(DEPTH):
        h = rms_norm(x, norm_mix[l])
        z = h @ w_in[l]
        q = z[..., :ATTN_WIDTH]
        k = z[..., ATTN_WIDTH:2 * ATTN_WIDTH]
        v = z[..., 2 * ATTN_WIDTH:a0]
        u = z[..., a0:a1]
        gate_a = jax.nn.sigmoid(z[..., a1:a2])
        gate_b = jax.nn.sigmoid(z[..., a2:])
        y_a = chunked_rel_attention(q, k, v, rel_bias[l])
        y_b = multiscale_pool(u, pool_w[l], pool_scale[l])
        merged = gate_a * (y_a @ w_branch_a[l]) + gate_b * (y_b @ w_branch_b[l])
        x = x + merged @ w_out[l]
        x = x + swiglu(rms_norm(x, norm_ffn[l]), w_gate_up[l], w_down[l])
    return rms_norm(x, norm_final)


D_MIX = D_MODEL
NSA_HEADS = 8
NSA_KV_HEADS = 2
NSA_GROUP = NSA_HEADS // NSA_KV_HEADS
NSA_HEAD_DIM = 128
NSA_WIDTH = NSA_HEADS * NSA_HEAD_DIM
NSA_KV_WIDTH = NSA_KV_HEADS * NSA_HEAD_DIM
CMP_BLOCK = 32
CMP_STRIDE = 16
SLC_BLOCK = 64
SLC_TOP_N = 16
WINDOW = 512
SLC_QBLK = 64
WIN_QBLK = 128
RWKV_WIDTH = D_MIX - NSA_WIDTH
RWKV_HEAD_DIM = 64
RWKV_HEADS = RWKV_WIDTH // RWKV_HEAD_DIM
DECAY_LORA = 64
AAA_LORA = 64
SHIFT_COLS = 3 * RWKV_WIDTH + DECAY_LORA + AAA_LORA
NUM_BUCKETS = 32
MAX_DISTANCE = 1024
NORM_EPS = 1e-6
RWKV_GN_EPS = 64e-5
COL_Q = NSA_WIDTH
COL_KV = 6 * NSA_KV_WIDTH
COL_GATE = 3 * NSA_HEADS
COL_ZA = NSA_WIDTH
COL_ZB = RWKV_WIDTH
IN_COLS = COL_Q + COL_KV + COL_GATE + COL_ZA + SHIFT_COLS + COL_ZB


def rms_norm_2(x, g):
    xf = x.astype(jnp.float32)
    y = xf * lax.rsqrt(jnp.mean(xf * xf, axis=-1, keepdims=True) + NORM_EPS)
    return (y * g.astype(jnp.float32)).astype(x.dtype)

def rel_bucket(dist):
    n = jnp.maximum(dist, 0)
    max_exact = NUM_BUCKETS // 2
    nf = jnp.maximum(n, 1).astype(jnp.float32)
    large = max_exact + (jnp.log(nf / max_exact) / math.log(MAX_DISTANCE / max_exact)
                         * (NUM_BUCKETS - max_exact)).astype(jnp.int32)
    large = jnp.minimum(large, NUM_BUCKETS - 1)
    return jnp.where(n < max_exact, n, large)

def masked_softmax(logits, mask, axis):
    logits = jnp.where(mask, logits, -jnp.inf)
    m = jnp.max(logits, axis=axis, keepdims=True)
    m = jnp.where(jnp.isfinite(m), m, 0.0)
    e = jnp.where(mask, jnp.exp(logits - m), 0.0)
    s = jnp.sum(e, axis=axis, keepdims=True)
    return e / jnp.maximum(s, 1e-30)

def compress(kv, pos, w1, w2):
    B, S, G, D = kv.shape
    n_cmp = (S - CMP_BLOCK) // CMP_STRIDE + 1
    idx = jnp.arange(n_cmp)[:, None] * CMP_STRIDE + jnp.arange(CMP_BLOCK)[None, :]
    blocks = kv[:, idx] + pos[None, None, :, None, :]
    flat = blocks.transpose(0, 1, 3, 2, 4).reshape(B, n_cmp, G, CMP_BLOCK * D)
    return jax.nn.silu(flat @ w1) @ w2

def nsa_mixer(q, k_cmp, v_cmp, k_slc, v_slc, k_win, v_win, gates, rel_bias_table,
              cmp_pos_k, cmp_pos_v, cmp_k_w1, cmp_k_w2, cmp_v_w1, cmp_v_w2):
    f32 = jnp.float32
    B, S = q.shape[:2]
    G, HG, D = NSA_KV_HEADS, NSA_GROUP, NSA_HEAD_DIM
    qf = q.astype(f32).reshape(B, S, G, HG, D) * (D ** -0.5)
    t = jnp.arange(S)
    table = rel_bias_table.astype(f32)

    kc = compress(k_cmp.astype(f32).reshape(B, S, G, D), cmp_pos_k.astype(f32),
                  cmp_k_w1.astype(f32), cmp_k_w2.astype(f32))
    vc = compress(v_cmp.astype(f32).reshape(B, S, G, D), cmp_pos_v.astype(f32),
                  cmp_v_w1.astype(f32), cmp_v_w2.astype(f32))
    n_cmp = kc.shape[1]
    blk_end = jnp.arange(n_cmp) * CMP_STRIDE + CMP_BLOCK - 1
    dist_c = t[:, None] - blk_end[None, :]
    mask_c = dist_c >= 0
    bias_c = table[rel_bucket(dist_c)].reshape(S, n_cmp, G, HG).transpose(2, 3, 0, 1)
    logits_c = jnp.einsum('bsghd,bigd->bghsi', qf, kc) + bias_c
    p_c = masked_softmax(logits_c, mask_c, -1)
    o_c = jnp.einsum('bghsi,bigd->bsghd', p_c, vc)

    n_blk = S // SLC_BLOCK
    cmp_start = jnp.arange(n_cmp) * CMP_STRIDE
    slc_start = jnp.arange(n_blk) * SLC_BLOCK
    overlap = ((cmp_start[:, None] < slc_start[None, :] + SLC_BLOCK)
               & (cmp_start[:, None] + CMP_BLOCK > slc_start[None, :])).astype(f32)
    imp = jnp.einsum('bghsi,ij->bgsj', p_c, overlap)
    cur = t // SLC_BLOCK
    j = jnp.arange(n_blk)
    forced = (j[None, :] == 0) | (j[None, :] == cur[:, None]) | (j[None, :] == cur[:, None] - 1)
    causal_blk = j[None, :] <= cur[:, None]
    score = jnp.where(forced, jnp.inf, jnp.where(causal_blk, imp, -jnp.inf))
    n_sel = min(SLC_TOP_N, n_blk)
    _, sel_idx = lax.top_k(score, n_sel)

    kb = k_slc.astype(f32).reshape(B, n_blk, SLC_BLOCK, G, D).transpose(0, 3, 1, 2, 4)
    vb = v_slc.astype(f32).reshape(B, n_blk, SLC_BLOCK, G, D).transpose(0, 3, 1, 2, 4)
    nqb = S // SLC_QBLK
    q_blocks = qf.reshape(B, nqb, SLC_QBLK, G, HG, D).transpose(1, 0, 2, 3, 4, 5)
    idx_blocks = sel_idx.reshape(B, G, nqb, SLC_QBLK, n_sel).transpose(2, 0, 1, 3, 4)
    t_blocks = t.reshape(nqb, SLC_QBLK)
    b_ix = jnp.arange(B)[:, None, None, None]
    g_ix = jnp.arange(G)[None, :, None, None]
    g_ix5 = jnp.arange(G)[None, :, None, None, None]
    tab = table.reshape(NUM_BUCKETS, G, HG)

    def slc_block(args):
        qb, ib, tb = args
        kg = kb[b_ix, g_ix, ib]
        vg = vb[b_ix, g_ix, ib]
        s_pos = ib[..., None] * SLC_BLOCK + jnp.arange(SLC_BLOCK)
        dist = tb[None, None, :, None, None] - s_pos
        valid_blk = ib <= (tb // SLC_BLOCK)[None, None, :, None]
        mask = (dist >= 0) & valid_blk[..., None]
        bias = tab[rel_bucket(dist), g_ix5]
        logits = jnp.einsum('bqghd,bgqnkd->bgqnkh', qb, kg) + bias
        m_tok = n_sel * SLC_BLOCK
        logits = logits.reshape(B, G, SLC_QBLK, m_tok, HG)
        p = masked_softmax(logits, mask.reshape(B, G, SLC_QBLK, m_tok)[..., None], -2)
        return jnp.einsum('bgqmh,bgqmd->bqghd', p, vg.reshape(B, G, SLC_QBLK, m_tok, D))

    o_s = lax.map(slc_block, (q_blocks, idx_blocks, t_blocks))
    o_s = o_s.transpose(1, 0, 2, 3, 4, 5).reshape(B, S, G, HG, D)

    nwb = S // WIN_QBLK
    n_pre = WINDOW // WIN_QBLK
    band = n_pre + 1
    m_win = band * WIN_QBLK
    pad = ((0, 0), (WINDOW, 0), (0, 0), (0, 0))
    kw = jnp.pad(k_win.astype(f32).reshape(B, S, G, D), pad).reshape(B, nwb + n_pre, WIN_QBLK, G, D)
    vw = jnp.pad(v_win.astype(f32).reshape(B, S, G, D), pad).reshape(B, nwb + n_pre, WIN_QBLK, G, D)
    kband = jnp.concatenate([kw[:, i:i + nwb] for i in range(band)], axis=2)
    vband = jnp.concatenate([vw[:, i:i + nwb] for i in range(band)], axis=2)
    qw = qf.reshape(B, nwb, WIN_QBLK, G, HG, D)
    tq = t.reshape(nwb, WIN_QBLK)
    s_pos = (jnp.arange(nwb) * WIN_QBLK - WINDOW)[:, None] + jnp.arange(m_win)[None, :]
    dist = tq[:, :, None] - s_pos[:, None, :]
    mask_w = (dist >= 0) & (dist < WINDOW) & (s_pos[:, None, :] >= 0)
    bias_w = table[rel_bucket(dist)].reshape(nwb, WIN_QBLK, m_win, G, HG).transpose(0, 3, 4, 1, 2)
    logits_w = jnp.einsum('bnqghd,bnmgd->bnghqm', qw, kband) + bias_w[None]
    p_w = masked_softmax(logits_w, mask_w[None, :, None, None], -1)
    o_w = jnp.einsum('bnghqm,bnmgd->bnqghd', p_w, vband).reshape(B, S, G, HG, D)

    gt = jax.nn.sigmoid(gates.astype(f32)).reshape(B, S, 3, G, HG, 1)
    o = gt[:, :, 0] * o_c + gt[:, :, 1] * o_s + gt[:, :, 2] * o_w
    return o.reshape(B, S, NSA_WIDTH)

def rwkv7_mixer(feat, mu, w0, w2, a0, a2, k_k, k_a, r_k, ln_w, ln_b):
    f32 = jnp.float32
    B, S, _ = feat.shape
    H, N, W = RWKV_HEADS, RWKV_HEAD_DIM, RWKV_WIDTH
    pf = feat.astype(f32)
    prev = jnp.pad(pf[:, :-1], ((0, 0), (1, 0), (0, 0)))
    pf = pf + mu.astype(f32) * (prev - pf)
    r, k, v, wd, ad = jnp.split(pf, [W, 2 * W, 3 * W, 3 * W + DECAY_LORA], axis=-1)
    w = -jax.nn.softplus(-(w0.astype(f32) + jnp.tanh(wd) @ w2.astype(f32))) - 0.5
    decay = jnp.exp(-jnp.exp(w))
    a = jax.nn.sigmoid(a0.astype(f32) + ad @ a2.astype(f32))
    kk = (k * k_k.astype(f32)).reshape(B, S, H, N)
    kk = kk / jnp.maximum(jnp.sqrt(jnp.sum(kk * kk, axis=-1, keepdims=True)), 1e-12)
    k = k * (1.0 + (a - 1.0) * k_a.astype(f32))
    r4, w4, k4, v4, a4 = (z.reshape(B, S, H, N) for z in (r, decay, k, v, a))
    aa = -kk
    bb = kk * a4

    def step(state, inp):
        r_t, w_t, k_t, v_t, a_t, b_t = inp
        sa = jnp.einsum('bhij,bhj->bhi', state, a_t)
        state = (state * w_t[:, :, None, :] + sa[..., None] * b_t[:, :, None, :]
                 + v_t[..., None] * k_t[:, :, None, :])
        return state, jnp.einsum('bhij,bhj->bhi', state, r_t)

    xs = tuple(z.transpose(1, 0, 2, 3) for z in (r4, w4, k4, v4, aa, bb))
    state0 = jnp.zeros((B, H, N, N), f32)
    _, y = lax.scan(step, state0, xs)
    y = y.transpose(1, 0, 2, 3)
    mean = jnp.mean(y, axis=-1, keepdims=True)
    var = jnp.mean(jnp.square(y - mean), axis=-1, keepdims=True)
    y = ((y - mean) * lax.rsqrt(var + RWKV_GN_EPS)).reshape(B, S, W) * ln_w.astype(f32) + ln_b.astype(f32)
    bonus = jnp.sum(r4 * k4 * r_k.astype(f32), axis=-1, keepdims=True) * v4
    return y + bonus.reshape(B, S, W)

def second_inputs(seed: int = 0) -> dict:
    key = jax.random.key(seed)
    ks = jax.random.split(key, 24)
    f32 = jnp.float32
    L = DEPTH
    HD = NSA_HEAD_DIM

    def nrm(k, shape, scale):
        return jax.random.normal(k, shape, f32) * scale

    return {
        'x': nrm(ks[0], (BATCH, SEQ, D_MODEL), 1.0),
        'pre_norm_g': 1.0 + nrm(ks[1], (L, D_MODEL), 0.05),
        'w_in': nrm(ks[2], (L, D_MODEL, IN_COLS), D_MODEL ** -0.5),
        'rel_bias_table': nrm(ks[3], (NUM_BUCKETS, NSA_HEADS), 0.5),
        'cmp_pos_k': nrm(ks[4], (L, CMP_BLOCK, HD), 0.1),
        'cmp_pos_v': nrm(ks[5], (L, CMP_BLOCK, HD), 0.1),
        'cmp_k_w1': nrm(ks[6], (L, CMP_BLOCK * HD, HD), (CMP_BLOCK * HD) ** -0.5),
        'cmp_k_w2': nrm(ks[7], (L, HD, HD), HD ** -0.5),
        'cmp_v_w1': nrm(ks[8], (L, CMP_BLOCK * HD, HD), (CMP_BLOCK * HD) ** -0.5),
        'cmp_v_w2': nrm(ks[9], (L, HD, HD), HD ** -0.5),
        'rwkv_mu': jax.random.uniform(ks[10], (L, SHIFT_COLS), f32),
        'rwkv_w0': jax.random.uniform(ks[11], (L, RWKV_WIDTH), f32, -6.0, -1.0),
        'rwkv_w2': nrm(ks[12], (L, DECAY_LORA, RWKV_WIDTH), 0.1),
        'rwkv_a0': nrm(ks[13], (L, RWKV_WIDTH), 0.1),
        'rwkv_a2': nrm(ks[14], (L, AAA_LORA, RWKV_WIDTH), 0.1),
        'rwkv_k_k': 0.85 + nrm(ks[15], (L, RWKV_WIDTH), 0.05),
        'rwkv_k_a': 1.0 + nrm(ks[16], (L, RWKV_WIDTH), 0.05),
        'rwkv_r_k': nrm(ks[17], (L, RWKV_HEADS, RWKV_HEAD_DIM), 0.1),
        'rwkv_ln_w': 1.0 + nrm(ks[18], (L, RWKV_WIDTH), 0.05),
        'rwkv_ln_b': nrm(ks[19], (L, RWKV_WIDTH), 0.02),
        'w_out': nrm(ks[20], (L, D_MIX, D_MODEL), D_MIX ** -0.5),
        'post_norm_g': 1.0 + nrm(ks[21], (L, D_MODEL), 0.05),
    }

def second_block(x, pre_norm_g, w_in, rel_bias_table, cmp_pos_k, cmp_pos_v, cmp_k_w1, cmp_k_w2,
              cmp_v_w1, cmp_v_w2, rwkv_mu, rwkv_w0, rwkv_w2, rwkv_a0, rwkv_a2, rwkv_k_k, rwkv_k_a,
              rwkv_r_k, rwkv_ln_w, rwkv_ln_b, w_out, post_norm_g):
    o1 = COL_Q
    o2 = o1 + COL_KV
    o3 = o2 + COL_GATE
    o4 = o3 + COL_ZA
    o5 = o4 + SHIFT_COLS
    h = x
    for l in range(DEPTH):
        hn = rms_norm_2(h, pre_norm_g[l])
        proj = hn @ w_in[l]
        q, kv6, gates, z_a, feat_b, z_b = jnp.split(proj, [o1, o2, o3, o4, o5], axis=-1)
        k_cmp, v_cmp, k_slc, v_slc, k_win, v_win = jnp.split(kv6, 6, axis=-1)
        o_a = nsa_mixer(q, k_cmp, v_cmp, k_slc, v_slc, k_win, v_win, gates, rel_bias_table,
                        cmp_pos_k[l], cmp_pos_v[l], cmp_k_w1[l], cmp_k_w2[l], cmp_v_w1[l], cmp_v_w2[l])
        o_b = rwkv7_mixer(feat_b, rwkv_mu[l], rwkv_w0[l], rwkv_w2[l], rwkv_a0[l], rwkv_a2[l],
                          rwkv_k_k[l], rwkv_k_a[l], rwkv_r_k[l], rwkv_ln_w[l], rwkv_ln_b[l])
        mix = jnp.concatenate([o_a * jax.nn.silu(z_a.astype(jnp.float32)),
                               o_b * jax.nn.silu(z_b.astype(jnp.float32))], axis=-1).astype(h.dtype)
        y = mix @ w_out[l]
        h = h + rms_norm_2(y, post_norm_g[l])
    return h


def setup_inputs(seed=0):
    out = dict(first_inputs(seed))
    for name, value in second_inputs(seed + 1).items():
        if name != "x":
            out[name + "_2"] = value
    return out


def reference(
    x, norm_mix, w_in, rel_bias, pool_w, pool_scale, w_branch_a, w_branch_b, w_out, norm_ffn,
    w_gate_up, w_down, norm_final, pre_norm_g_2, w_in_2, rel_bias_table_2, cmp_pos_k_2,
    cmp_pos_v_2, cmp_k_w1_2, cmp_k_w2_2, cmp_v_w1_2, cmp_v_w2_2, rwkv_mu_2, rwkv_w0_2,
    rwkv_w2_2, rwkv_a0_2, rwkv_a2_2, rwkv_k_k_2, rwkv_k_a_2, rwkv_r_k_2, rwkv_ln_w_2,
    rwkv_ln_b_2, w_out_2, post_norm_g_2,
):
    x = first_block(
        x, norm_mix, w_in, rel_bias, pool_w, pool_scale, w_branch_a, w_branch_b, w_out,
        norm_ffn, w_gate_up, w_down, norm_final,
    )
    return second_block(
        x, pre_norm_g_2, w_in_2, rel_bias_table_2, cmp_pos_k_2, cmp_pos_v_2, cmp_k_w1_2,
        cmp_k_w2_2, cmp_v_w1_2, cmp_v_w2_2, rwkv_mu_2, rwkv_w0_2, rwkv_w2_2, rwkv_a0_2,
        rwkv_a2_2, rwkv_k_k_2, rwkv_k_a_2, rwkv_r_k_2, rwkv_ln_w_2, rwkv_ln_b_2, w_out_2,
        post_norm_g_2,
    )


_drawn_inputs = setup_inputs


def setup_inputs(seed=0):
    import zlib

    import numpy as np

    out = dict(_drawn_inputs(seed))
    spreads = {}
    factors = {'norm_mix': 3.164,
     'rel_bias': 4.624,
     'pool_scale': 3.52,
     'cmp_pos_k_2': 27.11,
     'cmp_pos_v_2': 3.566,
     'rwkv_ln_b_2': 3.88,
     'norm_ffn': 8.0}
    for name, (base, spread) in spreads.items():
        noise = np.random.default_rng([zlib.crc32(name.encode()), seed]).standard_normal(out[name].shape)
        drawn = base * np.exp(spread * noise) if base else spread * noise
        out[name] = __import__('jax').numpy.asarray(drawn.astype(out[name].dtype))
    for name, factor in factors.items():
        out[name] = (out[name] * factor).astype(out[name].dtype)
    return out
```

```python
import math
from contextlib import ExitStack

import numpy as np

import concourse.bass as bass
from concourse import mybir

ALU = mybir.AluOpType
ACT = mybir.ActivationFunctionType
AX = mybir.AxisListType.X
F32 = mybir.dt.float32
F32R = mybir.dt.float32r

P = 128
S = 256
TT = S // P
D = 2048
KT = D // P
CC = 512
BT = 4
BLK = BT * CC
RAW_SLOTS = 4
SPLIT_SLOTS = 2
EPS = 1e-6
NEG = -1e30

AW = 1024
PW = 1024
FF = 5632
FKT = FF // P
REL = 128
HN = 8
NB = 32
NCMP = 15
C_KC, C_VC, C_KS, C_VS, C_KW, C_VW = (1024 + 256 * n for n in range(6))
C_GATE = 2560
C_ZA = 2584
C_R = 3608
C_LORA = C_R + 3072
C_ZB = 6808
N2 = 7832

B_WIN, B_MERGE, B_WOUT, B_GU, B_DOWN, B_WIN2, B_CMP, B_WOUT2 = 0, 64, 80, 96, 184, 228, 292, 296
N_BLOCKS = 312
Q_WIN, Q_MERGE, Q_WOUT, Q_GU, Q_DOWN, Q_WIN2, Q_WOUT2 = 0, 16, 24, 28, 50, 52, 68


def relative_buckets(dist):
    n = np.maximum(dist, 0)
    large = 16 + (np.log(np.maximum(n, 1).astype(np.float32) / np.float32(16))
                  / np.float32(math.log(1024 / 16)) * np.float32(16)).astype(np.int32)
    return np.where(n < 16, n, np.minimum(large, 31))


def shape_constants():
    c = {"ident": np.eye(P, dtype=np.float32)}
    z = np.arange(384)
    dist = 255 - z
    pick = np.zeros((384, 384), np.float32)
    pick[np.clip(dist, -REL, REL) + REL, z] = 1.0
    c["pick_rel"] = pick
    z = np.arange(512)
    dist = 255 - z
    pick = np.zeros((NB, 512), np.float32)
    pick[relative_buckets(dist), z] = 1.0
    c["pick_bucket"] = pick
    c["future"] = np.tile(np.where(dist < 0, NEG, 0.0).astype(np.float32), (HN, 1))
    t = np.arange(S)
    pool = np.zeros((4, S, S), np.float32)
    for g, w in enumerate((2, 4, 8, 16)):
        for tok in range(S):
            lo = max(tok + 1 - w, 0)
            pool[g, lo:tok + 1, tok] = np.float32(1.0) / np.float32(tok + 1 - lo)
            pool[g, tok, tok] -= 1.0
    c["pool_rows"] = pool
    s, q = np.arange(P)[:, None], np.arange(P)[None, :]
    chunk = s // 64 == q // 64
    strict, inclusive = (chunk & (s < q)), (chunk & (s <= q))
    masks = [strict, inclusive, strict, inclusive]
    for level in range(6):
        h = 1 << level
        masks.append((s // (2 * h) == q // (2 * h)) & (s % (2 * h) < h) & (q % (2 * h) >= h))
    masks.append(chunk)
    c["masks"] = np.stack(masks).astype(np.float32)
    return c


def program(nc, a, out):
    with ExitStack() as ctx:
        sems = {}

        def sem(name):
            if name not in sems:
                sems[name] = ctx.enter_context(nc.semaphore(name))
            return sems[name]

        BASE = 16640
        cursor = [BASE]

        def at(name, shape, dt=F32, offset=None):
            if offset is None:
                offset = cursor[0]
                size = 4 * int(np.prod(shape[1:]))
                cursor[0] += -(-size // 32) * 32
                assert cursor[0] <= 229368, (name, cursor[0])
            return nc.alloc_sbuf_tensor_at(name, shape, dt, offset=offset)

        class Region:
            def __init__(self, start, size):
                self.start, self.at, self.end = start, start, start + size

            def __call__(self, name, shape, dt=F32):
                size = -(-4 * int(np.prod(shape[1:])) // 32) * 32
                assert self.at + size <= self.end, (name, self.at + size - self.end)
                t = at(name, shape, dt, self.at)
                self.at += size
                return t

        resid = at("resid", [P, TT, D])
        XT0 = cursor[0]
        xT_hi = at("xT_hi", [P, KT, S], F32R)
        xT_lo = at("xT_lo", [P, KT, S], F32R)
        raw = at("raw", [P, RAW_SLOTS, BLK])
        w_hi = at("w_hi", [P, SPLIT_SLOTS, BLK], F32R)
        w_lo = at("w_lo", [P, SPLIT_SLOTS, BLK], F32R)
        Z0 = cursor[0]
        cursor[0] += 65536
        OY0 = cursor[0]
        cursor[0] += 16384
        ident = at("ident", [P, P])
        gains = at("gains", [P, 3, KT])
        pool_scale = at("pool_scale", [P, 8])
        par = at("par", [P, 5, 8])
        mu = at("mu", [P, 25])
        nw0a0 = at("nw0a0", [P, 2, 8])
        stats = at("stats", [P, 8])
        F0 = cursor[0]
        FSZ = 229368 - F0
        qkvu = at("qkvu", [P, TT, 4096], F32, Z0)
        gate = at("gate", [P, TT, 2 * D], F32, Z0 + 32768)
        mT_hi = at("mT_hi", [P, KT, S], F32R, Z0)
        mT_lo = at("mT_lo", [P, KT, S], F32R, Z0 + 16384)
        actT = at("actT", [P, FKT, S], F32, Z0)
        z2 = at("z2", [P, TT, N2], F32, Z0)
        scaled = at("scaled", [P, TT, D], F32, OY0)
        oy = at("oy", [P, TT, D], F32, OY0)
        r = Region(OY0, 16384)
        relb = r("relb", [P, 2, 256])
        qst = r("qst", [P, TT, P])
        kst = r("kst", [P, TT, P])
        vst = r("vst", [P, TT, P])
        qT = r("qT", [P, S])
        kT = r("kT", [P, S])
        prob = r("prob", [P, 2, 384])
        probT = r("probT", [P, 2, 384])
        r = Region(OY0, 16384)
        g_act = r("g_act", [P, TT, CC])
        h_act = r("h_act", [P, TT, CC])
        m_tmp = r("m_tmp", [P, TT, CC])
        r = Region(F0, FSZ)
        smax = r("smax", [P, 4])
        ssum = r("ssum", [P, 4])
        rowp = r("rowp", [P, 2, S])
        pwg = r("pwg", [P, 2, S])
        ust = r("ust", [P, TT, S])
        dT = r("dT", [P, 2, S])
        r = Region(Z0 + 32768, 32768)
        relT = r("relT", [P, 3, 16])
        pick_rel = r("pick_rel", [P, 3, 384])
        rel_row = r("rel_row", [16, 384])
        pick_b = r("pick_b", [NB, 512])
        future = r("future", [HN, 512])
        buck_row = r("buck_row", [HN, 512])
        tableT = r("tableT", [NB, HN])
        r = Region(F0, FSZ)
        aT_hi = r("aT_hi", [P, 2, S], F32R)
        aT_lo = r("aT_lo", [P, 2, S], F32R)
        fin_gain = at("fin_gain", [P, D], F32, XT0)
        r = Region(XT0, 32768)
        bias2 = r("bias2", [P, HN, 384])
        biasc = r("biasc", [P, HN, TT, 16])
        KTs = r("KTs", [P, 2, 2, S])
        kvcT = r("kvcT", [P, 2, 2, S])
        posT = r("posT", [P, 2, 32])
        blkA = at("blkA", [P, 32, 30], F32, OY0)
        A_hi = at("A_hi", [P, 32, 30], F32R, OY0 + 3840)
        A_lo = at("A_lo", [P, 32, 30], F32R, OY0 + 7680)
        A_hi2 = at("A_hi2", [P, 32, 30], F32R, OY0 + 11520)
        r = Region(F0, FSZ)
        pT2 = at("pT2", [P, 2, 384], F32, r.at)
        A_lo2 = r("A_lo2", [P, 32, 30], F32R)
        cw2 = r("cw2", [P, 2, P])
        hid = r("hid", [P, 2, 32])
        hexp = r("hexp", [P, 2, 32])
        kcT = r("kcT", [P, 32])
        vc = r("vc", [16, 2, P])
        gsig = r("gsig", [P, TT, 24])
        q2 = r("q2", [P, TT, P])
        q2T = r("q2T", [P, S])
        pr = r("pr", [P, 2, 384])
        prc = r("prc", [P, TT, 16])
        mx2 = r("mx2", [P, 3, TT])
        sm2 = r("sm2", [P, 3, TT])
        pcT = r("pcT", [16, S])
        r = Region(XT0, 32768)
        bv = r("bv", [P, TT, 1024])
        masks = r("masks", [P, 11, P])
        l2 = r("l2", [P, 1024])
        l2s = r("l2s", [P, P])
        lora = r("lora", [P, S])
        ar = r("ar", [P, TT, 2, P])
        bT = r("bT", [P, TT, P])
        kTt = r("kTt", [P, TT, P])
        tokm = r("tokm", [P, TT, 4, P])
        snap = r("snap", [P, 4, P])
        AtT = r("AtT", [P, TT, P])
        Ml1 = r("Ml1", [P, 4, P])
        r = Region(Z0, 10240)
        Mm = r("Mm", [P, 4, 4, P])
        Ml0 = r("Ml0", [P, 4, P])
        r = Region(Z0 + 4 * N2, 10240)
        TX = r("TX", [P, 2, 4, P])
        Tm, Xm = TX[:, 0, :, :], TX[:, 1, :, :]
        Ym = r("Ym", [P, 4, P])
        stg = r("stg", [P, TT, 3, P])
        r = Region(F0, FSZ)
        fT = r("fT", [P, 3, S + 1])
        pf = r("pf", [P, 3, S])
        wa = r("wa", [P, 2, S])
        Pc = r("Pc", [P, 4, 65])
        iP = r("iP", [P, S])
        kkn = r("kkn", [P, S])
        tmpf = r("tmpf", [P, S])
        zero64 = r("zero64", [P, 64])
        W1 = r("W1", [P, TT, 2, 64])
        Uu = r("Uu", [P, TT, 2, 64])
        bon = r("bon", [P, TT, 2])
        st16 = r("st16", [P, 2, TT, 16])
        r = Region(XT0 + 8192, 24576)
        ysq = r("ysq", [P, TT, 1024])
        lnw = r("lnw", [P, 1024])
        lnb = r("lnb", [P, 1024])
        y2 = at("y2", [P, TT, D], F32, Z0)
        post_gain = at("post_gain", [P, D], F32, Z0 + 16384)
        ysc = at("ysc", [P, TT, D], F32, XT0)

        ps = ctx.enter_context(nc.psum_tensor("ps", [P, 8, 512], F32))

        rel_dram = nc.dram_tensor("rel_row_dram", (16, 384), F32, kind="Internal").ap()
        rel_rows = nc.dram_tensor("rel_rows_dram", (P, 16, 384), F32, kind="Internal").ap()
        buck_rows = nc.dram_tensor("buck_rows_dram", (P, HN, 512), F32, kind="Internal").ap()
        buck_dram = nc.dram_tensor("buck_row_dram", (HN, 512), F32, kind="Internal").ap()

        landed = [sem(f"block_landed_{s}") for s in range(RAW_SLOTS)]
        hi_ready, block_split, block_used = sem("hi_ready"), sem("block_split"), sem("block_used")
        drained = [sem("acc_drained_0"), sem("acc_drained_1")]
        class Chain:
            def __init__(self, eng, name):
                self.eng, self.sem, self.base, self.n = eng, sem(name), 0, 0

            def __call__(self, ins):
                ins.then_inc(self.sem, 1)
                self.n += 1
                self.eng.wait_ge(self.sem, self.base + self.n)

            def loop(self, start, end, n):
                return ChainLoop(self, start, end, n)

        class ChainLoop:
            def __init__(self, chain, start, end, n):
                self.c, self.start, self.end, self.per = chain, start, end, n

            def __enter__(self):
                self.f = self.c.eng.Fori(self.start, self.end)
                i = self.f.__enter__()
                self.b0 = self.c.base + self.c.n
                self.c.base, self.c.n = (i - self.start) * self.per + self.b0 if self.start else i * self.per + self.b0, 0
                return i

            def __exit__(self, *e):
                r = self.f.__exit__(*e)
                if e[0] is None:
                    assert self.c.n == self.per, (self.c.n, self.per)
                    self.c.base, self.c.n = self.b0 + self.per * (self.end - self.start), 0
                return r

        def blocks_of(w, col0=0, width=CC):
            return w.rearrange("(t p) n -> p t n", p=P)

        W = {k: blocks_of(a[k][0]) for k in ("w_in", "w_branch_a", "w_branch_b", "w_out", "w_gate_up",
                                            "w_in_2", "w_out_2", "cmp_k_w1_2", "cmp_v_w1_2")}
        w_down = a["w_down"][0].rearrange("(t p) n -> t p n", p=P)

        def load(sp, k, dst, src, b_const, b_reg=None, group=4):
            sp.wait_ge(block_split, b_const + 1 if b_reg is None else b_reg + (b_const + 1))
            sp.dma_start(dst, src).then_inc(landed[k % 4], 16)

        def slot(k, width=CC):
            return raw[:, k % 4, 0:BT * width].rearrange("p (t n) -> p t n", t=BT)

        def cols(w, kb, c0, width=CC):
            return w[:, kb * BT:(kb + 1) * BT, c0:c0 + width]

        def dcols(w, kb, creg, width=CC):
            return w[:, kb * BT:(kb + 1) * BT, bass.ds(creg, width)]

        def stream(sp, i, phase, k):
            if phase == "w_in":
                load(sp, k, slot(k), dcols(W["w_in"], k, i * CC), B_WIN + k, i * 4)
            elif phase == "merge":
                w = W["w_branch_a"] if k < 2 else W["w_branch_b"]
                load(sp, k, slot(k), dcols(w, k % 2, i * CC), B_MERGE + k, i * 4)
            elif phase == "w_out":
                load(sp, k, slot(k), dcols(W["w_out"], k, i * CC), B_WOUT + k, i * 4)
            elif phase == "gate_up":
                c = i * CC if k < 4 else i * CC + FF
                load(sp, k, slot(k), dcols(W["w_gate_up"], k % 4, c), B_GU + k, i * 8)
            elif phase == "down":
                load(sp, k, raw[:, k % 4, :],
                     w_down[bass.ds(i * 4 + k, 1)].rearrange("a p n -> (a p) n"), B_DOWN + k, i * 4)
            elif phase == "w_in2":
                load(sp, k, slot(k), dcols(W["w_in_2"], k, i * CC), B_WIN2 + k, i * 4)
            elif phase == "w_in2_tail":
                load(sp, k, slot(k, N2 - 15 * CC), cols(W["w_in_2"], k, 15 * CC, N2 - 15 * CC), B_WIN2 + 60 + k)
            elif phase == "compress":
                w = W["cmp_k_w1_2"] if k < 2 else W["cmp_v_w1_2"]
                load(sp, k, raw[:, k % 4, :].rearrange("p (t n) -> p t n", t=16),
                     w[:, (k % 2) * 16:(k % 2) * 16 + 16, :], B_CMP + k)
            elif phase == "w_out2":
                load(sp, k, slot(k), dcols(W["w_out_2"], k, i * CC), B_WOUT2 + k, i * 4)

        STREAMS = [("w_in", 16, 4), ("merge", 4, 4), ("w_out", 4, 4), ("gate_up", 11, 8), ("down", 11, 4),
                   ("w_in2", 15, 4), ("w_in2_tail", 0, 4), ("compress", 0, 4), ("w_out2", 4, 4)]

        def split_hi(act, b0, per, i, k):
            assert b0 % 4 == 0 and per % 4 == 0
            act.wait_ge(landed[k % 4], i * (4 * per) + 16 * ((b0 + k) // 4 + 1))
            act.wait_ge(block_used, i * per + (b0 + k + 1))
            nc.scalar.copy(w_hi[:, k % 2, :], raw[:, k % 4, :]).then_inc(hi_ready, 1)

        def split_lo(dve, b0, per, i, k):
            dve.wait_ge(hi_ready, i * per + (b0 + k + 1))
            nc.vector.tensor_tensor(w_lo[:, k % 2, :], raw[:, k % 4, :], w_hi[:, k % 2, :].bitcast(F32),
                                    ALU.subtract).then_inc(block_split, 1)

        def chunk_done(eng, b0, per, i, k):
            eng.wait_ge(block_used, i * per + (b0 + k + 1 + SPLIT_SLOTS))

        def product_steps(eng, split, b0, per, i, ends):
            for k in range(per):
                split(eng, b0, per, i, k + 2)
                if k in ends:
                    chunk_done(eng, b0, per, i, k)
                    ends[k](i)

        def mm_block(pe, b0, per, i, k, hi, lo, kt0, bank, start, stop, width=CC):
            pe.wait_ge(block_split, i * per + (b0 + k + 1 + RAW_SLOTS))
            for t in range(BT):
                for tok in range(TT):
                    xh = hi[:, kt0 + t, tok * P:(tok + 1) * P]
                    xl = lo[:, kt0 + t, tok * P:(tok + 1) * P]
                    wh = w_hi[:, k % 2, t * width:(t + 1) * width]
                    wl = w_lo[:, k % 2, t * width:(t + 1) * width]
                    o = ps[:, bank + tok, 0:width]
                    nc.tensor.matmul(o, xh, wh, start=start and t == 0, stop=False)
                    nc.tensor.matmul(o, xh, wl, start=False, stop=False)
                    mm = nc.tensor.matmul(o, xl, wh, start=False, stop=stop and t == BT - 1)
            mm.then_inc(block_used, 1)

        def acc_free(pe, q, i=0, per=0):
            for tok in range(TT):
                pe.wait_ge(drained[tok], i * per + (q + 1))

        def plain_product(pe, b0, q0, n2, hi, lo):
            with pe.Fori(0, n2) as i:
                for c in range(2):
                    acc_free(pe, q0 + c, i, 2)
                    for k in range(4):
                        mm_block(pe, b0, 8, i, 4 * c + k, hi, lo, 4 * k, 2 * c, k == 0, k == 3)

        turned, turned_hi, turned_lo = sem("tile_turned"), sem("turned_hi"), sem("turned_lo")
        rows_scaled = sem("rows_scaled")

        def turn_rows(pe, src, ready, n_ready, base):
            pe.wait_ge(ready, n_ready)
            for kt in range(KT):
                n = base + kt
                if n >= 4:
                    pe.wait_ge(turned_lo, n - 3)
                for tok in range(TT):
                    tr = nc.tensor.transpose(ps[:, 4 + n % 4, tok * P:(tok + 1) * P],
                                             src[:, tok, kt * P:(kt + 1) * P], ident[:])
                tr.then_inc(turned, 1)

        def turned_to_hi(act, base, g):
            for kt in range(KT):
                n = base + kt
                act.wait_ge(turned, n + 1)
                scale = gains[:, g, kt:kt + 1] if g is not None else 1.0
                nc.scalar.activation(xT_hi[:, kt, :], ps[:, 4 + n % 4, 0:S], ACT.Copy,
                                     scale=scale).then_inc(turned_hi, 1)

        def turned_to_lo(dve, base, g):
            for kt in range(KT):
                n = base + kt
                dve.wait_ge(turned_hi, n + 1)
                src, hi = ps[:, 4 + n % 4, 0:S], xT_hi[:, kt, :].bitcast(F32)
                if g is None:
                    ins = nc.vector.tensor_tensor(xT_lo[:, kt, :], src, hi, ALU.subtract)
                else:
                    ins = nc.vector.scalar_tensor_tensor(xT_lo[:, kt, :], src, gains[:, g, kt:kt + 1],
                                                         hi, ALU.mult, ALU.subtract)
                ins.then_inc(turned_lo, 1)

        def rms_act(act, x, scratch, n):
            for tok in range(TT):
                nc.scalar.activation(scratch[:, tok, :], x[:, tok, :], ACT.Square,
                                     accum_out=stats[:, tok:tok + 1]).then_inc(sem("square_sums"), 1)
            act.wait_ge(sem("mean_squares"), n + 1)
            nc.scalar.activation(stats[:, 4:6], stats[:, 2:4], ACT.Sqrt).then_inc(sem("rms_roots"), 1)

        def rms_dve(dve, link, n):
            dve.wait_ge(sem("square_sums"), TT * (n + 1))
            nc.vector.tensor_scalar(stats[:, 2:4], stats[:, 0:2], 1.0 / D, EPS, ALU.mult, ALU.add)\
                .then_inc(sem("mean_squares"), 1)
            dve.wait_ge(sem("rms_roots"), n + 1)
            link(nc.vector.reciprocal(stats[:, 6:8], stats[:, 4:6]))

        def scale_rows(x, y):
            for tok in range(TT):
                nc.vector.tensor_scalar(y[:, tok, :], x[:, tok, :], stats[:, 6 + tok:7 + tok], None,
                                        ALU.mult).then_inc(rows_scaled, 1)


        T0, T1, T2, T3 = 4, 5, 6, 7

        def shifted(rows, width):
            _, heads, pitch = rows.shape
            return bass.AP(tensor=rows.tensor, offset=P - 1, ap=[[heads * pitch - 1, P], [pitch, heads], [1, width]])

        def windows(kv, g):
            v = kvcT[:, kv, g, :]
            return bass.AP(tensor=v.tensor, offset=v.offset, ap=[list(v.ap[0]), [1, 32], [16, NCMP]])

        LEVELS = 5
        HALF = float(np.float32(math.exp(-0.5)))

        def rwkv_act(act, link):
            act.wait_ge(sem("lora_turned"), 1)
            act.wait_ge(sem("edges_set"), 1)
            nc.scalar.copy(fT[:, 0, 1:S + 1], ps[:, T0, 0:S]).then_inc(sem("lora_copied"), 1)
            act.wait_ge(sem("lora_mixed"), 1)
            nc.scalar.activation(lora[0:64, :], lora[0:64, :], ACT.Tanh).then_inc(sem("lora_ready"), 1)
            act.wait_ge(sem("rwkv_loaded"), 48)

            def stage(i):
                for x in range(3):
                    nc.scalar.copy(stg[:, :, x, :], z2[:, :, bass.ds(i * P + (C_R + 1024 * x), P)])\
                        .then_inc(sem("feat_staged"), 1)
                nc.scalar.copy(l2s[:], l2[:, bass.ds(i * P, P)]).then_inc(sem("l2_staged"), 1)

            def features(i):
                act.wait_ge(sem("feat_turned"), i + 1)
                nc.scalar.copy(fT[:, 0:2, 1:S + 1], ps[:, T0, :].rearrange("p (x n) -> p x n", x=2))\
                    .then_inc(sem("fT_ready"), 1)
                nc.scalar.copy(fT[:, 2, 1:S + 1], ps[:, T1, 0:S]).then_inc(sem("fT_ready"), 1)

            def exps(i):
                act.wait_ge(sem("lora_done"), i + 1)
                for x in range(2):
                    nc.scalar.activation(wa[:, x, :], ps[:, T2 + x, 0:S], ACT.Exp, scale=-1.0,
                                         bias=nw0a0[:, x, bass.ds(i, 1)]).then_inc(sem("wa_exp"), 1)

            def decay(i):
                act.wait_ge(sem("wa_sigmoid"), i + 1)
                nc.scalar.activation(wa[:, 0, :], wa[:, 0, :], ACT.Exp, scale=-HALF).then_inc(sem("decay_ready"), 1)

            def norm(i):
                act.wait_ge(sem("kk_summed"), i + 1)
                nc.scalar.activation(tmpf[:], ps[:, T0, 0:S], ACT.Sqrt).then_inc(sem("kk_norm"), 1)

            def pair(i, ahead):
                act.wait_ge(sem("tok_turned"), i + 1)
                nc.scalar.copy(tokm[:, 0, :, :], ps[:, T1, :].rearrange("p (x n) -> p x n", x=4))\
                    .then_inc(sem("tokm_ready_0"), 1)
                if ahead:
                    stage(i + 1)
                for h in range(2):
                    act.wait_ge(sem("x1_turned"), i * 2 + (h + 1))
                    nc.scalar.copy(Tm[:, 2 * h:2 * h + 2, :], ps[:, h, 0:S].rearrange("p (m n) -> p m n", m=2))\
                        .then_inc(sem("t1_ready"), 1)
                for lev in range(LEVELS):
                    for h in range(2):
                        act.wait_ge(sem("y_made"), i * (2 * LEVELS) + (2 * lev + h + 1))
                        nc.scalar.copy(Ym[:, 2 * h:2 * h + 2, :], ps[:, h, 0:S].rearrange("p (m n) -> p m n", m=2))\
                            .then_inc(sem("y_copied"), 1)
                    if ahead and lev < 4:
                        (features, exps, decay, norm)[lev](i + 1)
                act.wait_ge(sem("at_made"), i + 1)
                nc.scalar.copy(AtT[:], ps[:, 1, 0:S].rearrange("p (t n) -> p t n", t=TT)).then_inc(sem("at_ready"), 1)

            stage(0)
            for step in (features, exps, decay, norm):
                step(0)
            with act.Fori(0, 7) as i:
                pair(i, True)
            pair(7, False)
            act.wait_ge(sem("gn_var"), 1)
            nc.scalar.activation(st16[:, 1, :, :], st16[:, 1, :, :], ACT.Sqrt).then_inc(sem("gn_root"), 1)

        def rwkv_dve(dve, link):
            dve.wait_ge(sem("nsa_out_ready"), HN)
            link(nc.vector.memset(fT[:, :, 0:1], 0.0))
            link(nc.vector.memset(zero64[:], 0.0))
            link(nc.vector.memset(Pc[:, :, 0:1], 1.0))
            link(nc.vector.memset(snap[:, 0, :], 0.0))
            link(nc.vector.tensor_scalar(nw0a0[:], par[:, 0:2, :], -1.0, None, ALU.mult))
            dve.sem_inc(sem("edges_set"), 1)
            dve.wait_ge(sem("lora_copied"), 1)
            link(nc.vector.tensor_tensor(lora[:], fT[:, 0, 0:S], fT[:, 0, 1:S + 1], ALU.subtract))
            link(nc.vector.scalar_tensor_tensor(lora[:], lora[:], mu[:, 24:25], fT[:, 0, 1:S + 1], ALU.mult, ALU.add))
            dve.sem_inc(sem("lora_mixed"), 1)
            dve.wait_ge(sem("rwkv_loaded"), 48)


            def shift(i):
                dve.wait_ge(sem("fT_ready"), i * 2 + 2)
                link(nc.vector.tensor_tensor(pf[:], fT[:, :, 0:S], fT[:, :, 1:S + 1], ALU.subtract))
                for x in range(3):
                    link(nc.vector.scalar_tensor_tensor(pf[:, x, :], pf[:, x, :], mu[:, bass.ds(i + 8 * x, 1)],
                                                        fT[:, x, 1:S + 1], ALU.mult, ALU.add))
                link(nc.vector.tensor_scalar(kkn[:], pf[:, 1, :], par[:, 2, bass.ds(i, 1)], None, ALU.mult))
                link(nc.vector.tensor_tensor(tmpf[:], kkn[:], kkn[:], ALU.mult))
                dve.sem_inc(sem("kk_squared"), 1)

            def sigmoids(i):
                dve.wait_ge(sem("wa_exp"), i * 2 + 2)
                link(nc.vector.tensor_scalar(wa[:], wa[:], 1.0, None, ALU.add))
                link(nc.vector.reciprocal(wa[:], wa[:]))
                dve.sem_inc(sem("wa_sigmoid"), 1)

            def normed(i):
                dve.wait_ge(sem("kk_norm"), i + 1)
                link(nc.vector.tensor_scalar(tmpf[:], tmpf[:], 1e-12, None, ALU.max))
                link(nc.vector.reciprocal(tmpf[:], tmpf[:]))
                link(nc.vector.tensor_tensor(kkn[:], kkn[:], tmpf[:], ALU.mult))

            def pair(i, ahead):
                dve.wait_ge(sem("decay_ready"), i + 1)
                for c in range(4):
                    link(nc.vector.tensor_tensor_scan(Pc[:, c, 1:65], wa[:, 0, 64 * c:64 * c + 64], zero64[:], 1.0,
                                                      ALU.mult, ALU.add))
                link(nc.vector.reciprocal(iP[:].rearrange("p (c n) -> p c n", c=4), Pc[:, :, 1:65]))
                for t in range(TT):
                    kv = kkn[:, t * P:(t + 1) * P].rearrange("p (c n) -> p c n", c=2)
                    rv = pf[:, 0, t * P:(t + 1) * P].rearrange("p (c n) -> p c n", c=2)
                    link(nc.vector.scalar_tensor_tensor(ar[:, t, 0, :].rearrange("p (c n) -> p c n", c=2), kv, -1.0,
                                                        Pc[:, 2 * t:2 * t + 2, 0:64], ALU.mult, ALU.mult))
                    link(nc.vector.tensor_tensor(ar[:, t, 1, :].rearrange("p (c n) -> p c n", c=2), rv,
                                                 Pc[:, 2 * t:2 * t + 2, 1:65], ALU.mult))
                link(nc.vector.tensor_tensor(kkn[:], kkn[:], wa[:, 1, :], ALU.mult))
                link(nc.vector.tensor_tensor(bT[:].rearrange("p t n -> p (t n)"), kkn[:], iP[:], ALU.mult))
                link(nc.vector.tensor_scalar(wa[:, 0, :], wa[:, 1, :], 1.0, par[:, 3, bass.ds(i, 1)],
                                             ALU.subtract, ALU.mult))
                link(nc.vector.scalar_tensor_tensor(wa[:, 0, :], wa[:, 0, :], 1.0, pf[:, 1, :], ALU.add, ALU.mult))
                link(nc.vector.tensor_tensor(kTt[:].rearrange("p t n -> p (t n)"), wa[:, 0, :], iP[:], ALU.mult))
                link(nc.vector.scalar_tensor_tensor(tmpf[:], pf[:, 0, :], par[:, 4, bass.ds(i, 1)], wa[:, 0, :],
                                                    ALU.mult, ALU.mult))
                dve.sem_inc(sem("features_ready"), 1)
                dve.wait_ge(sem("m_made"), i + 1)
                for m in range(4):
                    link(nc.vector.tensor_tensor(Mm[:, m, :, :], ps[:, m, :].rearrange("p (x n) -> p x n", x=4),
                                                 masks[:, 0:4, :], ALU.mult))
                dve.sem_inc(sem("m_masked"), 1)
                for h in range(2):
                    x = Xm[:, 2 * h:2 * h + 2, :]
                    link(nc.vector.tensor_tensor(x, Mm[:, 2 * h:2 * h + 2, 0, :],
                                                 masks[:, 4:5, :].broadcast_to([P, 2, P]), ALU.mult))
                    link(nc.vector.tensor_tensor(x, x, ident[:].unsqueeze(1).broadcast_to([P, 2, P]), ALU.add))
                    dve.sem_inc(sem("x1_ready"), 1)
                dve.wait_ge(sem("tok_turned"), i + 1)
                link(nc.vector.tensor_copy(tokm[:, 1, :, :], ps[:, T2, :].rearrange("p (x n) -> p x n", x=4)))
                dve.sem_inc(sem("tokm_ready_1"), 1)
                link(nc.vector.tensor_copy(bon[:], ps[:, T3, 0:4].rearrange("p (t h) -> p t h", t=TT)))
                dve.sem_inc(sem("bonus_read"), 1)
                for lev in range(LEVELS):
                    for h in range(2):
                        dve.wait_ge(sem("level_made"), i * (2 * LEVELS) + (2 * lev + h + 1))
                        if lev < LEVELS - 1:
                            x = TX[:, :, 2 * h:2 * h + 2, :].rearrange("p x m n -> p x (m n)")
                            d = ps[:, 2 + h, :].rearrange("p (x n) -> p x n", x=2)
                        else:
                            x = Xm[:, 2 * h:2 * h + 2, :].rearrange("p m n -> p (m n)")
                            d = ps[:, 2 + h, S:2 * S]
                        nc.vector.tensor_tensor(x, x, d, ALU.add).then_inc(sem("level_added"), 1)
                    if lev == 0:
                        dve.wait_ge(sem("tokm_ready_0"), i + 1)
                        for t in range(TT):
                            for hd in range(2):
                                nc.vector.tensor_scalar(bv[:, t, bass.ds(i * P + 64 * hd, 64)],
                                                        tokm[:, t, 3, 64 * hd:64 * hd + 64], bon[:, t, hd:hd + 1],
                                                        None, ALU.mult).then_inc(sem("bonus_ready"), 1)
                    if ahead and 1 <= lev <= 2:
                        (shift, sigmoids)[lev - 1](i + 1)
                if ahead:
                    normed(i + 1)
                dve.wait_ge(sem("w0_made"), i + 1)
                link(nc.vector.tensor_copy(Uu[:].rearrange("p t h n -> p (t h n)"), ps[:, 0, 0:S]))
                dve.sem_inc(sem("w0_ready"), 1)
                dve.wait_ge(sem("w1_made"), i + 1)
                link(nc.vector.tensor_copy(W1[:].rearrange("p t h n -> p (t h n)"), ps[:, 2, 0:S]))
                for c in range(4):
                    t, rows = c // 2, slice(64 * (c % 2), 64 * (c % 2) + 64)
                    dve.wait_ge(sem("u_made"), i * 4 + (c + 1))
                    nc.vector.tensor_tensor(Uu[rows, t, :, :].rearrange("p h n -> p (h n)"), ps[rows, 0, 0:P],
                                            W1[rows, t, :, :].rearrange("p h n -> p (h n)"), ALU.add)\
                        .then_inc(sem("u_ready"), 1)
                    if c < 3:
                        dve.wait_ge(sem("s_made"), i * 3 + (c + 1))
                        nc.vector.tensor_tensor(snap[:, c + 1, :], ps[:, 3, 0:P], snap[:, c, :], ALU.add)\
                            .then_inc(sem("s_added"), 1)
                        dve.wait_ge(sem("s_added"), i * 3 + (c + 1))
                        nc.vector.scalar_tensor_tensor(snap[:, c + 1, :], snap[:, c + 1, :], Pc[:, c, 64:65],
                                                       masks[:, 10, :], ALU.mult, ALU.mult)\
                            .then_inc(sem("s_ready"), 1)
                        dve.wait_ge(sem("s_ready"), i * 3 + (c + 1))
                dve.wait_ge(sem("y_out_made"), i + 1)
                nc.vector.tensor_copy(oy[:, :, bass.ds(i * P + 1024, P)],
                                      ps[:, 1, 0:S].rearrange("p (t n) -> p t n", t=TT)).then_inc(sem("pair_done"), 1)

            shift(0)
            sigmoids(0)
            normed(0)
            with link.loop(0, 7, 38) as i:
                pair(i, True)
            pair(7, False)
            dve.wait_ge(sem("pair_done"), 8)
            dve.wait_ge(sem("bonus_ready"), 32)
            yh = oy[:, :, 1024:D].rearrange("p t (h n) -> p t h n", h=16)
            yq = ysq[:].rearrange("p t (h n) -> p t h n", h=16)
            mean, var = st16[:, 0, :, :], st16[:, 1, :, :]
            wide = [P, TT, 16, 64]
            link(nc.vector.tensor_reduce(mean, yh, AX, ALU.add))
            link(nc.vector.tensor_scalar(mean, mean, 1.0 / 64, None, ALU.mult))
            link(nc.vector.tensor_tensor(yh, yh, mean.unsqueeze(3).broadcast_to(wide), ALU.subtract))
            link(nc.vector.tensor_tensor(yq, yh, yh, ALU.mult))
            link(nc.vector.tensor_reduce(var, yq, AX, ALU.add))
            link(nc.vector.tensor_scalar(var, var, 1.0 / 64, 64e-5, ALU.mult, ALU.add))
            dve.sem_inc(sem("gn_var"), 1)
            dve.wait_ge(sem("gn_root"), 1)
            link(nc.vector.reciprocal(var, var))
            link(nc.vector.tensor_tensor(yh, yh, var.unsqueeze(3).broadcast_to(wide), ALU.mult))
            dve.wait_ge(sem("ln_loaded"), 32)
            y = oy[:, :, 1024:D]
            link(nc.vector.tensor_tensor(y, y, lnw[:].unsqueeze(1).broadcast_to([P, TT, 1024]), ALU.mult))
            link(nc.vector.tensor_tensor(y, y, lnb[:].unsqueeze(1).broadcast_to([P, TT, 1024]), ALU.add))
            link(nc.vector.tensor_tensor(y, y, bv[:], ALU.add))
            dve.sem_inc(sem("rwkv_done"), 1)

        def rwkv_pe(pe):
            for tok in range(TT):
                tr = nc.tensor.transpose(ps[:, T0, tok * P:(tok + 1) * P], z2[:, tok, C_LORA:C_LORA + P], ident[:])
            tr.then_inc(sem("lora_turned"), 1)
            pe.wait_ge(sem("lora_ready"), 1)

            def turn_features(i):
                pe.wait_ge(sem("feat_staged"), i * 3 + 3)
                for x in range(3):
                    for tok in range(TT):
                        c = (x % 2) * S + tok * P
                        tr = nc.tensor.transpose(ps[:, T0 + x // 2, c:c + P], stg[:, tok, x, :], ident[:])
                tr.then_inc(sem("feat_turned"), 1)

            def low_rank(i):
                pe.wait_ge(sem("l2_staged"), i + 1)
                nc.tensor.matmul(ps[:, T2, 0:S], l2s[0:64, :], lora[0:64, :], start=True, stop=True)
                nc.tensor.matmul(ps[:, T3, 0:S], l2s[64:128, :], lora[64:128, :], start=True, stop=True)\
                    .then_inc(sem("lora_done"), 1)

            def kk_sums(i):
                pe.wait_ge(sem("kk_squared"), i + 1)
                nc.tensor.matmul(ps[:, T0, 0:S], masks[:, 10, :], tmpf[:], start=True, stop=True)\
                    .then_inc(sem("kk_summed"), 1)

            def pair(i, ahead):
                pe.wait_ge(sem("features_ready"), i + 1)
                for tok in range(TT):
                    for x, src in enumerate((ar[:, tok, 0, :], bT[:, tok, :], kTt[:, tok, :],
                                             pf[:, 2, tok * P:(tok + 1) * P])):
                        nc.tensor.transpose(ps[:, T1 + tok, x * P:(x + 1) * P], src, ident[:])
                for tok in range(TT):
                    mm = nc.tensor.matmul(ps[:, T3, 2 * tok:2 * tok + 2], tmpf[:, tok * P:(tok + 1) * P],
                                          masks[:, 10, 0:P:64], start=True, stop=True)
                mm.then_inc(sem("tok_turned"), 1)
                for tok in range(TT):
                    for src, c in ((bT, 0), (kTt, S)):
                        for hd in range(2):
                            h = slice(64 * hd, 64 * hd + 64)
                            mm = nc.tensor.matmul(ps[:, 2 * tok + hd, c:c + S], src[h, tok, :],
                                                  ar[h, tok, :, :].rearrange("p x n -> p (x n)"), start=True, stop=True)
                mm.then_inc(sem("m_made"), 1)
                for h in range(2):
                    pe.wait_ge(sem("x1_ready"), i * 2 + (h + 1))
                    for m in range(2):
                        tr = nc.tensor.transpose(ps[:, h, m * P:(m + 1) * P], Xm[:, 2 * h + m, :], ident[:])
                    tr.then_inc(sem("x1_turned"), 1)
                if ahead:
                    pe.wait_ge(sem("tokm_ready_0"), i + 1)
                    pe.wait_ge(sem("bonus_read"), i + 1)
                    turn_features(i + 1)
                    low_rank(i + 1)
                for lev in range(LEVELS):
                    Ml = (Ml0, Ml1)[lev % 2]
                    pe.wait_ge(sem("level_ready"), i * LEVELS + (lev + 1))
                    for h in range(2):
                        if lev:
                            pe.wait_ge(sem("level_added"), i * (2 * LEVELS) + (2 * lev + h - 1))
                        else:
                            pe.wait_ge(sem("t1_ready"), i * 2 + (h + 1))
                        for m in range(2):
                            mm = nc.tensor.matmul(ps[:, h, m * P:(m + 1) * P], Ml[:, 2 * h + m, :],
                                                  Tm[:, 2 * h + m, :], start=True, stop=True)
                        mm.then_inc(sem("y_made"), 1)
                    for h in range(2):
                        pe.wait_ge(sem("y_copied"), i * (2 * LEVELS) + (2 * lev + h + 1))
                        for m in range(2):
                            x, y = Xm[:, 2 * h + m, :], Ym[:, 2 * h + m, :]
                            if lev < LEVELS - 1:
                                nc.tensor.matmul(ps[:, 2 + h, m * P:(m + 1) * P], x, y, start=True, stop=True)
                            mm = nc.tensor.matmul(ps[:, 2 + h, S + m * P:S + (m + 1) * P], y, x, start=True, stop=True)
                        mm.then_inc(sem("level_made"), 1)
                    if ahead and lev == 2:
                        kk_sums(i + 1)
                for m in range(4):
                    h = slice(64 * (m % 2), 64 * (m % 2) + 64)
                    mm = nc.tensor.matmul(ps[:, 0, m * 64:(m + 1) * 64], Mm[:, m, 2, :], tokm[:, m // 2, 3, h],
                                          start=True, stop=True)
                mm.then_inc(sem("w0_made"), 1)
                pe.wait_ge(sem("level_added"), i * (2 * LEVELS) + 2 * LEVELS)
                for m in range(4):
                    h = slice(64 * (m % 2), 64 * (m % 2) + 64)
                    mm = nc.tensor.matmul(ps[h, 1, (m // 2) * P:(m // 2 + 1) * P], tokm[:, m // 2, 0, h], Xm[:, m, :],
                                          start=True, stop=True)
                mm.then_inc(sem("at_made"), 1)
                pe.wait_ge(sem("w0_ready"), i + 1)
                for m in range(4):
                    mm = nc.tensor.matmul(ps[:, 2, m * 64:(m + 1) * 64], Xm[:, m, :], Uu[:, m // 2, m % 2, :],
                                          start=True, stop=True)
                mm.then_inc(sem("w1_made"), 1)
                pe.wait_ge(sem("at_ready"), i + 1)
                for c in range(4):
                    t, rows = c // 2, slice(64 * (c % 2), 64 * (c % 2) + 64)
                    if c:
                        pe.wait_ge(sem("s_ready"), i * 3 + c)
                    nc.tensor.matmul(ps[:, 0, 0:P], AtT[:, t, :], snap[:, c, :], start=True, stop=True)\
                        .then_inc(sem("u_made"), 1)
                    pe.wait_ge(sem("u_ready"), i * 4 + (c + 1))
                    if c < 3:
                        nc.tensor.matmul(ps[:, 3, 0:P], tokm[rows, t, 1, :],
                                         Uu[rows, t, :, :].rearrange("p h n -> p (h n)"), start=True, stop=False)
                        nc.tensor.matmul(ps[:, 3, 0:P], tokm[rows, t, 2, :], tokm[rows, t, 3, :],
                                         start=False, stop=True).then_inc(sem("s_made"), 1)
                for t in range(TT):
                    for c in (2 * t, 2 * t + 1):
                        rows = slice(64 * (c % 2), 64 * (c % 2) + 64)
                        nc.tensor.matmul(ps[rows, 1, t * P:(t + 1) * P], ar[:, t, 1, rows], snap[:, c, :],
                                         start=True, stop=False, skip_group_check=True)
                    for hd in range(2):
                        h = slice(64 * hd, 64 * hd + 64)
                        o = ps[:, 1, t * P + 64 * hd:t * P + 64 * hd + 64]
                        nc.tensor.matmul(o, Mm[:, 2 * t + hd, 1, :], Uu[:, t, hd, :], start=False, stop=False,
                                         skip_group_check=True)
                        mm = nc.tensor.matmul(o, Mm[:, 2 * t + hd, 3, :], tokm[:, t, 3, h], start=False, stop=True,
                                              skip_group_check=True)
                mm.then_inc(sem("y_out_made"), 1)

            turn_features(0)
            low_rank(0)
            kk_sums(0)
            with pe.Fori(0, 7) as i:
                pair(i, True)
            pair(7, False)

        block = ctx.enter_context(nc.Block())

        @block.sync
        def _(sp):
            sp.dma_start(resid[:], a["x"][0].rearrange("(t p) n -> p t n", p=P)).then_inc(sem("x_loaded"), 16)
            for phase, n, per in STREAMS:
                if n:
                    with sp.Fori(0, n) as i:
                        for k in range(per):
                            stream(sp, i, phase, k)
                else:
                    for k in range(per):
                        stream(sp, 0, phase, k)
            sp.wait_ge(sem("out_ready"), TT)
            sp.dma_start(out[0].rearrange("(t p) n -> p t n", p=P), y2[:]).then_inc(sem("out_stored"), 16)
            sp.wait_ge(sem("out_stored"), 16)

        @block.gpsimd
        def _(pool):
            def vec(dst, src):
                pool.dma_start(dst, src.rearrange("(k p) -> p k", p=P)).then_inc(sem("params_loaded"), 16)

            rel, buck = sem("rel_loaded"), sem("bucket_loaded")
            pool.dma_start(ident[:], a["ident"]).then_inc(sem("ident_loaded"), 16)
            with nc.allow_non_contiguous_dma("small parameters, one element per partition"):
                vec(gains[:, 0, :], a["norm_mix"][0])
                vec(gains[:, 1, :], a["norm_ffn"][0])
                vec(gains[:, 2, :], a["pre_norm_g_2"][0])
                vec(pool_scale[:], a["pool_scale"][0])
                for j, name in enumerate(("rwkv_w0_2", "rwkv_a0_2", "rwkv_k_k_2", "rwkv_k_a_2")):
                    vec(par[:, j, :], a[name][0])
                vec(par[:, 4, :], a["rwkv_r_k_2"][0].rearrange("h n -> (h n)"))
                vec(mu[:], a["rwkv_mu_2"][0])
                for j in range(3):
                    n = min(P, 2 * REL + 1 - j * P)
                    pool.dma_start(relT[0:n, j, :], a["rel_bias"][0][:, j * P:j * P + n]
                                   .rearrange("h b -> b h")).then_inc(rel, 16)
            pool.dma_start(pick_rel[:], a["pick_rel"].rearrange("(k p) n -> p k n", p=P)).then_inc(rel, 16)
            pool.dma_start(tableT[:], a["rel_bias_table_2"]).then_inc(buck, 16)
            pool.dma_start(pick_b[:], a["pick_bucket"]).then_inc(buck, 16)
            pool.dma_start(future[:], a["future"]).then_inc(buck, 16)
            pool.wait_ge(sem("rel_row_ready"), 1)
            pool.dma_start(rel_dram, rel_row[:]).then_inc(sem("rel_row_stored"), 16)
            pool.wait_ge(sem("buck_row_ready"), 1)
            pool.dma_start(buck_dram, buck_row[:]).then_inc(sem("buck_row_stored"), 16)
            pool.wait_ge(sem("rel_row_stored"), 16)
            pool.dma_start(rel_rows, rel_dram.partition_broadcast(P)).then_inc(sem("rel_rows_stored"), 16)
            pool.wait_ge(sem("buck_row_stored"), 16)
            pool.dma_start(buck_rows, buck_dram.partition_broadcast(P)).then_inc(sem("buck_rows_stored"), 16)
            pool.wait_ge(sem("rel_rows_stored"), 16)
            pool.wait_ge(sem("buck_rows_stored"), 16)
            pool.wait_ge(block_used, B_DOWN + SPLIT_SLOTS)
            pool.dma_start(fin_gain[:], a["norm_final"].partition_broadcast(P)).then_inc(sem("fin_gain_loaded"), 16)
            nsa = sem("nsa_loaded")
            pool.wait_ge(block_used, B_CMP + SPLIT_SLOTS)
            pool.dma_start(bias2[:], shifted(buck_rows, 384)).then_inc(nsa, 16)
            with nc.allow_non_contiguous_dma("positions, transposed"):
                for j, name in enumerate(("cmp_pos_k_2", "cmp_pos_v_2")):
                    pool.dma_start(posT[:, j, :], a[name][0].rearrange("t d -> d t")).then_inc(nsa, 16)
            for j, name in enumerate(("cmp_k_w2_2", "cmp_v_w2_2")):
                pool.dma_start(cw2[:, j, :], a[name][0]).then_inc(nsa, 16)
            rw = sem("rwkv_loaded")
            pool.wait_ge(sem("nsa_out_ready"), HN)
            pool.dma_start(masks[:], a["masks"].rearrange("m p n -> p m n")).then_inc(rw, 16)
            pool.dma_start(l2[0:64, :], a["rwkv_w2_2"][0]).then_inc(rw, 16)
            pool.dma_start(l2[64:128, :], a["rwkv_a2_2"][0]).then_inc(rw, 16)
            def level(i, lev):
                if lev < 2:
                    pool.wait_ge(sem("m_masked"), i + 1)
                else:
                    pool.wait_ge(sem("level_made"), i * (2 * LEVELS) + 2 * (lev - 1))
                pool.tensor_tensor((Ml0, Ml1)[lev % 2][:], Mm[:, :, 0, :],
                                   masks[:, 5 + lev:6 + lev, :].broadcast_to([P, 4, P]), ALU.mult)\
                    .then_inc(sem("level_ready"), 1)

            pool.wait_ge(rw, 48)
            with pool.Fori(0, 8) as i:
                for lev in range(LEVELS):
                    level(i, lev)
            pool.wait_ge(sem("pair_done"), 8)
            pool.dma_start(lnw[:], a["rwkv_ln_w_2"][0].partition_broadcast(P)).then_inc(sem("ln_loaded"), 16)
            pool.dma_start(lnb[:], a["rwkv_ln_b_2"][0].partition_broadcast(P)).then_inc(sem("ln_loaded"), 16)
            pool.wait_ge(turned_lo, 4 * KT)
            pool.wait_ge(sem("mix_ready"), 1)
            pool.dma_start(post_gain[:], a["post_norm_g_2"][0].partition_broadcast(P))\
                .then_inc(sem("post_gain_loaded"), 16)

        @block.scalar
        def _(act):
            link = Chain(act, "act_chain")

            act.wait_ge(sem("x_loaded"), 16)
            rms_act(act, resid, scaled, 0)
            split_hi(act, B_WIN, 0, 0, 0)
            split_hi(act, B_WIN, 0, 0, 1)
            act.wait_ge(sem("params_loaded"), 160)
            turned_to_hi(act, 0, 0)

            def store(dst, bank, col):
                def f(i):
                    nc.scalar.copy(dst[:, 0, bass.ds(i * 2 * CC + col, CC)], ps[:, bank, :])\
                        .then_inc(drained[0], 1)
                return f

            def gates(bank, col):
                def f(i):
                    for tok in range(TT):
                        nc.scalar.activation(gate[:, tok, bass.ds(i * 2 * CC + (col - 4096), CC)],
                                             ps[:, bank + tok, :], ACT.Sigmoid).then_inc(drained[tok], 1)
                return f

            with act.Fori(0, 4) as i:
                product_steps(act, split_hi, B_WIN, 8, i, {3: store(qkvu, 0, 0), 7: store(qkvu, 2, CC)})
            act.wait_ge(sem("rel_row_stored"), 16)
            act.wait_ge(sem("buck_row_stored"), 16)
            with act.Fori(4, 8) as i:
                product_steps(act, split_hi, B_WIN, 8, i, {3: gates(0, 0), 7: gates(2, CC)})

            act.wait_ge(drained[1], 2 + 16)
            act.wait_ge(drained[0], 2 + 16)
            act.wait_ge(turned, KT)
            act.wait_ge(sem("rel_rows_stored"), 16)
            with act.Fori(0, 8) as i:
                act.wait_ge(sem("relb_used"), i + 1)
                act.dma_start(relb[:], shifted(rel_rows, 256)[:, bass.ds(2 * i, 2), :])\
                    .then_inc(sem("relb_loaded"), 16)
                nc.scalar.copy(kst[:], qkvu[:, :, bass.ds(i * P + 1024, P)]).then_inc(sem("k_staged"), 1)
                nc.scalar.copy(vst[:], qkvu[:, :, bass.ds(i * P + 2048, P)]).then_inc(sem("v_staged"), 1)
                act.wait_ge(sem("qk_turned"), i + 1)
                nc.scalar.copy(qT[:], ps[:, T0, 0:S]).then_inc(sem("qT_ready"), 1)
                act.wait_ge(sem("att_max"), i + 1)
                for hd in range(2):
                    for qt in range(TT):
                        seg = prob[:, hd, 0:P] if qt == 0 else prob[:, hd, P:384]
                        c = 2 * qt + hd
                        nc.scalar.activation(seg, seg, ACT.Exp, bias=smax[:, c:c + 1],
                                             accum_out=ssum[:, c:c + 1]).then_inc(sem("att_exp"), 1)
                act.wait_ge(sem("probs_turned"), i + 1)
                nc.scalar.copy(probT[:, 0, :], ps[:, T2, 0:384]).then_inc(sem("pT_ready_0"), 1)
                act.wait_ge(sem("pv_done"), i + 1)
                nc.scalar.copy(xT_hi[:, bass.ds(i, 1), :].rearrange("p a n -> p (a n)"), ps[:, T0, 0:S])\
                    .then_inc(sem("att_hi"), 1)

            with act.Fori(0, 4) as g:
                act.wait_ge(sem("pool_mixed"), g + 1)
                act.dma_start(rowp[:], a["pool_rows"][bass.ds(g, 1)]
                              .rearrange("a (k p) n -> p (a k) n", p=P)).then_inc(sem("pool_loaded"), 16)
                act.dma_start(pwg[:], a["pool_w"][0][bass.ds(g, 1)]
                              .rearrange("a (k p) n -> p (a k) n", p=P)).then_inc(sem("pool_loaded"), 16)
                nc.scalar.copy(ust[:], qkvu[:, :, bass.ds(g * S + 3072, S)]).then_inc(sem("u_staged"), 1)
                act.wait_ge(sem("pool_mean"), g + 1)
                nc.scalar.copy(dT[:, 0, :], ps[:, T0, 0:S]).then_inc(sem("dT_ready_0"), 1)
                act.wait_ge(sem("pool_mixed"), g + 2)
                for e in range(2):
                    nc.scalar.activation(xT_hi[:, bass.ds(g * 2 + (8 + e), 1), :].rearrange("p a n -> p (a n)"),
                                         ps[:, T2 + e, 0:S], ACT.Copy,
                                         scale=pool_scale[:, bass.ds(g * 2 + e, 1)]).then_inc(sem("pool_hi"), 1)

            def merged_hi(i, back):
                for j in range(4):
                    act.wait_ge(sem("merged_turned"), i * 4 + (j + 1 - 4 * back))
                    nc.scalar.copy(mT_hi[:, bass.ds(i * 4 + (j - 4 * back), 1), :].rearrange("p a n -> p (a n)")
                                   if not isinstance(i, int) else mT_hi[:, 4 * (i - back) + j, :],
                                   ps[:, T0 + j, 0:S]).then_inc(sem("merged_hi"), 1)

            product_steps(act, split_hi, B_MERGE, 4, 0, {})
            with act.Fori(1, 4) as i:
                product_steps(act, split_hi, B_MERGE, 4, i, {1: lambda i: merged_hi(i, 1)})
            merged_hi(4, 1)

            with act.Fori(0, 2) as i:
                product_steps(act, split_hi, B_WOUT, 8, i, {})

            for tok in range(TT):
                act.wait_ge(drained[tok], 2 + Q_GU)
            rms_act(act, resid, scaled, 1)
            turned_to_hi(act, KT, 1)

            def sig(i):
                for tok in range(TT):
                    nc.scalar.activation(g_act[:, tok, :], ps[:, tok, :], ACT.Sigmoid)\
                        .then_inc(sem("sig_ready"), 1)

            def hidden_back(i, back=1):
                act.wait_ge(sem("hidden_turned"), i + (1 - back))
                for j in range(2):
                    if isinstance(i, int):
                        dst = actT[:, 4 * (i - back) + 2 * j:4 * (i - back) + 2 * j + 2, :]
                    else:
                        dst = actT[:, bass.ds(i * 4 + (2 * j - 4 * back), 2), :]
                    nc.scalar.copy(dst, ps[:, T0 + j, :].rearrange("p (k n) -> p k n", k=2))\
                        .then_inc(sem("hidden_ready"), 1)

            product_steps(act, split_hi, B_GU, 8, 0, {3: sig})
            with act.Fori(1, 11) as i:
                product_steps(act, split_hi, B_GU, 8, i, {3: lambda i: (hidden_back(i), sig(i))})
            hidden_back(11)

            def stage_hi(i, k):
                if isinstance(i, int):
                    src = actT[:, 4 * i + k, :]
                else:
                    src = actT[:, bass.ds(i * 4 + k, 1), :].rearrange("p a n -> p (a n)")
                nc.scalar.copy(aT_hi[:, k % 2, :], src).then_inc(sem("hidden_hi"), 1)

            act.wait_ge(sem("hidden_ready"), 22)
            stage_hi(0, 0)
            stage_hi(0, 1)
            with act.Fori(0, 10) as i:
                for k in range(4):
                    split_hi(act, B_DOWN, 4, i, k + 2)
                    stage_hi(i, k + 2)
            for k in range(4):
                split_hi(act, B_DOWN, 4, 10, k + 2)
                if k < 2:
                    stage_hi(10, k + 2)

            for tok in range(TT):
                act.wait_ge(drained[tok], 2 + Q_WIN2)
            act.wait_ge(sem("down_added"), 4)
            rms_act(act, resid, scaled, 2)
            act.wait_ge(sem("final_normed"), 2)
            rms_act(act, resid, scaled, 3)
            turned_to_hi(act, 2 * KT, 2)

            def store2(bank, col, width=CC):
                def f(i):
                    dst = z2[:, 0, col:col + width] if isinstance(i, int) else \
                        z2[:, 0, bass.ds(i * 2 * CC + col, width)]
                    nc.scalar.copy(dst, ps[:, bank, 0:width]).then_inc(drained[0], 1)
                return f

            with act.Fori(0, 7) as i:
                product_steps(act, split_hi, B_WIN2, 8, i, {3: store2(0, 0), 7: store2(2, CC)})
            product_steps(act, split_hi, B_WIN2 + 56, 8, 0,
                          {3: store2(0, 14 * CC), 7: store2(2, 15 * CC, N2 - 15 * CC)})

            for j in range(2):
                act.wait_ge(sem("keys_turned"), j + 1)
                nc.scalar.copy(KTs[:, j, :, :], ps[:, T0 + j, :].rearrange("p (g n) -> p g n", g=2))\
                    .then_inc(sem("keysT_ready"), 1)
            act.wait_ge(drained[0], 2 + 68 - 0)
            act.wait_ge(drained[1], 2 + 68 - 0)
            nc.scalar.activation(gsig[:, :, 0:16], z2[:, :, C_GATE + 8:C_GATE + 24], ACT.Exp, scale=-1.0)\
                .then_inc(sem("gate_exp"), 1)
            nc.scalar.activation(gsig[:, :, 16:24], z2[:, :, C_GATE:C_GATE + 8], ACT.Exp, scale=-1.0)\
                .then_inc(sem("gate_exp"), 1)
            for k in range(4):
                split_hi(act, B_CMP, 4, 0, k + 2)
            chunk_done(act, B_CMP, 4, 0, 3)
            nc.scalar.activation(hexp[:, :, 0:30], ps[:, 0:2, 0:30], ACT.Exp, scale=-1.0)\
                .then_inc(sem("hid_exp"), 1)
            act.wait_ge(sem("compressed"), 1)
            nc.scalar.copy(kcT[:, 0:30], ps[:, 2, 0:30]).then_inc(sem("kcT_ready"), 1)

            with act.Fori(0, 2) as g:
                for hh in range(4):
                    n = g * 4 + hh
                    act.wait_ge(sem("q2_turned"), n + 1)
                    nc.scalar.copy(q2T[:], ps[:, T0, 0:S]).then_inc(sem("q2T_ready"), 1)
                    act.wait_ge(sem("nsa_max"), n + 1)
                    for b in range(3):
                        for qt in range(TT):
                            if b == 2:
                                seg = prc[:, qt, 0:NCMP]
                            else:
                                seg = pr[:, b, 0:P] if qt == 0 else pr[:, b, P:384]
                            nc.scalar.activation(seg, seg, ACT.Exp, bias=mx2[:, b, qt:qt + 1],
                                                 accum_out=sm2[:, b, qt:qt + 1]).then_inc(sem("nsa_exp"), 1)
                    act.wait_ge(sem("probs2_turned"), n + 1)
                    nc.scalar.copy(pT2[:, 0, :], ps[:, T1, 0:384]).then_inc(sem("pT2_ready_0"), 1)
                    nc.scalar.copy(pcT[0:NCMP, :], ps[0:NCMP, T3, 0:S]).then_inc(sem("pT2_ready_0"), 1)
                    act.wait_ge(sem("pv2_done"), n + 1)
                    nc.scalar.copy(oy[:, :, bass.ds(n * P, P)],
                                   ps[:, 3, 0:S].rearrange("p (t n) -> p t n", t=TT))\
                        .then_inc(sem("nsa_out_ready"), 1)

            rwkv_act(act, link)

            act.wait_ge(sem("rwkv_done"), 1)
            for c in (C_ZA, C_ZB):
                nc.scalar.activation(ysc[:, :, 0:1024] if c == C_ZA else ysc[:, :, 1024:D],
                                     z2[:, :, c:c + 1024], ACT.Sigmoid).then_inc(sem("z_sig"), 1)
            turned_to_hi(act, 3 * KT, None)

            def store3(bank, col):
                def f(i):
                    nc.scalar.copy(y2[:, 0, bass.ds(i * 2 * CC + col, CC)], ps[:, bank, :])\
                        .then_inc(drained[0], 1)
                return f

            with act.Fori(0, 1) as i:
                product_steps(act, split_hi, B_WOUT2, 8, i, {3: store3(0, 0), 7: store3(2, CC)})
            for k in range(8):
                if k < 6:
                    split_hi(act, B_WOUT2 + 8, 8, 0, k + 2)
                if k % 4 == 3:
                    chunk_done(act, B_WOUT2 + 8, 8, 0, k)
                    nc.scalar.copy(y2[:, 0, (2 + k // 4) * CC:(3 + k // 4) * CC], ps[:, 2 * (k // 4), :])\
                        .then_inc(drained[0], 1)
            act.wait_ge(drained[1], 2 + 72)
            act.wait_ge(drained[0], 2 + 72)
            rms_act(act, y2, ysc, 4)

        @block.vector
        def _(dve):
            link = Chain(dve, "dve_chain")
            dve.sem_inc(block_split, RAW_SLOTS)
            dve.sem_inc(block_used, SPLIT_SLOTS)
            dve.sem_inc(drained[0], 2)
            dve.sem_inc(drained[1], 2)
            dve.sem_inc(sem("relb_used"), 1)
            dve.sem_inc(sem("pool_mixed"), 1)

            rms_dve(dve, link, 0)
            scale_rows(resid, scaled)
            split_lo(dve, B_WIN, 0, 0, 0)
            split_lo(dve, B_WIN, 0, 0, 1)
            dve.wait_ge(sem("rows_made"), 1)
            nc.vector.tensor_copy(rel_row[:], ps[0:16, 0, 0:384]).then_inc(sem("rel_row_ready"), 1)
            dve.wait_ge(sem("bucket_loaded"), 48)
            nc.vector.tensor_tensor(buck_row[:], ps[0:HN, 1, :], future[:], ALU.add).then_inc(sem("buck_row_ready"), 1)
            dve.wait_ge(sem("params_loaded"), 160)
            turned_to_lo(dve, 0, 0)

            def store(bank, col):
                def f(i):
                    nc.vector.tensor_copy(qkvu[:, 1, bass.ds(i * 2 * CC + col, CC)], ps[:, bank + 1, :])\
                        .then_inc(drained[1], 1)
                return f

            with dve.Fori(0, 4) as i:
                product_steps(dve, split_lo, B_WIN, 8, i, {3: store(0, 0), 7: store(2, CC)})
            with dve.Fori(4, 8) as i:
                product_steps(dve, split_lo, B_WIN, 8, i, {})

            dve.wait_ge(drained[1], 2 + 16)
            dve.wait_ge(drained[0], 2 + 16)
            with link.loop(0, 8, 6) as i:
                nc.vector.tensor_scalar(qst[:], qkvu[:, :, bass.ds(i * P, P)], 0.125, None, ALU.mult)\
                    .then_inc(sem("q_staged"), 1)
                dve.wait_ge(sem("qk_turned"), i + 1)
                nc.vector.tensor_copy(kT[:], ps[:, T1, 0:S]).then_inc(sem("kT_ready"), 1)
                dve.wait_ge(sem("scores_ready"), i + 1)
                dve.wait_ge(sem("relb_loaded"), i * 16 + 16)
                link(nc.vector.memset(relb[0:64, :, 192:256], NEG))
                link(nc.vector.tensor_tensor(prob[:, :, 0:P], ps[:, 0:2, 0:P], relb[:, :, P:256], ALU.add))
                nc.vector.tensor_tensor(prob[:, :, P:384], ps[:, 0:2, P:384], relb[:], ALU.add)\
                    .then_inc(sem("relb_used"), 1)
                dve.wait_ge(sem("relb_used"), i + 2)
                link(nc.vector.tensor_reduce(smax[:, 0:2], prob[:, :, 0:P], AX, ALU.max))
                link(nc.vector.tensor_reduce(smax[:, 2:4], prob[:, :, P:384], AX, ALU.max))
                nc.vector.tensor_scalar(smax[:], smax[:], -1.0, None, ALU.mult).then_inc(sem("att_max"), 1)
                dve.wait_ge(sem("att_exp"), i * 4 + 4)
                link(nc.vector.reciprocal(ssum[:], ssum[:]))
                for hd in range(2):
                    for qt in range(TT):
                        seg = prob[:, hd, 0:P] if qt == 0 else prob[:, hd, P:384]
                        c = 2 * qt + hd
                        nc.vector.tensor_scalar(seg, seg, ssum[:, c:c + 1], None, ALU.mult)\
                            .then_inc(sem("probs_ready"), 1)
                dve.wait_ge(sem("probs_turned"), i + 1)
                link(nc.vector.tensor_copy(probT[:, 1, :], ps[:, T3, 0:384]))
                dve.sem_inc(sem("pT_ready_1"), 1)
                dve.wait_ge(sem("att_hi"), i + 1)
                nc.vector.tensor_tensor(xT_lo[:, bass.ds(i, 1), :].rearrange("p a n -> p (a n)"), ps[:, T0, 0:S],
                                        xT_hi[:, bass.ds(i, 1), :].rearrange("p a n -> p (a n)").bitcast(F32),
                                        ALU.subtract).then_inc(sem("att_lo"), 1)

            with dve.Fori(0, 4) as g:
                dve.wait_ge(sem("pool_mean"), g + 1)
                nc.vector.tensor_copy(dT[:, 1, :], ps[:, T1, 0:S]).then_inc(sem("dT_ready_1"), 1)
                for e in range(2):
                    kt = bass.ds(g * 2 + (8 + e), 1)
                    dve.wait_ge(sem("pool_hi"), g * 2 + (e + 1))
                    nc.vector.scalar_tensor_tensor(
                        xT_lo[:, kt, :].rearrange("p a n -> p (a n)"), ps[:, T2 + e, 0:S],
                        pool_scale[:, bass.ds(g * 2 + e, 1)],
                        xT_hi[:, kt, :].rearrange("p a n -> p (a n)").bitcast(F32),
                        ALU.mult, ALU.subtract).then_inc(sem("pool_lo"), 1)

            def branch(i, which):
                buf = g_act if which == 0 else h_act
                if which == 0 and not isinstance(i, int):
                    dve.wait_ge(sem("merged_ready"), i)
                for tok in range(TT):
                    col = i * CC + which * D
                    src = gate[:, tok, col:col + CC] if isinstance(i, int) else gate[:, tok, bass.ds(col, CC)]
                    nc.vector.tensor_tensor(buf[:, tok, :], ps[:, 2 * which + tok, :], src, ALU.mult)\
                        .then_inc(drained[tok], 1)
                if which == 1:
                    for tok in range(TT):
                        dve.wait_ge(drained[tok], i * 2 + (Q_MERGE + 2 + 2))
                    nc.vector.tensor_tensor(m_tmp[:], g_act[:], h_act[:], ALU.add)\
                        .then_inc(sem("merged_ready"), 1)

            def merged_lo(i):
                for j in range(4):
                    dve.wait_ge(sem("merged_hi"), i * 4 + (j + 1 - 4))
                    if isinstance(i, int):
                        lo, hi = mT_lo[:, 4 * (i - 1) + j, :], mT_hi[:, 4 * (i - 1) + j, :]
                    else:
                        kt = bass.ds(i * 4 + (j - 4), 1)
                        lo, hi = (m[:, kt, :].rearrange("p a n -> p (a n)") for m in (mT_lo, mT_hi))
                    nc.vector.tensor_tensor(lo, ps[:, T0 + j, 0:S], hi.bitcast(F32), ALU.subtract)\
                        .then_inc(sem("merged_lo"), 1)

            product_steps(dve, split_lo, B_MERGE, 4, 0,
                          {1: lambda i: branch(i, 0), 3: lambda i: branch(i, 1)})
            with dve.Fori(1, 4) as i:
                product_steps(dve, split_lo, B_MERGE, 4, i,
                              {1: lambda i: (branch(i, 0), merged_lo(i)), 3: lambda i: branch(i, 1)})
            merged_lo(4)

            def add(bank, col):
                def f(i):
                    for tok in range(TT):
                        x = resid[:, tok, bass.ds(i * 2 * CC + col, CC)]
                        nc.vector.tensor_tensor(x, x, ps[:, bank + tok, :], ALU.add).then_inc(drained[tok], 1)
                return f

            with dve.Fori(0, 2) as i:
                product_steps(dve, split_lo, B_WOUT, 8, i, {3: add(0, 0), 7: add(2, CC)})
            dve.wait_ge(drained[1], 2 + Q_GU)

            dve.wait_ge(drained[0], 2 + Q_GU)
            rms_dve(dve, link, 1)
            scale_rows(resid, scaled)
            turned_to_lo(dve, KT, 1)

            def gated(i):
                for tok in range(TT):
                    dve.wait_ge(sem("sig_ready"), i * 2 + (tok + 1))
                    nc.vector.tensor_tensor(g_act[:, tok, :], g_act[:, tok, :], ps[:, tok, :], ALU.mult)\
                        .then_inc(drained[tok], 1)

            def hidden(i):
                for tok in range(TT):
                    dve.wait_ge(drained[tok], i * 2 + (Q_GU + 2 + 1))
                    nc.vector.tensor_tensor(h_act[:, tok, :], g_act[:, tok, :], ps[:, 2 + tok, :], ALU.mult)\
                        .then_inc(drained[tok], 1)

            with dve.Fori(0, 11) as i:
                product_steps(dve, split_lo, B_GU, 8, i, {3: gated, 7: hidden})

            def stage_lo(i, k):
                dve.wait_ge(sem("hidden_hi"), i * 4 + (k + 1))
                if isinstance(i, int):
                    src = actT[:, 4 * i + k, :]
                else:
                    src = actT[:, bass.ds(i * 4 + k, 1), :].rearrange("p a n -> p (a n)")
                nc.vector.tensor_tensor(aT_lo[:, k % 2, :], src, aT_hi[:, k % 2, :].bitcast(F32), ALU.subtract)\
                    .then_inc(sem("hidden_staged"), 1)

            stage_lo(0, 0)
            stage_lo(0, 1)
            with dve.Fori(0, 10) as i:
                for k in range(4):
                    split_lo(dve, B_DOWN, 4, i, k + 2)
                    stage_lo(i, k + 2)
            for k in range(4):
                split_lo(dve, B_DOWN, 4, 10, k + 2)
                if k < 2:
                    stage_lo(10, k + 2)
            chunk_done(dve, B_DOWN, 4, 10, 3)
            for n in range(4):
                for tok in range(TT):
                    x = resid[:, tok, n * CC:(n + 1) * CC]
                    ins = nc.vector.tensor_tensor(x, x, ps[:, 2 * n + tok, :], ALU.add)
                    ins.then_inc(drained[tok] if n < 2 else sem("down_added"), 1)
            dve.wait_ge(sem("down_added"), 4)

            rms_dve(dve, link, 2)
            dve.wait_ge(sem("fin_gain_loaded"), 16)
            for tok in range(TT):
                nc.vector.scalar_tensor_tensor(resid[:, tok, :], resid[:, tok, :], stats[:, 6 + tok:7 + tok],
                                               fin_gain[:], ALU.mult, ALU.mult).then_inc(sem("final_normed"), 1)
            dve.wait_ge(sem("final_normed"), 2)
            rms_dve(dve, link, 3)
            scale_rows(resid, scaled)
            turned_to_lo(dve, 2 * KT, 2)

            def store2(bank, col, width=CC):
                def f(i):
                    dst = z2[:, 1, col:col + width] if isinstance(i, int) else \
                        z2[:, 1, bass.ds(i * 2 * CC + col, width)]
                    nc.vector.tensor_copy(dst, ps[:, bank + 1, 0:width]).then_inc(drained[1], 1)
                return f

            with dve.Fori(0, 7) as i:
                product_steps(dve, split_lo, B_WIN2, 8, i, {3: store2(0, 0), 7: store2(2, CC)})
            product_steps(dve, split_lo, B_WIN2 + 56, 8, 0,
                          {3: store2(0, 14 * CC), 7: store2(2, 15 * CC, N2 - 15 * CC)})

            for j in range(2):
                dve.wait_ge(sem("keys_turned"), j + 3)
                link(nc.vector.tensor_copy(kvcT[:, j, :, :], ps[:, T2 + j, :].rearrange("p (g n) -> p g n", g=2)))
            dve.wait_ge(sem("nsa_loaded"), 80)
            for kv, (hi, lo) in enumerate(((A_hi, A_lo), (A_hi2, A_lo2))):
                for g in range(2):
                    pos = posT[:, kv, :].unsqueeze(2).broadcast_to([P, 32, NCMP])
                    link(nc.vector.tensor_tensor(blkA[:, :, g * NCMP:(g + 1) * NCMP], windows(kv, g), pos, ALU.add))
                link(nc.vector.tensor_copy(hi[:], blkA[:]))
                link(nc.vector.tensor_tensor(lo[:], blkA[:], hi[:].bitcast(F32), ALU.subtract))
            dve.sem_inc(sem("windows_ready"), 1)
            for qt in range(TT):
                c = 159 - P * qt
                link(nc.vector.tensor_copy(biasc[:, :, qt, 0:NCMP], bias2[:, :, c:c + 16 * NCMP - 15:16]))
            dve.wait_ge(sem("gate_exp"), 2)
            link(nc.vector.tensor_scalar(gsig[:], gsig[:], 1.0, None, ALU.add))
            link(nc.vector.reciprocal(gsig[:], gsig[:]))
            for k in range(4):
                split_lo(dve, B_CMP, 4, 0, k + 2)
            dve.wait_ge(sem("hid_exp"), 1)
            link(nc.vector.tensor_scalar(hexp[:, :, 0:30], hexp[:, :, 0:30], 1.0, None, ALU.add))
            link(nc.vector.reciprocal(hexp[:, :, 0:30], hexp[:, :, 0:30]))
            nc.vector.tensor_tensor(hid[:, :, 0:30], ps[:, 0:2, 0:30], hexp[:, :, 0:30], ALU.mult)\
                .then_inc(sem("hid_ready"), 1)
            dve.wait_ge(sem("compressed"), 1)
            link(nc.vector.tensor_copy(vc[0:NCMP, :, :], ps[0:NCMP, 3, 0:256].rearrange("p (g n) -> p g n", g=2)))
            dve.sem_inc(sem("vc_ready"), 1)

            with link.loop(0, 2, 4 * 9) as g:
                for hh in range(4):
                    n = g * 4 + hh
                    nc.vector.tensor_scalar(q2[:], z2[:, :, bass.ds(n * P, P)], float(P) ** -0.5, None, ALU.mult)\
                        .then_inc(sem("q2_staged"), 1)
                    dve.wait_ge(sem("scores2_ready"), n + 1)
                    hb = bias2[:, bass.ds(n, 1), :]
                    for b in range(2):
                        link(nc.vector.tensor_tensor(pr[:, b, 0:P], ps[:, b, 0:P],
                                                     hb[:, :, P:256].rearrange("p a n -> p (a n)"), ALU.add))
                        link(nc.vector.tensor_tensor(pr[:, b, P:384], ps[:, b, P:384],
                                                     hb[:, :, 0:256].rearrange("p a n -> p (a n)"), ALU.add))
                    nc.vector.tensor_tensor(
                        prc[:, :, 0:NCMP], ps[:, 2, 0:32].rearrange("p (t n) -> p t n", t=TT)[:, :, 0:NCMP],
                        biasc[:, bass.ds(n, 1), :, 0:NCMP].rearrange("p a t n -> p (a t) n"), ALU.add)\
                        .then_inc(sem("prc_biased"), 1)
                    dve.wait_ge(sem("prc_biased"), n + 1)
                    link(nc.vector.tensor_reduce(mx2[:, 0:2, 0], pr[:, :, 0:P], AX, ALU.max))
                    link(nc.vector.tensor_reduce(mx2[:, 0:2, 1], pr[:, :, P:384], AX, ALU.max))
                    link(nc.vector.tensor_reduce(mx2[:, 2, :], prc[:, :, 0:NCMP], AX, ALU.max))
                    nc.vector.tensor_scalar(mx2[:], mx2[:], 0.9 * NEG, -1.0, ALU.max, ALU.mult)\
                        .then_inc(sem("nsa_max"), 1)
                    dve.wait_ge(sem("nsa_exp"), n * 6 + 6)
                    nc.vector.tensor_scalar(sm2[:], sm2[:], 1e-30, None, ALU.max).then_inc(sem("sums_kept"), 1)
                    dve.wait_ge(sem("sums_kept"), n + 1)
                    link(nc.vector.reciprocal(sm2[:], sm2[:]))
                    gs = gsig[:].rearrange("p t (b h) -> p b t h", b=3)[:, :, :, bass.ds(n, 1)]
                    link(nc.vector.tensor_tensor(sm2[:], sm2[:], gs.rearrange("p b t a -> p b (t a)"), ALU.mult))
                    for b in range(3):
                        for qt in range(TT):
                            if b == 2:
                                seg = prc[:, qt, 0:NCMP]
                            else:
                                seg = pr[:, b, 0:P] if qt == 0 else pr[:, b, P:384]
                            nc.vector.tensor_scalar(seg, seg, sm2[:, b, qt:qt + 1], None, ALU.mult)\
                                .then_inc(sem("probs2_ready"), 1)
                    dve.wait_ge(sem("probs2_turned"), n + 1)
                    nc.vector.tensor_copy(pT2[:, 1, :], ps[:, T2, 0:384]).then_inc(sem("pT2_ready_1"), 1)

            rwkv_dve(dve, link)

            for j, c in enumerate((C_ZA, C_ZB)):
                dve.wait_ge(sem("z_sig"), j + 1)
                part = slice(1024 * j, 1024 * j + 1024)
                link(nc.vector.tensor_tensor(ysc[:, :, part], ysc[:, :, part], z2[:, :, c:c + 1024], ALU.mult))
                link(nc.vector.tensor_tensor(oy[:, :, part], oy[:, :, part], ysc[:, :, part], ALU.mult))
            dve.sem_inc(sem("mix_ready"), 1)
            turned_to_lo(dve, 3 * KT, None)

            def store3(bank, col):
                def f(i):
                    nc.vector.tensor_copy(y2[:, 1, bass.ds(i * 2 * CC + col, CC)], ps[:, bank + 1, :])\
                        .then_inc(drained[1], 1)
                return f

            with dve.Fori(0, 1) as i:
                product_steps(dve, split_lo, B_WOUT2, 8, i, {3: store3(0, 0), 7: store3(2, CC)})
            for k in range(8):
                if k < 6:
                    split_lo(dve, B_WOUT2 + 8, 8, 0, k + 2)
                if k % 4 == 3:
                    chunk_done(dve, B_WOUT2 + 8, 8, 0, k)
                    nc.vector.tensor_copy(y2[:, 1, (2 + k // 4) * CC:(3 + k // 4) * CC], ps[:, 2 * (k // 4) + 1, :])\
                        .then_inc(drained[1], 1)
            rms_dve(dve, link, 4)
            dve.wait_ge(sem("post_gain_loaded"), 16)
            for tok in range(TT):
                link(nc.vector.scalar_tensor_tensor(y2[:, tok, :], y2[:, tok, :], stats[:, 6 + tok:7 + tok],
                                                    post_gain[:], ALU.mult, ALU.mult))
                nc.vector.tensor_tensor(y2[:, tok, :], y2[:, tok, :], resid[:, tok, :], ALU.add)\
                    .then_inc(sem("out_ready"), 1)

        @block.tensor
        def _(pe):
            pe.wait_ge(sem("rel_loaded"), 64)
            for j in range(3):
                n = min(P, 2 * REL + 1 - j * P)
                nc.tensor.matmul(ps[0:16, 0, 0:384], relT[0:n, j, :], pick_rel[0:n, j, :], start=j == 0, stop=j == 2)
            pe.wait_ge(sem("bucket_loaded"), 48)
            nc.tensor.matmul(ps[0:HN, 1, :], tableT[:], pick_b[:], start=True, stop=True).then_inc(sem("rows_made"), 1)

            pe.wait_ge(sem("ident_loaded"), 16)
            turn_rows(pe, scaled, rows_scaled, TT, 0)

            pe.wait_ge(sem("buck_row_ready"), 1)
            pe.wait_ge(turned_lo, KT)
            plain_product(pe, B_WIN, Q_WIN, 8, xT_hi, xT_lo)

            for tok in range(TT):
                pe.wait_ge(drained[tok], 2 + 16)
            with pe.Fori(0, 8) as i:
                pe.wait_ge(sem("q_staged"), i + 1)
                pe.wait_ge(sem("k_staged"), i + 1)
                for tok in range(TT):
                    nc.tensor.transpose(ps[:, T0, tok * P:(tok + 1) * P], qst[:, tok, :], ident[:])
                    tr = nc.tensor.transpose(ps[:, T1, tok * P:(tok + 1) * P], kst[:, tok, :], ident[:])
                tr.then_inc(sem("qk_turned"), 1)
                pe.wait_ge(sem("qT_ready"), i + 1)
                pe.wait_ge(sem("kT_ready"), i + 1)
                for hd in range(2):
                    h = slice(64 * hd, 64 * hd + 64)
                    nc.tensor.matmul(ps[:, hd, 0:P], qT[h, 0:P], kT[h, 0:P], start=True, stop=True)
                    mm = nc.tensor.matmul(ps[:, hd, P:384], qT[h, P:S], kT[h, :], start=True, stop=True)
                mm.then_inc(sem("scores_ready"), 1)
                pe.wait_ge(sem("probs_ready"), i * 4 + 4)
                for hd in range(2):
                    for j in range(3):
                        tr = nc.tensor.transpose(ps[:, T2 + hd, j * P:(j + 1) * P],
                                                 prob[:, hd, j * P:(j + 1) * P], ident[:])
                tr.then_inc(sem("probs_turned"), 1)
                pe.wait_ge(sem("pT_ready_0"), i + 1)
                pe.wait_ge(sem("pT_ready_1"), i + 1)
                pe.wait_ge(sem("v_staged"), i + 1)
                for hd in range(2):
                    h = slice(64 * hd, 64 * hd + 64)
                    nc.tensor.matmul(ps[h, T0, 0:S], vst[:, 0, h], probT[:, hd, 0:S], start=True, stop=False)
                    mm = nc.tensor.matmul(ps[h, T0, P:S], vst[:, 1, h], probT[:, hd, S:384], start=False, stop=True)
                mm.then_inc(sem("pv_done"), 1)

            pe.wait_ge(sem("att_lo"), 8)
            with pe.Fori(0, 4) as g:
                pe.wait_ge(sem("u_staged"), g + 1)
                pe.wait_ge(sem("pool_loaded"), g * 32 + 32)
                for c in range(2):
                    for t in range(TT):
                        mm = nc.tensor.matmul(ps[:, T0 + c, 0:S], ust[:, t, c * P:(c + 1) * P], rowp[:, t, :],
                                              start=t == 0, stop=t == 1)
                mm.then_inc(sem("pool_mean"), 1)
                pe.wait_ge(sem("dT_ready_0"), g + 1)
                pe.wait_ge(sem("dT_ready_1"), g + 1)
                for e in range(2):
                    for c in range(2):
                        mm = nc.tensor.matmul(ps[:, T2 + e, 0:S], pwg[:, c, e * P:(e + 1) * P], dT[:, c, :],
                                              start=c == 0, stop=c == 1)
                mm.then_inc(sem("pool_mixed"), 1)

            def branches(i, ks, lead=0):
                for k in ks:
                    if k % 2 == 0:
                        acc_free(pe, Q_MERGE + k // 2, i, 2)
                    mm_block(pe, B_MERGE, 4, i, k, xT_hi, xT_lo, 4 * (k % 4), k % 4 // 2 * 2,
                             k % 2 == 0, k % 2 == 1)

            def turn_merged(i):
                pe.wait_ge(sem("merged_ready"), i + 1)
                for j in range(4):
                    for tok in range(TT):
                        tr = nc.tensor.transpose(ps[:, T0 + j, tok * P:(tok + 1) * P],
                                                 m_tmp[:, tok, j * P:(j + 1) * P], ident[:])
                    tr.then_inc(sem("merged_turned"), 1)

            pe.wait_ge(sem("att_lo"), 8)
            pe.wait_ge(sem("pool_lo"), 8)
            branches(0, (0, 1))
            with pe.Fori(0, 3) as i:
                branches(i, (2, 3, 4, 5))
                turn_merged(i)
            branches(3, (2, 3))
            turn_merged(3)

            pe.wait_ge(sem("merged_lo"), KT)
            plain_product(pe, B_WOUT, Q_WOUT, 2, mT_hi, mT_lo)

            turn_rows(pe, scaled, rows_scaled, 2 * TT, KT)

            def up_gate(i, ks):
                for k in ks:
                    if k % 4 == 0:
                        acc_free(pe, Q_GU + k // 4, i, 2)
                    mm_block(pe, B_GU, 8, i, k, xT_hi, xT_lo, 4 * (k % 4), k % 8 // 4 * 2,
                             k % 4 == 0, k % 4 == 3)

            def turn_hidden(i):
                for tok in range(TT):
                    pe.wait_ge(drained[tok], i * 2 + (Q_GU + 2 + 2))
                for j in range(4):
                    for tok in range(TT):
                        c = j % 2 * S + tok * P
                        tr = nc.tensor.transpose(ps[:, T0 + j // 2, c:c + P],
                                                 h_act[:, tok, j * P:(j + 1) * P], ident[:])
                tr.then_inc(sem("hidden_turned"), 1)

            pe.wait_ge(turned_lo, 2 * KT)
            up_gate(0, (0, 1))
            with pe.Fori(0, 10) as i:
                up_gate(i, range(2, 10))
                turn_hidden(i)
            up_gate(10, range(2, 8))
            turn_hidden(10)

            def down_block(i, k, start, stop):
                pe.wait_ge(sem("hidden_staged"), i * 4 + (k + 1))
                pe.wait_ge(block_split, i * 4 + (B_DOWN + k + 1 + RAW_SLOTS))
                for tok in range(TT):
                    xh = aT_hi[:, k % 2, tok * P:(tok + 1) * P]
                    xl = aT_lo[:, k % 2, tok * P:(tok + 1) * P]
                    for n in range(4):
                        wh = w_hi[:, k % 2, n * CC:(n + 1) * CC]
                        wl = w_lo[:, k % 2, n * CC:(n + 1) * CC]
                        o = ps[:, 2 * n + tok, :]
                        nc.tensor.matmul(o, xh, wh, start=start, stop=False)
                        nc.tensor.matmul(o, xh, wl, start=False, stop=False)
                        mm = nc.tensor.matmul(o, xl, wh, start=False, stop=stop)
                mm.then_inc(block_used, 1)

            acc_free(pe, Q_DOWN + 1)
            for k in range(4):
                down_block(0, k, k == 0, False)
            with pe.Fori(1, 10) as i:
                for k in range(4):
                    down_block(i, k, False, False)
            for k in range(4):
                down_block(10, k, False, k == 3)

            pe.wait_ge(sem("down_added"), 4)
            turn_rows(pe, scaled, rows_scaled, 3 * TT, 2 * KT)

            pe.wait_ge(turned_lo, 3 * KT)
            plain_product(pe, B_WIN2, Q_WIN2, 7, xT_hi, xT_lo)
            for c, width in ((14, CC), (15, N2 - 15 * CC)):
                acc_free(pe, Q_WIN2 + c)
                for k in range(4):
                    mm_block(pe, B_WIN2 + 4 * c, 4, 0, k, xT_hi, xT_lo, 4 * k, 2 * (c % 2), k == 0, k == 3, width)

            for tok in range(TT):
                pe.wait_ge(drained[tok], 2 + 68)
            for j, cols_ in enumerate((C_KS, C_KW, C_KC, C_VC)):
                for g in range(2):
                    for tok in range(TT):
                        tr = nc.tensor.transpose(ps[:, T0 + j, g * S + tok * P:g * S + (tok + 1) * P],
                                                 z2[:, tok, cols_ + g * P:cols_ + (g + 1) * P], ident[:])
                tr.then_inc(sem("keys_turned"), 1)
            pe.wait_ge(sem("windows_ready"), 1)
            for k in range(4):
                kv = k // 2
                hi, lo = ((A_hi, A_lo), (A_hi2, A_lo2))[kv]
                pe.wait_ge(block_split, B_CMP + k + 1 + RAW_SLOTS)
                for t in range(16):
                    wh = w_hi[:, k % 2, t * P:(t + 1) * P]
                    wl = w_lo[:, k % 2, t * P:(t + 1) * P]
                    p = 16 * (k % 2) + t
                    o = ps[:, kv, 0:30]
                    nc.tensor.matmul(o, wh, hi[:, p, :], start=p == 0, stop=False)
                    nc.tensor.matmul(o, wh, lo[:, p, :], start=False, stop=False)
                    mm = nc.tensor.matmul(o, wl, hi[:, p, :], start=False, stop=p == 31)
                mm.then_inc(block_used, 1)
            pe.wait_ge(sem("hid_ready"), 1)
            nc.tensor.matmul(ps[:, 2, 0:30], cw2[:, 0, :], hid[:, 0, 0:30], start=True, stop=True)
            for g in range(2):
                mm = nc.tensor.matmul(ps[0:NCMP, 3, g * P:(g + 1) * P], hid[:, 1, g * NCMP:(g + 1) * NCMP],
                                      cw2[:, 1, :], start=True, stop=True)
            mm.then_inc(sem("compressed"), 1)

            pe.wait_ge(sem("kcT_ready"), 1)
            pe.wait_ge(sem("vc_ready"), 1)
            with pe.Fori(0, 2) as g:
                def keysT(b):
                    return KTs[:, b, bass.ds(g, 1), :].rearrange("p a n -> p (a n)")

                for hh in range(4):
                    n = g * 4 + hh
                    pe.wait_ge(sem("q2_staged"), n + 1)
                    for tok in range(TT):
                        tr = nc.tensor.transpose(ps[:, T0, tok * P:(tok + 1) * P], q2[:, tok, :], ident[:])
                    tr.then_inc(sem("q2_turned"), 1)
                    pe.wait_ge(sem("q2T_ready"), n + 1)
                    for qt in range(TT):
                        q = q2T[:, qt * P:(qt + 1) * P]
                        for b in range(2):
                            o = ps[:, b, 0:P] if qt == 0 else ps[:, b, P:384]
                            nc.tensor.matmul(o, q, keysT(b)[:, 0:P] if qt == 0 else keysT(b), start=True, stop=True)
                        mm = nc.tensor.matmul(ps[:, 2, 16 * qt:16 * qt + NCMP], q,
                                              kcT[:, bass.ds(g * NCMP, NCMP)], start=True, stop=True)
                    mm.then_inc(sem("scores2_ready"), 1)
                    pe.wait_ge(sem("probs2_ready"), n * 6 + 6)
                    for b in range(2):
                        for j in range(3):
                            nc.tensor.transpose(ps[:, T1 + b, j * P:(j + 1) * P], pr[:, b, j * P:(j + 1) * P], ident[:])
                    for qt in range(TT):
                        tr = nc.tensor.transpose(ps[0:NCMP, T3, qt * P:(qt + 1) * P], prc[:, qt, 0:NCMP], ident[:])
                    tr.then_inc(sem("probs2_turned"), 1)
                    pe.wait_ge(sem("pT2_ready_0"), n * 2 + 2)
                    pe.wait_ge(sem("pT2_ready_1"), n + 1)
                    for qt in range(TT):
                        o = ps[:, 3, qt * P:(qt + 1) * P]
                        for b, c in enumerate((C_VS, C_VW)):
                            for j in range(qt + 1):
                                seg = (0, P, 2 * P)[qt + j]
                                nc.tensor.matmul(o, pT2[:, b, seg:seg + P], z2[:, j, bass.ds(g * P + c, P)],
                                                 start=b == 0 and j == 0, stop=False)
                        mm = nc.tensor.matmul(o, pcT[0:NCMP, qt * P:(qt + 1) * P],
                                              vc[0:NCMP, bass.ds(g, 1), :].rearrange("p a n -> p (a n)"),
                                              start=False, stop=True)
                    mm.then_inc(sem("pv2_done"), 1)

            rwkv_pe(pe)

            turn_rows(pe, oy, sem("mix_ready"), 1, 3 * KT)

            pe.wait_ge(turned_lo, 4 * KT)
            plain_product(pe, B_WOUT2, Q_WOUT2, 2, xT_hi, xT_lo)


INPUTS = ("x", "norm_mix", "w_in", "rel_bias", "pool_w", "pool_scale", "w_branch_a", "w_branch_b", "w_out",
          "norm_ffn", "w_gate_up", "w_down", "norm_final", "pre_norm_g_2", "w_in_2", "rel_bias_table_2",
          "cmp_pos_k_2", "cmp_pos_v_2", "cmp_k_w1_2", "cmp_k_w2_2", "cmp_v_w1_2", "cmp_v_w2_2", "rwkv_mu_2",
          "rwkv_w0_2", "rwkv_w2_2", "rwkv_a0_2", "rwkv_a2_2", "rwkv_k_k_2", "rwkv_k_a_2", "rwkv_r_k_2",
          "rwkv_ln_w_2", "rwkv_ln_b_2", "w_out_2", "post_norm_g_2")


def kernel(**inputs):
    import numpy as _np
    import concourse.bacc as _bacc
    from concourse.bass_utils import run_bass_kernel_spmd as _run

    nc = _bacc.Bacc("TRN2", target_bir_lowering=False, num_devices=1)
    arrays, aps = {}, {}
    given = {name: _np.ascontiguousarray(inputs[name]) for name in INPUTS}
    for name, value in list(given.items()) + list(shape_constants().items()):
        arrays[f"in_{name}"] = value
        aps[name] = nc.dram_tensor(f"in_{name}", value.shape, F32, kind="ExternalInput").ap()
    out = nc.dram_tensor("out", (1, S, D), F32, kind="ExternalOutput").ap()
    program(nc, aps, out)
    r = _run(nc, [arrays], core_ids=[0])
    return r.results[0]["out"]
```

```python
import math
from contextlib import ExitStack

import numpy as np

import concourse.bass as bass
from concourse import mybir

ALU = mybir.AluOpType
ACT = mybir.ActivationFunctionType
AX = mybir.AxisListType.X
F32 = mybir.dt.float32
F32R = mybir.dt.float32r

P = 128
S = 256
TT = S // P
D = 2048
KT = D // P
CC = 512
BT = 4
BLK = BT * CC
RAW_SLOTS = 4
SPLIT_SLOTS = 2
EPS = 1e-6
NEG = -1e30

AW = 1024
PW = 1024
FF = 5632
FKT = FF // P
REL = 128
HN = 8
NB = 32
NCMP = 15
C_KC, C_VC, C_KS, C_VS, C_KW, C_VW = (1024 + 256 * n for n in range(6))
C_GATE = 2560
C_ZA = 2584
C_R = 3608
C_LORA = C_R + 3072
C_ZB = 6808
N2 = 7832

B_WIN, B_MERGE, B_WOUT, B_GU, B_DOWN, B_WIN2, B_CMP, B_WOUT2 = 0, 64, 80, 96, 184, 228, 292, 296
N_BLOCKS = 312
Q_WIN, Q_MERGE, Q_WOUT, Q_GU, Q_DOWN, Q_WIN2, Q_WOUT2 = 0, 16, 24, 28, 50, 52, 68


def relative_buckets(dist):
    n = np.maximum(dist, 0)
    large = 16 + (np.log(np.maximum(n, 1).astype(np.float32) / np.float32(16))
                  / np.float32(math.log(1024 / 16)) * np.float32(16)).astype(np.int32)
    return np.where(n < 16, n, np.minimum(large, 31))


def shape_constants():
    c = {"ident": np.eye(P, dtype=np.float32)}
    z = np.arange(384)
    dist = 255 - z
    pick = np.zeros((384, 384), np.float32)
    pick[np.clip(dist, -REL, REL) + REL, z] = 1.0
    c["pick_rel"] = pick
    z = np.arange(512)
    dist = 255 - z
    pick = np.zeros((NB, 512), np.float32)
    pick[relative_buckets(dist), z] = 1.0
    c["pick_bucket"] = pick
    c["future"] = np.tile(np.where(dist < 0, NEG, 0.0).astype(np.float32), (HN, 1))
    t = np.arange(S)
    pool = np.zeros((4, S, S), np.float32)
    for g, w in enumerate((2, 4, 8, 16)):
        for tok in range(S):
            lo = max(tok + 1 - w, 0)
            pool[g, lo:tok + 1, tok] = np.float32(1.0) / np.float32(tok + 1 - lo)
            pool[g, tok, tok] -= 1.0
    c["pool_rows"] = pool
    s, q = np.arange(P)[:, None], np.arange(P)[None, :]
    chunk = s // 64 == q // 64
    strict, inclusive = (chunk & (s < q)), (chunk & (s <= q))
    masks = [strict, inclusive, strict, inclusive]
    for level in range(6):
        h = 1 << level
        masks.append((s // (2 * h) == q // (2 * h)) & (s % (2 * h) < h) & (q % (2 * h) >= h))
    masks.append(chunk)
    c["masks"] = np.stack(masks).astype(np.float32)
    return c


def program(nc, a, out):
    with ExitStack() as ctx:
        sems = {}

        def sem(name):
            if name not in sems:
                sems[name] = ctx.enter_context(nc.semaphore(name))
            return sems[name]

        BASE = 16640
        cursor = [BASE]

        def at(name, shape, dt=F32, offset=None):
            if offset is None:
                offset = cursor[0]
                size = 4 * int(np.prod(shape[1:]))
                cursor[0] += -(-size // 32) * 32
                assert cursor[0] <= 229368, (name, cursor[0])
            return nc.alloc_sbuf_tensor_at(name, shape, dt, offset=offset)

        class Region:
            def __init__(self, start, size):
                self.start, self.at, self.end = start, start, start + size

            def __call__(self, name, shape, dt=F32):
                size = -(-4 * int(np.prod(shape[1:])) // 32) * 32
                assert self.at + size <= self.end, (name, self.at + size - self.end)
                t = at(name, shape, dt, self.at)
                self.at += size
                return t

        resid = at("resid", [P, TT, D])
        XT0 = cursor[0]
        xT_hi = at("xT_hi", [P, KT, S], F32R)
        xT_lo = at("xT_lo", [P, KT, S], F32R)
        raw = at("raw", [P, RAW_SLOTS, BLK])
        w_hi = at("w_hi", [P, SPLIT_SLOTS, BLK], F32R)
        w_lo = at("w_lo", [P, SPLIT_SLOTS, BLK], F32R)
        Z0 = cursor[0]
        cursor[0] += 65536
        OY0 = cursor[0]
        cursor[0] += 16384
        ident = at("ident", [P, P])
        per_feature = at("per_feature", [P, 121])
        gains = per_feature[:, 0:48].rearrange("p (g k) -> p g k", g=3)
        pool_scale = per_feature[:, 48:56]
        par = per_feature[:, 56:96].rearrange("p (x k) -> p x k", x=5)
        mu = per_feature[:, 96:121]
        nw0a0 = at("nw0a0", [P, 2, 8])
        stats = at("stats", [P, 4 + 2 * TT])
        rinv = stats[:, 4:8].rearrange("p (x t) -> p x t", x=2)
        F0 = cursor[0]
        FSZ = 229368 - F0
        qkvu = at("qkvu", [P, TT, 4096], F32, Z0)
        gate = at("gate", [P, TT, 2 * D], F32, Z0 + 32768)
        mT_hi = at("mT_hi", [P, KT, S], F32R, Z0)
        mT_lo = at("mT_lo", [P, KT, S], F32R, Z0 + 16384)
        actT = at("actT", [P, FKT, S], F32, Z0)
        z2 = at("z2", [P, TT, N2], F32, Z0)
        scaled = at("scaled", [P, TT, D], F32, OY0)
        oy = at("oy", [P, TT, D], F32, OY0)
        r = Region(OY0, 16384)
        relb = r("relb", [P, 2, 256])
        qst = r("qst", [P, TT, P])
        kst = r("kst", [P, TT, P])
        vst = r("vst", [P, TT, P])
        qkT = r("qkT", [P, 2, S])
        prob = r("prob", [P, 2, 384])
        probT = r("probT", [P, 2, 384])
        r = Region(OY0, 16384)
        g_act = r("g_act", [P, TT, CC])
        h_act = r("h_act", [P, TT, CC])
        m_tmp = r("m_tmp", [P, TT, CC])
        r = Region(F0, FSZ)
        smax = r("smax", [P, 4])
        ssum = r("ssum", [P, 4])
        rowp = r("rowp", [P, 2, S])
        pwg = r("pwg", [P, 2, S])
        ust = r("ust", [P, TT, S])
        dT = r("dT", [P, 2, S])
        r = Region(Z0 + 32768, 32768)
        mix_rows = r("mix_rows", [KT, P])
        par_rows = r("par_rows", [121 - KT, P])
        rel_in = r("rel_in", [16, 2 * REL + 1])
        relT = r("relT", [P, 3, 16])
        pick_rel = r("pick_rel", [P, 3, 384])
        rel_row = r("rel_row", [16, 384])
        pick_b = r("pick_b", [NB, 512])
        future = r("future", [HN, 512])
        buck_row = r("buck_row", [HN, 512])
        tableT = r("tableT", [NB, HN])
        r = Region(F0, FSZ)
        aT_hi = r("aT_hi", [P, 2, S], F32R)
        aT_lo = r("aT_lo", [P, 2, S], F32R)
        fin_gain = at("fin_gain", [P, D], F32, XT0)
        r = Region(XT0, 32768)
        bias2 = r("bias2", [P, HN, 384])
        biasc = r("biasc", [P, HN, TT, 16])
        KTs = r("KTs", [P, 2, 2, S])
        kvcT = r("kvcT", [P, 2, 2, S])
        posT = r("posT", [P, 2, 32])
        blkA = at("blkA", [P, 32, 30], F32, OY0)
        A_hi = at("A_hi", [P, 32, 30], F32R, OY0 + 3840)
        A_lo = at("A_lo", [P, 32, 30], F32R, OY0 + 7680)
        A_hi2 = at("A_hi2", [P, 32, 30], F32R, OY0 + 11520)
        r = Region(F0, FSZ)
        pT2 = at("pT2", [P, 2, 384], F32, r.at)
        A_lo2 = r("A_lo2", [P, 32, 30], F32R)
        cw2 = r("cw2", [P, 2, P])
        hid = r("hid", [P, 2, 32])
        hexp = r("hexp", [P, 2, 32])
        kcT = r("kcT", [P, 32])
        vc = r("vc", [16, 2, P])
        gsig = r("gsig", [P, TT, 24])
        q2 = r("q2", [P, TT, P])
        q2T = r("q2T", [P, S])
        pr = r("pr", [P, 2, 384])
        prc = r("prc", [P, TT, 16])
        mx2 = r("mx2", [P, 3, TT])
        sm2 = r("sm2", [P, 3, TT])
        pcT = r("pcT", [16, S])
        r = Region(XT0, 32768)
        bv = r("bv", [P, TT, 1024])
        masks = r("masks", [P, 11, P])
        l2 = r("l2", [P, 1024])
        l2s = r("l2s", [P, P])
        lora = r("lora", [P, S])
        ar = r("ar", [P, TT, 2, P])
        bT = r("bT", [P, TT, P])
        kTt = r("kTt", [P, TT, P])
        tokm = r("tokm", [P, TT, 4, P])
        snap = r("snap", [P, 4, P])
        AtT = r("AtT", [P, TT, P])
        Ml1 = r("Ml1", [P, 4, P])
        r = Region(Z0, 10240)
        Mm = r("Mm", [P, 4, 4, P])
        Ml0 = r("Ml0", [P, 4, P])
        r = Region(Z0 + 4 * N2, 10240)
        TX = r("TX", [P, 2, 4, P])
        Tm, Xm = TX[:, 0, :, :], TX[:, 1, :, :]
        Ym = r("Ym", [P, 4, P])
        stg = r("stg", [P, TT, 3, P])
        r = Region(F0, FSZ)
        fT = r("fT", [P, 3, S + 1])
        pf = r("pf", [P, 3, S])
        wa = r("wa", [P, 2, S])
        Pc = r("Pc", [P, 4, 65])
        iP = r("iP", [P, S])
        kkn = r("kkn", [P, S])
        tmpf = r("tmpf", [P, S])
        zero64 = r("zero64", [P, 64])
        W1 = r("W1", [P, TT, 2, 64])
        Uu = r("Uu", [P, TT, 2, 64])
        bon = r("bon", [P, TT, 2])
        st16 = r("st16", [P, 2, TT, 16])
        r = Region(XT0 + 8192, 24576)
        ysq = r("ysq", [P, TT, 1024])
        lnw = r("lnw", [P, 1024])
        lnb = r("lnb", [P, 1024])
        y2 = at("y2", [P, TT, D], F32, Z0)
        post_gain = at("post_gain", [P, D], F32, Z0 + 16384)
        ysc = at("ysc", [P, TT, D], F32, XT0)

        ps = ctx.enter_context(nc.psum_tensor("ps", [P, 8, 512], F32))

        rel_dram = nc.dram_tensor("rel_row_dram", (16, 384), F32, kind="Internal").ap()
        rel_rows = nc.dram_tensor("rel_rows_dram", (P, 16, 384), F32, kind="Internal").ap()
        buck_rows = nc.dram_tensor("buck_rows_dram", (P, HN, 512), F32, kind="Internal").ap()
        buck_dram = nc.dram_tensor("buck_row_dram", (HN, 512), F32, kind="Internal").ap()

        landed = [sem(f"block_landed_{s}") for s in range(RAW_SLOTS)]
        hi_ready, block_split, block_used = sem("hi_ready"), sem("block_split"), sem("block_used")
        drained = [sem("acc_drained_0"), sem("acc_drained_1")]
        class Chain:
            def __init__(self, eng, name):
                self.eng, self.sem, self.base, self.n = eng, sem(name), 0, 0

            def __call__(self, ins):
                ins.then_inc(self.sem, 1)
                self.n += 1
                self.eng.wait_ge(self.sem, self.base + self.n)

            def loop(self, start, end, n):
                return ChainLoop(self, start, end, n)

        class ChainLoop:
            def __init__(self, chain, start, end, n):
                self.c, self.start, self.end, self.per = chain, start, end, n

            def __enter__(self):
                self.f = self.c.eng.Fori(self.start, self.end)
                i = self.f.__enter__()
                self.b0 = self.c.base + self.c.n
                self.c.base, self.c.n = (i - self.start) * self.per + self.b0 if self.start else i * self.per + self.b0, 0
                return i

            def __exit__(self, *e):
                r = self.f.__exit__(*e)
                if e[0] is None:
                    assert self.c.n == self.per, (self.c.n, self.per)
                    self.c.base, self.c.n = self.b0 + self.per * (self.end - self.start), 0
                return r

        def blocks_of(w, col0=0, width=CC):
            return w.rearrange("(t p) n -> p t n", p=P)

        W = {k: blocks_of(a[k][0]) for k in ("w_in", "w_branch_a", "w_branch_b", "w_out", "w_gate_up",
                                            "w_in_2", "w_out_2", "cmp_k_w1_2", "cmp_v_w1_2")}
        w_down = a["w_down"][0].rearrange("(t p) n -> t p n", p=P)

        def load(sp, k, dst, src, b_const, b_reg=None, group=4):
            sp.wait_ge(block_split, b_const + 1 if b_reg is None else b_reg + (b_const + 1))
            sp.dma_start(dst, src).then_inc(landed[k % 4], 16)

        def slot(k, width=CC):
            return raw[:, k % 4, 0:BT * width].rearrange("p (t n) -> p t n", t=BT)

        def cols(w, kb, c0, width=CC):
            return w[:, kb * BT:(kb + 1) * BT, c0:c0 + width]

        def dcols(w, kb, creg, width=CC):
            return w[:, kb * BT:(kb + 1) * BT, bass.ds(creg, width)]

        def stream(sp, i, phase, k):
            if phase == "w_in":
                load(sp, k, slot(k), dcols(W["w_in"], k, i * CC), B_WIN + k, i * 4)
            elif phase == "merge":
                w = W["w_branch_a"] if k < 2 else W["w_branch_b"]
                load(sp, k, slot(k), dcols(w, k % 2, i * CC), B_MERGE + k, i * 4)
            elif phase == "w_out":
                load(sp, k, slot(k), dcols(W["w_out"], k, i * CC), B_WOUT + k, i * 4)
            elif phase == "gate_up":
                c = i * CC if k < 4 else i * CC + FF
                load(sp, k, slot(k), dcols(W["w_gate_up"], k % 4, c), B_GU + k, i * 8)
            elif phase == "down":
                load(sp, k, raw[:, k % 4, :],
                     w_down[bass.ds(i * 4 + k, 1)].rearrange("a p n -> (a p) n"), B_DOWN + k, i * 4)
            elif phase == "w_in2":
                load(sp, k, slot(k), dcols(W["w_in_2"], k, i * CC), B_WIN2 + k, i * 4)
            elif phase == "w_in2_tail":
                load(sp, k, slot(k, N2 - 15 * CC), cols(W["w_in_2"], k, 15 * CC, N2 - 15 * CC), B_WIN2 + 60 + k)
            elif phase == "compress":
                w = W["cmp_k_w1_2"] if k < 2 else W["cmp_v_w1_2"]
                load(sp, k, raw[:, k % 4, :].rearrange("p (t n) -> p t n", t=16),
                     w[:, (k % 2) * 16:(k % 2) * 16 + 16, :], B_CMP + k)
            elif phase == "w_out2":
                load(sp, k, slot(k), dcols(W["w_out_2"], k, i * CC), B_WOUT2 + k, i * 4)

        STREAMS = [("w_in", 16, 4), ("merge", 4, 4), ("w_out", 4, 4), ("gate_up", 11, 8), ("down", 11, 4),
                   ("w_in2", 15, 4), ("w_in2_tail", 0, 4), ("compress", 0, 4), ("w_out2", 4, 4)]

        def split_hi(act, b0, per, i, k):
            assert b0 % 4 == 0 and per % 4 == 0
            act.wait_ge(landed[k % 4], i * (4 * per) + 16 * ((b0 + k) // 4 + 1))
            act.wait_ge(block_used, i * per + (b0 + k + 1))
            nc.scalar.copy(w_hi[:, k % 2, :], raw[:, k % 4, :]).then_inc(hi_ready, 1)

        def split_lo(dve, b0, per, i, k):
            dve.wait_ge(hi_ready, i * per + (b0 + k + 1))
            nc.vector.tensor_tensor(w_lo[:, k % 2, :], raw[:, k % 4, :], w_hi[:, k % 2, :].bitcast(F32),
                                    ALU.subtract).then_inc(block_split, 1)

        def chunk_done(eng, b0, per, i, k):
            eng.wait_ge(block_used, i * per + (b0 + k + 1 + SPLIT_SLOTS))

        def product_steps(eng, split, b0, per, i, ends, before={}):
            for k in range(per):
                for step in before.get(k, ()):
                    step(i)
                split(eng, b0, per, i, k + 2)
                if k in ends:
                    chunk_done(eng, b0, per, i, k)
                    ends[k](i)

        def mm_block(pe, b0, per, i, k, hi, lo, kt0, bank, start, stop, width=CC):
            pe.wait_ge(block_split, i * per + (b0 + k + 1 + RAW_SLOTS))
            for t in range(BT):
                for tok in range(TT):
                    xh = hi[:, kt0 + t, tok * P:(tok + 1) * P]
                    xl = lo[:, kt0 + t, tok * P:(tok + 1) * P]
                    wh = w_hi[:, k % 2, t * width:(t + 1) * width]
                    wl = w_lo[:, k % 2, t * width:(t + 1) * width]
                    o = ps[:, bank + tok, 0:width]
                    nc.tensor.matmul(o, xh, wh, start=start and t == 0, stop=False)
                    nc.tensor.matmul(o, xh, wl, start=False, stop=False)
                    mm = nc.tensor.matmul(o, xl, wh, start=False, stop=stop and t == BT - 1)
            mm.then_inc(block_used, 1)

        def acc_free(pe, q, i=0, per=0):
            for tok in range(TT):
                pe.wait_ge(drained[tok], i * per + (q + 1))

        def plain_product(pe, b0, q0, n2, hi, lo, first=0, between=None):
            with pe.Fori(first, n2) as i:
                for c in range(2):
                    if between:
                        between(i, c, 0)
                    acc_free(pe, q0 + c, i, 2)
                    for k in range(4):
                        if between and k:
                            between(i, c, k)
                        mm_block(pe, b0, 8, i, 4 * c + k, hi, lo, 4 * k, 2 * c, k == 0, k == 3)
                    if between:
                        between(i, c, 4)

        def branch_inputs(x, j):
            n = P if j < 2 else S
            return (x[:, 4 * j:4 * j + 4, :].rearrange("p i (t n) -> p t i n", t=TT) if j < 2 else
                    x[:, 4 * j:4 * j + 4, :].rearrange("p (i t) n -> p t i n", t=TT),
                    qkvu[:, :, (0, CC, 3072, 3072 + CC)[j]:(CC, 2 * CC, 3072 + CC, 4096)[j]]
                    .rearrange("p t (i n) -> p t i n", n=n))

        turned, turned_hi, turned_lo = sem("tile_turned"), sem("turned_hi"), sem("turned_lo")

        def turn_rows(pe, src, base, kts=range(KT)):
            for kt in kts:
                n = base + kt
                if n >= 4:
                    pe.wait_ge(turned_lo, n - 3)
                for tok in range(TT):
                    tr = nc.tensor.transpose(ps[:, 4 + n % 4, tok * P:(tok + 1) * P],
                                             src[:, tok, kt * P:(kt + 1) * P], ident[:])
                tr.then_inc(turned, 1)

        def turned_to_hi(act, base, g, kts=range(KT)):
            for kt in kts:
                n = base + kt
                act.wait_ge(turned, n + 1)
                scale = gains[:, g, kt:kt + 1] if g is not None else 1.0
                nc.scalar.activation(xT_hi[:, kt, :], ps[:, 4 + n % 4, 0:S], ACT.Copy,
                                     scale=scale).then_inc(turned_hi, 1)

        def turned_to_lo(dve, base, g, kts=range(KT)):
            for kt in kts:
                n = base + kt
                dve.wait_ge(turned_hi, n + 1)
                src, hi = ps[:, 4 + n % 4, 0:S], xT_hi[:, kt, :].bitcast(F32)
                if g is None:
                    ins = nc.vector.tensor_tensor(xT_lo[:, kt, :], src, hi, ALU.subtract)
                else:
                    ins = nc.vector.scalar_tensor_tensor(xT_lo[:, kt, :], src, gains[:, g, kt:kt + 1],
                                                         hi, ALU.mult, ALU.subtract)
                ins.then_inc(turned_lo, 1)

        def rms_act(act, x, scratch, n):
            for tok in range(TT):
                nc.scalar.activation(scratch[:, tok, :], x[:, tok, :], ACT.Square,
                                     accum_out=stats[:, tok:tok + 1]).then_inc(sem("square_sums"), 1)
            act.wait_ge(sem("mean_squares"), n + 1)
            nc.scalar.activation(stats[:, 2:4], stats[:, 0:2], ACT.Sqrt).then_inc(sem("rms_roots"), 1)

        def rms_dve(dve, link, n):
            dve.wait_ge(sem("square_sums"), TT * (n + 1))
            nc.vector.tensor_scalar(stats[:, 0:2], stats[:, 0:2], 1.0 / D, EPS, ALU.mult, ALU.add)\
                .then_inc(sem("mean_squares"), 1)
            dve.wait_ge(sem("rms_roots"), n + 1)
            nc.vector.reciprocal(rinv[:, n % 2, :], stats[:, 2:4]).then_inc(sem("rinv_ready"), 1)
            dve.wait_ge(sem("rinv_ready"), n + 1)


        T0, T1, T2, T3 = 4, 5, 6, 7

        def shifted(rows, width):
            _, heads, pitch = rows.shape
            return bass.AP(tensor=rows.tensor, offset=P - 1, ap=[[heads * pitch - 1, P], [pitch, heads], [1, width]])

        def windows(kv, g):
            v = kvcT[:, kv, g, :]
            return bass.AP(tensor=v.tensor, offset=v.offset, ap=[list(v.ap[0]), [1, 32], [16, NCMP]])

        LEVELS = 5
        HALF = float(np.float32(math.exp(-0.5)))

        def rwkv_act(act, link):
            act.wait_ge(sem("lora_turned"), 1)
            act.wait_ge(sem("edges_set"), 1)
            nc.scalar.copy(fT[:, 0, 1:S + 1], ps[:, T0, 0:S]).then_inc(sem("lora_copied"), 1)
            act.wait_ge(sem("lora_mixed"), 1)
            nc.scalar.activation(lora[0:64, :], lora[0:64, :], ACT.Tanh).then_inc(sem("lora_ready"), 1)
            act.wait_ge(sem("rwkv_loaded"), 48)

            def stage(i):
                for x in range(3):
                    nc.scalar.copy(stg[:, :, x, :], z2[:, :, bass.ds(i * P + (C_R + 1024 * x), P)])\
                        .then_inc(sem("feat_staged"), 1)
                nc.scalar.copy(l2s[:], l2[:, bass.ds(i * P, P)]).then_inc(sem("l2_staged"), 1)

            def features(i):
                act.wait_ge(sem("feat_turned"), i + 1)
                nc.scalar.copy(fT[:, 0:2, 1:S + 1], ps[:, T0, :].rearrange("p (x n) -> p x n", x=2))\
                    .then_inc(sem("fT_ready"), 1)
                nc.scalar.copy(fT[:, 2, 1:S + 1], ps[:, T1, 0:S]).then_inc(sem("fT_ready"), 1)

            def exps(i):
                act.wait_ge(sem("lora_done"), i + 1)
                for x in range(2):
                    nc.scalar.activation(wa[:, x, :], ps[:, T2 + x, 0:S], ACT.Exp, scale=-1.0,
                                         bias=nw0a0[:, x, bass.ds(i, 1)]).then_inc(sem("wa_exp"), 1)

            def decay(i):
                act.wait_ge(sem("wa_sigmoid"), i + 1)
                nc.scalar.activation(wa[:, 0, :], wa[:, 0, :], ACT.Exp, scale=-HALF).then_inc(sem("decay_ready"), 1)

            def norm(i):
                act.wait_ge(sem("kk_summed"), i + 1)
                nc.scalar.activation(tmpf[:], ps[:, T0, 0:S], ACT.Sqrt).then_inc(sem("kk_norm"), 1)

            def pair(i, ahead):
                act.wait_ge(sem("tok_turned"), i + 1)
                nc.scalar.copy(tokm[:, 0, :, :], ps[:, T1, :].rearrange("p (x n) -> p x n", x=4))\
                    .then_inc(sem("tokm_ready_0"), 1)
                if ahead:
                    stage(i + 1)
                for h in range(2):
                    act.wait_ge(sem("x1_turned"), i * 2 + (h + 1))
                    nc.scalar.copy(Tm[:, 2 * h:2 * h + 2, :], ps[:, h, 0:S].rearrange("p (m n) -> p m n", m=2))\
                        .then_inc(sem("t1_ready"), 1)
                for lev in range(LEVELS):
                    for h in range(2):
                        act.wait_ge(sem("y_made"), i * (2 * LEVELS) + (2 * lev + h + 1))
                        nc.scalar.copy(Ym[:, 2 * h:2 * h + 2, :], ps[:, h, 0:S].rearrange("p (m n) -> p m n", m=2))\
                            .then_inc(sem("y_copied"), 1)
                    if ahead and lev < 4:
                        (features, exps, decay, norm)[lev](i + 1)
                act.wait_ge(sem("at_made"), i + 1)
                nc.scalar.copy(AtT[:], ps[:, 1, 0:S].rearrange("p (t n) -> p t n", t=TT)).then_inc(sem("at_ready"), 1)

            stage(0)
            for step in (features, exps, decay, norm):
                step(0)
            with act.Fori(0, 7) as i:
                pair(i, True)
            pair(7, False)
            act.wait_ge(sem("gn_var"), 1)
            nc.scalar.activation(st16[:, 1, :, :], st16[:, 1, :, :], ACT.Sqrt).then_inc(sem("gn_root"), 1)

        def rwkv_dve(dve, link):
            dve.wait_ge(sem("nsa_out_ready"), HN)
            link(nc.vector.memset(fT[:, :, 0:1], 0.0))
            link(nc.vector.memset(zero64[:], 0.0))
            link(nc.vector.memset(Pc[:, :, 0:1], 1.0))
            link(nc.vector.memset(snap[:, 0, :], 0.0))
            link(nc.vector.tensor_scalar(nw0a0[:], par[:, 0:2, :], -1.0, None, ALU.mult))
            dve.sem_inc(sem("edges_set"), 1)
            dve.wait_ge(sem("lora_copied"), 1)
            link(nc.vector.tensor_tensor(lora[:], fT[:, 0, 0:S], fT[:, 0, 1:S + 1], ALU.subtract))
            link(nc.vector.scalar_tensor_tensor(lora[:], lora[:], mu[:, 24:25], fT[:, 0, 1:S + 1], ALU.mult, ALU.add))
            dve.sem_inc(sem("lora_mixed"), 1)
            dve.wait_ge(sem("rwkv_loaded"), 48)


            def shift(i):
                dve.wait_ge(sem("fT_ready"), i * 2 + 2)
                link(nc.vector.tensor_tensor(pf[:], fT[:, :, 0:S], fT[:, :, 1:S + 1], ALU.subtract))
                for x in range(3):
                    link(nc.vector.scalar_tensor_tensor(pf[:, x, :], pf[:, x, :], mu[:, bass.ds(i + 8 * x, 1)],
                                                        fT[:, x, 1:S + 1], ALU.mult, ALU.add))
                link(nc.vector.tensor_scalar(kkn[:], pf[:, 1, :], par[:, 2, bass.ds(i, 1)], None, ALU.mult))
                link(nc.vector.tensor_tensor(tmpf[:], kkn[:], kkn[:], ALU.mult))
                dve.sem_inc(sem("kk_squared"), 1)

            def sigmoids(i):
                dve.wait_ge(sem("wa_exp"), i * 2 + 2)
                link(nc.vector.tensor_scalar(wa[:], wa[:], 1.0, None, ALU.add))
                link(nc.vector.reciprocal(wa[:], wa[:]))
                dve.sem_inc(sem("wa_sigmoid"), 1)

            def normed(i):
                dve.wait_ge(sem("kk_norm"), i + 1)
                link(nc.vector.tensor_scalar(tmpf[:], tmpf[:], 1e-12, None, ALU.max))
                link(nc.vector.reciprocal(tmpf[:], tmpf[:]))
                link(nc.vector.tensor_tensor(kkn[:], kkn[:], tmpf[:], ALU.mult))

            def pair(i, ahead):
                dve.wait_ge(sem("decay_ready"), i + 1)
                for c in range(4):
                    link(nc.vector.tensor_tensor_scan(Pc[:, c, 1:65], wa[:, 0, 64 * c:64 * c + 64], zero64[:], 1.0,
                                                      ALU.mult, ALU.add))
                link(nc.vector.reciprocal(iP[:].rearrange("p (c n) -> p c n", c=4), Pc[:, :, 1:65]))
                for t in range(TT):
                    kv = kkn[:, t * P:(t + 1) * P].rearrange("p (c n) -> p c n", c=2)
                    rv = pf[:, 0, t * P:(t + 1) * P].rearrange("p (c n) -> p c n", c=2)
                    link(nc.vector.scalar_tensor_tensor(ar[:, t, 0, :].rearrange("p (c n) -> p c n", c=2), kv, -1.0,
                                                        Pc[:, 2 * t:2 * t + 2, 0:64], ALU.mult, ALU.mult))
                    link(nc.vector.tensor_tensor(ar[:, t, 1, :].rearrange("p (c n) -> p c n", c=2), rv,
                                                 Pc[:, 2 * t:2 * t + 2, 1:65], ALU.mult))
                link(nc.vector.tensor_tensor(kkn[:], kkn[:], wa[:, 1, :], ALU.mult))
                link(nc.vector.tensor_tensor(bT[:].rearrange("p t n -> p (t n)"), kkn[:], iP[:], ALU.mult))
                link(nc.vector.tensor_scalar(wa[:, 0, :], wa[:, 1, :], 1.0, par[:, 3, bass.ds(i, 1)],
                                             ALU.subtract, ALU.mult))
                link(nc.vector.scalar_tensor_tensor(wa[:, 0, :], wa[:, 0, :], 1.0, pf[:, 1, :], ALU.add, ALU.mult))
                link(nc.vector.tensor_tensor(kTt[:].rearrange("p t n -> p (t n)"), wa[:, 0, :], iP[:], ALU.mult))
                link(nc.vector.scalar_tensor_tensor(tmpf[:], pf[:, 0, :], par[:, 4, bass.ds(i, 1)], wa[:, 0, :],
                                                    ALU.mult, ALU.mult))
                dve.sem_inc(sem("features_ready"), 1)
                dve.wait_ge(sem("m_made"), i + 1)
                for m in range(4):
                    link(nc.vector.tensor_tensor(Mm[:, m, :, :], ps[:, m, :].rearrange("p (x n) -> p x n", x=4),
                                                 masks[:, 0:4, :], ALU.mult))
                dve.sem_inc(sem("m_masked"), 1)
                for h in range(2):
                    x = Xm[:, 2 * h:2 * h + 2, :]
                    link(nc.vector.tensor_tensor(x, Mm[:, 2 * h:2 * h + 2, 0, :],
                                                 masks[:, 4:5, :].broadcast_to([P, 2, P]), ALU.mult))
                    link(nc.vector.tensor_tensor(x, x, ident[:].unsqueeze(1).broadcast_to([P, 2, P]), ALU.add))
                    dve.sem_inc(sem("x1_ready"), 1)
                dve.wait_ge(sem("tok_turned"), i + 1)
                link(nc.vector.tensor_copy(tokm[:, 1, :, :], ps[:, T2, :].rearrange("p (x n) -> p x n", x=4)))
                dve.sem_inc(sem("tokm_ready_1"), 1)
                link(nc.vector.tensor_copy(bon[:], ps[:, T3, 0:4].rearrange("p (t h) -> p t h", t=TT)))
                dve.sem_inc(sem("bonus_read"), 1)
                for lev in range(LEVELS):
                    for h in range(2):
                        dve.wait_ge(sem("level_made"), i * (2 * LEVELS) + (2 * lev + h + 1))
                        if lev < LEVELS - 1:
                            x = TX[:, :, 2 * h:2 * h + 2, :].rearrange("p x m n -> p x (m n)")
                            d = ps[:, 2 + h, :].rearrange("p (x n) -> p x n", x=2)
                        else:
                            x = Xm[:, 2 * h:2 * h + 2, :].rearrange("p m n -> p (m n)")
                            d = ps[:, 2 + h, S:2 * S]
                        nc.vector.tensor_tensor(x, x, d, ALU.add).then_inc(sem("level_added"), 1)
                    if lev == 0:
                        dve.wait_ge(sem("tokm_ready_0"), i + 1)
                        for t in range(TT):
                            for hd in range(2):
                                nc.vector.tensor_scalar(bv[:, t, bass.ds(i * P + 64 * hd, 64)],
                                                        tokm[:, t, 3, 64 * hd:64 * hd + 64], bon[:, t, hd:hd + 1],
                                                        None, ALU.mult).then_inc(sem("bonus_ready"), 1)
                    if ahead and 1 <= lev <= 2:
                        (shift, sigmoids)[lev - 1](i + 1)
                if ahead:
                    normed(i + 1)
                dve.wait_ge(sem("w0_made"), i + 1)
                link(nc.vector.tensor_copy(Uu[:].rearrange("p t h n -> p (t h n)"), ps[:, 0, 0:S]))
                dve.sem_inc(sem("w0_ready"), 1)
                dve.wait_ge(sem("w1_made"), i + 1)
                link(nc.vector.tensor_copy(W1[:].rearrange("p t h n -> p (t h n)"), ps[:, 2, 0:S]))
                for c in range(4):
                    t, rows = c // 2, slice(64 * (c % 2), 64 * (c % 2) + 64)
                    dve.wait_ge(sem("u_made"), i * 4 + (c + 1))
                    nc.vector.tensor_tensor(Uu[rows, t, :, :].rearrange("p h n -> p (h n)"), ps[rows, 0, 0:P],
                                            W1[rows, t, :, :].rearrange("p h n -> p (h n)"), ALU.add)\
                        .then_inc(sem("u_ready"), 1)
                    if c < 3:
                        dve.wait_ge(sem("s_made"), i * 3 + (c + 1))
                        nc.vector.tensor_tensor(snap[:, c + 1, :], ps[:, 3, 0:P], snap[:, c, :], ALU.add)\
                            .then_inc(sem("s_added"), 1)
                        dve.wait_ge(sem("s_added"), i * 3 + (c + 1))
                        nc.vector.scalar_tensor_tensor(snap[:, c + 1, :], snap[:, c + 1, :], Pc[:, c, 64:65],
                                                       masks[:, 10, :], ALU.mult, ALU.mult)\
                            .then_inc(sem("s_ready"), 1)
                        dve.wait_ge(sem("s_ready"), i * 3 + (c + 1))
                dve.wait_ge(sem("y_out_made"), i + 1)
                nc.vector.tensor_copy(oy[:, :, bass.ds(i * P + 1024, P)],
                                      ps[:, 1, 0:S].rearrange("p (t n) -> p t n", t=TT)).then_inc(sem("pair_done"), 1)

            shift(0)
            sigmoids(0)
            normed(0)
            with link.loop(0, 7, 38) as i:
                pair(i, True)
            pair(7, False)
            dve.wait_ge(sem("pair_done"), 8)
            dve.wait_ge(sem("bonus_ready"), 32)
            yh = oy[:, :, 1024:D].rearrange("p t (h n) -> p t h n", h=16)
            yq = ysq[:].rearrange("p t (h n) -> p t h n", h=16)
            mean, var = st16[:, 0, :, :], st16[:, 1, :, :]
            wide = [P, TT, 16, 64]
            link(nc.vector.tensor_reduce(mean, yh, AX, ALU.add))
            link(nc.vector.tensor_scalar(mean, mean, 1.0 / 64, None, ALU.mult))
            link(nc.vector.tensor_tensor(yh, yh, mean.unsqueeze(3).broadcast_to(wide), ALU.subtract))
            link(nc.vector.tensor_tensor(yq, yh, yh, ALU.mult))
            link(nc.vector.tensor_reduce(var, yq, AX, ALU.add))
            link(nc.vector.tensor_scalar(var, var, 1.0 / 64, 64e-5, ALU.mult, ALU.add))
            dve.sem_inc(sem("gn_var"), 1)
            dve.wait_ge(sem("gn_root"), 1)
            link(nc.vector.reciprocal(var, var))
            link(nc.vector.tensor_tensor(yh, yh, var.unsqueeze(3).broadcast_to(wide), ALU.mult))
            dve.wait_ge(sem("ln_loaded"), 32)
            y = oy[:, :, 1024:D]
            link(nc.vector.tensor_tensor(y, y, lnw[:].unsqueeze(1).broadcast_to([P, TT, 1024]), ALU.mult))
            link(nc.vector.tensor_tensor(y, y, lnb[:].unsqueeze(1).broadcast_to([P, TT, 1024]), ALU.add))
            link(nc.vector.tensor_tensor(y, y, bv[:], ALU.add))
            dve.sem_inc(sem("rwkv_done"), 1)

        def rwkv_pe(pe):
            for tok in range(TT):
                tr = nc.tensor.transpose(ps[:, T0, tok * P:(tok + 1) * P], z2[:, tok, C_LORA:C_LORA + P], ident[:])
            tr.then_inc(sem("lora_turned"), 1)
            pe.wait_ge(sem("lora_ready"), 1)

            def turn_features(i):
                pe.wait_ge(sem("feat_staged"), i * 3 + 3)
                for x in range(3):
                    for tok in range(TT):
                        c = (x % 2) * S + tok * P
                        tr = nc.tensor.transpose(ps[:, T0 + x // 2, c:c + P], stg[:, tok, x, :], ident[:])
                tr.then_inc(sem("feat_turned"), 1)

            def low_rank(i):
                pe.wait_ge(sem("l2_staged"), i + 1)
                nc.tensor.matmul(ps[:, T2, 0:S], l2s[0:64, :], lora[0:64, :], start=True, stop=True)
                nc.tensor.matmul(ps[:, T3, 0:S], l2s[64:128, :], lora[64:128, :], start=True, stop=True)\
                    .then_inc(sem("lora_done"), 1)

            def kk_sums(i):
                pe.wait_ge(sem("kk_squared"), i + 1)
                nc.tensor.matmul(ps[:, T0, 0:S], masks[:, 10, :], tmpf[:], start=True, stop=True)\
                    .then_inc(sem("kk_summed"), 1)

            def pair(i, ahead):
                pe.wait_ge(sem("features_ready"), i + 1)
                for tok in range(TT):
                    for x, src in enumerate((ar[:, tok, 0, :], bT[:, tok, :], kTt[:, tok, :],
                                             pf[:, 2, tok * P:(tok + 1) * P])):
                        nc.tensor.transpose(ps[:, T1 + tok, x * P:(x + 1) * P], src, ident[:])
                for tok in range(TT):
                    mm = nc.tensor.matmul(ps[:, T3, 2 * tok:2 * tok + 2], tmpf[:, tok * P:(tok + 1) * P],
                                          masks[:, 10, 0:P:64], start=True, stop=True)
                mm.then_inc(sem("tok_turned"), 1)
                for tok in range(TT):
                    for src, c in ((bT, 0), (kTt, S)):
                        for hd in range(2):
                            h = slice(64 * hd, 64 * hd + 64)
                            mm = nc.tensor.matmul(ps[:, 2 * tok + hd, c:c + S], src[h, tok, :],
                                                  ar[h, tok, :, :].rearrange("p x n -> p (x n)"), start=True, stop=True)
                mm.then_inc(sem("m_made"), 1)
                for h in range(2):
                    pe.wait_ge(sem("x1_ready"), i * 2 + (h + 1))
                    for m in range(2):
                        tr = nc.tensor.transpose(ps[:, h, m * P:(m + 1) * P], Xm[:, 2 * h + m, :], ident[:])
                    tr.then_inc(sem("x1_turned"), 1)
                if ahead:
                    pe.wait_ge(sem("tokm_ready_0"), i + 1)
                    pe.wait_ge(sem("bonus_read"), i + 1)
                    turn_features(i + 1)
                    low_rank(i + 1)
                for lev in range(LEVELS):
                    Ml = (Ml0, Ml1)[lev % 2]
                    pe.wait_ge(sem("level_ready"), i * LEVELS + (lev + 1))
                    for h in range(2):
                        if lev:
                            pe.wait_ge(sem("level_added"), i * (2 * LEVELS) + (2 * lev + h - 1))
                        else:
                            pe.wait_ge(sem("t1_ready"), i * 2 + (h + 1))
                        for m in range(2):
                            mm = nc.tensor.matmul(ps[:, h, m * P:(m + 1) * P], Ml[:, 2 * h + m, :],
                                                  Tm[:, 2 * h + m, :], start=True, stop=True)
                        mm.then_inc(sem("y_made"), 1)
                    for h in range(2):
                        pe.wait_ge(sem("y_copied"), i * (2 * LEVELS) + (2 * lev + h + 1))
                        for m in range(2):
                            x, y = Xm[:, 2 * h + m, :], Ym[:, 2 * h + m, :]
                            if lev < LEVELS - 1:
                                nc.tensor.matmul(ps[:, 2 + h, m * P:(m + 1) * P], x, y, start=True, stop=True)
                            mm = nc.tensor.matmul(ps[:, 2 + h, S + m * P:S + (m + 1) * P], y, x, start=True, stop=True)
                        mm.then_inc(sem("level_made"), 1)
                    if ahead and lev == 2:
                        kk_sums(i + 1)
                for m in range(4):
                    h = slice(64 * (m % 2), 64 * (m % 2) + 64)
                    mm = nc.tensor.matmul(ps[:, 0, m * 64:(m + 1) * 64], Mm[:, m, 2, :], tokm[:, m // 2, 3, h],
                                          start=True, stop=True)
                mm.then_inc(sem("w0_made"), 1)
                pe.wait_ge(sem("level_added"), i * (2 * LEVELS) + 2 * LEVELS)
                for m in range(4):
                    h = slice(64 * (m % 2), 64 * (m % 2) + 64)
                    mm = nc.tensor.matmul(ps[h, 1, (m // 2) * P:(m // 2 + 1) * P], tokm[:, m // 2, 0, h], Xm[:, m, :],
                                          start=True, stop=True)
                mm.then_inc(sem("at_made"), 1)
                pe.wait_ge(sem("w0_ready"), i + 1)
                for m in range(4):
                    mm = nc.tensor.matmul(ps[:, 2, m * 64:(m + 1) * 64], Xm[:, m, :], Uu[:, m // 2, m % 2, :],
                                          start=True, stop=True)
                mm.then_inc(sem("w1_made"), 1)
                pe.wait_ge(sem("at_ready"), i + 1)
                for c in range(4):
                    t, rows = c // 2, slice(64 * (c % 2), 64 * (c % 2) + 64)
                    if c:
                        pe.wait_ge(sem("s_ready"), i * 3 + c)
                    nc.tensor.matmul(ps[:, 0, 0:P], AtT[:, t, :], snap[:, c, :], start=True, stop=True)\
                        .then_inc(sem("u_made"), 1)
                    pe.wait_ge(sem("u_ready"), i * 4 + (c + 1))
                    if c < 3:
                        nc.tensor.matmul(ps[:, 3, 0:P], tokm[rows, t, 1, :],
                                         Uu[rows, t, :, :].rearrange("p h n -> p (h n)"), start=True, stop=False)
                        nc.tensor.matmul(ps[:, 3, 0:P], tokm[rows, t, 2, :], tokm[rows, t, 3, :],
                                         start=False, stop=True).then_inc(sem("s_made"), 1)
                for t in range(TT):
                    for c in (2 * t, 2 * t + 1):
                        rows = slice(64 * (c % 2), 64 * (c % 2) + 64)
                        nc.tensor.matmul(ps[rows, 1, t * P:(t + 1) * P], ar[:, t, 1, rows], snap[:, c, :],
                                         start=True, stop=False, skip_group_check=True)
                    for hd in range(2):
                        h = slice(64 * hd, 64 * hd + 64)
                        o = ps[:, 1, t * P + 64 * hd:t * P + 64 * hd + 64]
                        nc.tensor.matmul(o, Mm[:, 2 * t + hd, 1, :], Uu[:, t, hd, :], start=False, stop=False,
                                         skip_group_check=True)
                        mm = nc.tensor.matmul(o, Mm[:, 2 * t + hd, 3, :], tokm[:, t, 3, h], start=False, stop=True,
                                              skip_group_check=True)
                mm.then_inc(sem("y_out_made"), 1)

            turn_features(0)
            low_rank(0)
            kk_sums(0)
            with pe.Fori(0, 7) as i:
                pair(i, True)
            pair(7, False)

        block = ctx.enter_context(nc.Block())

        @block.sync
        def _(sp):
            for j in range(4):
                sp.dma_start(resid[:, :, j * CC:(j + 1) * CC], a["x"][0].rearrange("(t p) n -> p t n", p=P)
                             [:, :, j * CC:(j + 1) * CC]).then_inc(sem(f"x_loaded_{j}"), 16)
            for phase, n, per in STREAMS:
                if n:
                    with sp.Fori(0, n) as i:
                        for k in range(per):
                            stream(sp, i, phase, k)
                else:
                    for k in range(per):
                        stream(sp, 0, phase, k)
            sp.wait_ge(sem("out_ready"), TT)
            sp.dma_start(out[0].rearrange("(t p) n -> p t n", p=P), y2[:]).then_inc(sem("out_stored"), 16)
            sp.wait_ge(sem("out_stored"), 16)

        @block.gpsimd
        def _(pool):
            rel, buck = sem("rel_loaded"), sem("bucket_loaded")
            pool.dma_start(ident[:], a["ident"]).then_inc(sem("ident_loaded"), 16)
            pool.wait_ge(sem("x_loaded_3"), 16)
            pool.dma_start(pick_rel[:], a["pick_rel"].rearrange("(k p) n -> p k n", p=P)).then_inc(rel, 16)
            pool.dma_start(tableT[:], a["rel_bias_table_2"]).then_inc(buck, 16)
            pool.dma_start(pick_b[:], a["pick_bucket"]).then_inc(buck, 16)
            pool.dma_start(future[:], a["future"]).then_inc(buck, 16)
            pool.wait_ge(sem("rel_row_ready"), 1)
            pool.dma_start(rel_dram, rel_row[:]).then_inc(sem("rel_row_stored"), 16)
            pool.wait_ge(sem("buck_row_ready"), 1)
            pool.dma_start(buck_dram, buck_row[:]).then_inc(sem("buck_row_stored"), 16)
            pool.wait_ge(sem("rel_row_stored"), 16)
            pool.dma_start(rel_rows, rel_dram.partition_broadcast(P)).then_inc(sem("rel_rows_stored"), 16)
            pool.wait_ge(sem("buck_row_stored"), 16)
            pool.dma_start(buck_rows, buck_dram.partition_broadcast(P)).then_inc(sem("buck_rows_stored"), 16)
            pool.wait_ge(sem("rel_rows_stored"), 16)
            pool.wait_ge(sem("buck_rows_stored"), 16)
            pool.wait_ge(block_used, B_DOWN + SPLIT_SLOTS)
            pool.dma_start(fin_gain[:], a["norm_final"].partition_broadcast(P)).then_inc(sem("fin_gain_loaded"), 16)
            nsa = sem("nsa_loaded")
            pool.wait_ge(block_used, B_CMP + SPLIT_SLOTS)
            pool.dma_start(bias2[:], shifted(buck_rows, 384)).then_inc(nsa, 16)
            with nc.allow_non_contiguous_dma("positions, transposed"):
                for j, name in enumerate(("cmp_pos_k_2", "cmp_pos_v_2")):
                    pool.dma_start(posT[:, j, :], a[name][0].rearrange("t d -> d t")).then_inc(nsa, 16)
            for j, name in enumerate(("cmp_k_w2_2", "cmp_v_w2_2")):
                pool.dma_start(cw2[:, j, :], a[name][0]).then_inc(nsa, 16)
            rw = sem("rwkv_loaded")
            pool.wait_ge(sem("nsa_out_ready"), HN)
            pool.dma_start(masks[:], a["masks"].rearrange("m p n -> p m n")).then_inc(rw, 16)
            pool.dma_start(l2[0:64, :], a["rwkv_w2_2"][0]).then_inc(rw, 16)
            pool.dma_start(l2[64:128, :], a["rwkv_a2_2"][0]).then_inc(rw, 16)
            def level(i, lev):
                if lev < 2:
                    pool.wait_ge(sem("m_masked"), i + 1)
                else:
                    pool.wait_ge(sem("level_made"), i * (2 * LEVELS) + 2 * (lev - 1))
                pool.tensor_tensor((Ml0, Ml1)[lev % 2][:], Mm[:, :, 0, :],
                                   masks[:, 5 + lev:6 + lev, :].broadcast_to([P, 4, P]), ALU.mult)\
                    .then_inc(sem("level_ready"), 1)

            pool.wait_ge(rw, 48)
            with pool.Fori(0, 8) as i:
                for lev in range(LEVELS):
                    level(i, lev)
            pool.wait_ge(sem("pair_done"), 8)
            pool.dma_start(lnw[:], a["rwkv_ln_w_2"][0].partition_broadcast(P)).then_inc(sem("ln_loaded"), 16)
            pool.dma_start(lnb[:], a["rwkv_ln_b_2"][0].partition_broadcast(P)).then_inc(sem("ln_loaded"), 16)
            pool.wait_ge(turned_lo, 4 * KT)
            pool.wait_ge(sem("mix_ready"), 1)
            pool.dma_start(post_gain[:], a["post_norm_g_2"][0].partition_broadcast(P))\
                .then_inc(sem("post_gain_loaded"), 16)

        @block.scalar
        def _(act):
            link = Chain(act, "act_chain")

            act.dma_start(mix_rows[:], a["norm_mix"][0].rearrange("(k p) -> k p", p=P)).then_inc(sem("norm_mix_loaded"), 16)
            row = 0
            for name in ("norm_ffn", "pre_norm_g_2", "pool_scale", "rwkv_w0_2", "rwkv_a0_2",
                         "rwkv_k_k_2", "rwkv_k_a_2", "rwkv_r_k_2", "rwkv_mu_2"):
                v = a[name][0]
                if len(v.shape) == 2:
                    v = v.rearrange("h n -> (h n)")
                rows = v.shape[0] // P
                act.dma_start(par_rows[row:row + rows, :], v.rearrange("(k p) -> k p", p=P))\
                    .then_inc(sem("params_loaded"), 16)
                row += rows
            act.dma_start(rel_in[:], a["rel_bias"][0]).then_inc(sem("rel_bias_loaded"), 16)
            act.wait_ge(sem("params_ready"), 1)
            turned_to_hi(act, 0, 0, range(8))
            split_hi(act, B_WIN, 0, 0, 0)
            turned_to_hi(act, 0, 0, range(8, KT))
            split_hi(act, B_WIN, 0, 0, 1)
            for j in range(4):
                act.wait_ge(sem(f"x_loaded_{j}"), 16)
            rms_act(act, resid, scaled, 0)
            act.wait_ge(sem("rinv_ready"), 1)
            act.wait_ge(sem("params_ready"), 2)

            def store(dst, bank, col):
                def f(i):
                    nc.scalar.activation(dst[:, 0, bass.ds(i * 2 * CC + col, CC)], ps[:, bank, :], ACT.Copy,
                                         scale=rinv[:, 0, 0:1]).then_inc(drained[0], 1)
                return f

            def gates(bank, col):
                def f(i):
                    for tok in range(TT):
                        nc.scalar.activation(gate[:, tok, bass.ds(i * 2 * CC + (col - 4096), CC)],
                                             ps[:, bank + tok, :], ACT.Sigmoid, scale=rinv[:, 0, tok:tok + 1])\
                            .then_inc(drained[tok], 1)
                return f

            with act.Fori(0, 4) as i:
                product_steps(act, split_hi, B_WIN, 8, i, {3: store(qkvu, 0, 0), 7: store(qkvu, 2, CC)})
            act.wait_ge(sem("rel_row_stored"), 16)
            act.wait_ge(sem("buck_row_stored"), 16)
            for tok in range(TT):
                act.wait_ge(drained[tok], 2 + 8)
            act.wait_ge(sem("square_sums"), TT)
            act.wait_ge(sem("rel_rows_stored"), 16)

            def stage_k(n):
                nc.scalar.copy(kst[:], qkvu[:, :, bass.ds(n * P + 1024, P)]).then_inc(sem("k_staged"), 1)

            def begin(c):
                def f(i):
                    n = i * 2 + (c - 8)
                    act.wait_ge(sem("relb_used"), n + 1)
                    act.dma_start(relb[:], shifted(rel_rows, 256)[:, bass.ds(n * 2, 2), :])\
                        .then_inc(sem("relb_loaded"), 16)
                    if c == 0:
                        g = i - 4
                        act.wait_ge(sem("pool_mixed"), g + 1)
                        act.dma_start(rowp[:], a["pool_rows"][bass.ds(g, 1)]
                                      .rearrange("a (k p) n -> p (a k) n", p=P)).then_inc(sem("pool_loaded"), 16)
                        act.dma_start(pwg[:], a["pool_w"][0][bass.ds(g, 1)]
                                      .rearrange("a (k p) n -> p (a k) n", p=P)).then_inc(sem("pool_loaded"), 16)
                    act.wait_ge(sem("qk_turned"), n + 1)
                    nc.scalar.copy(qkT[:].rearrange("p x n -> p (x n)"), ps[:, T0, :]).then_inc(sem("qkT_ready"), 1)
                    nc.scalar.copy(vst[:], qkvu[:, :, bass.ds(n * P + 2048, P)]).then_inc(sem("v_staged"), 1)
                    if c == 0:
                        nc.scalar.copy(ust[:], qkvu[:, :, bass.ds(i * S + (3072 - 4 * S), S)])\
                            .then_inc(sem("u_staged"), 1)
                return f

            def exps(c, last):
                def f(i):
                    n = i * 2 + (c - 8)
                    if not last:
                        stage_k(n + 1)
                    act.wait_ge(sem("att_max"), n + 1)
                    for hd in range(2):
                        for qt in range(TT):
                            seg = prob[:, hd, 0:P] if qt == 0 else prob[:, hd, P:384]
                            e = 2 * qt + hd
                            nc.scalar.activation(seg, seg, ACT.Exp, bias=smax[:, e:e + 1],
                                                 accum_out=ssum[:, e:e + 1]).then_inc(sem("att_exp"), 1)
                return f

            def pooled(i):
                act.wait_ge(sem("pool_mixed"), i - 2)
                for e in range(2):
                    nc.scalar.activation(qkvu[:, e, bass.ds(i * S + (3072 - 4 * S), S)], ps[:, T0, e * S:(e + 1) * S],
                                         ACT.Copy, scale=pool_scale[:, bass.ds(i * 2 + (e - 8), 1)])\
                        .then_inc(sem("pool_stored"), 1)

            def probs_back(c):
                def f(i):
                    act.wait_ge(sem("probs_turned"), i * 2 + (c - 7))
                    nc.scalar.copy(probT[:, 0, :], ps[:, T2, 0:384]).then_inc(sem("pT_ready_0"), 1)
                return f

            def finish(c, bank):
                def f(i):
                    gates(bank, c * CC)(i)
                    act.wait_ge(sem("pv_done"), i * 2 + (c - 7))
                    nc.scalar.copy(qkvu[:, :, bass.ds(i * S + (c * P - 8 * P), P)],
                                   ps[:, T1, 0:S].rearrange("p (t n) -> p t n", t=TT)).then_inc(sem("att_stored"), 1)
                return f

            def with_attention(i, last):
                product_steps(act, split_hi, B_WIN, 8, i, {3: finish(0, 0), 7: finish(1, 2)},
                              {0: [begin(0)], 1: [exps(0, False)], 3: [probs_back(0)],
                               4: [begin(1)], 5: [exps(1, last)], 6: [pooled], 7: [probs_back(1)]})

            stage_k(0)
            with act.Fori(4, 7) as i:
                with_attention(i, False)
            with_attention(7, True)

            act.wait_ge(block_used, B_MERGE + SPLIT_SLOTS)
            act.wait_ge(sem("att_stored"), 9)
            act.wait_ge(sem("pool_stored"), 10)
            for j in range(4):
                dst, src = branch_inputs(xT_hi, j)
                nc.scalar.copy(dst, src).then_inc(sem("inputs_hi"), 1)

            def merged_hi(i, back):
                for j in range(4):
                    act.wait_ge(sem("merged_turned"), i * 4 + (j + 1 - 4 * back))
                    nc.scalar.copy(mT_hi[:, bass.ds(i * 4 + (j - 4 * back), 1), :].rearrange("p a n -> p (a n)")
                                   if not isinstance(i, int) else mT_hi[:, 4 * (i - back) + j, :],
                                   ps[:, T0 + j, 0:S]).then_inc(sem("merged_hi"), 1)

            product_steps(act, split_hi, B_MERGE, 4, 0, {})
            with act.Fori(1, 4) as i:
                product_steps(act, split_hi, B_MERGE, 4, i, {1: lambda i: merged_hi(i, 1)})
            merged_hi(4, 1)

            def turned_back(i):
                turned_to_hi(act, KT, 1, range(4 * i - 4, 4 * i))

            for c in range(4):
                product_steps(act, split_hi, B_WOUT, 4, c, {}, {3: [turned_back]} if c else {})

            turned_back(4)
            for tok in range(TT):
                act.wait_ge(drained[tok], 2 + Q_GU)
            rms_act(act, resid, scaled, 1)
            act.wait_ge(sem("rinv_ready"), 2)

            def sig(i):
                for tok in range(TT):
                    nc.scalar.activation(g_act[:, tok, :], ps[:, tok, :], ACT.Sigmoid, scale=rinv[:, 1, tok:tok + 1])\
                        .then_inc(sem("sig_ready"), 1)

            def hidden_back(i, back=1):
                act.wait_ge(sem("hidden_turned"), i + (1 - back))
                for j in range(2):
                    if isinstance(i, int):
                        dst = actT[:, 4 * (i - back) + 2 * j:4 * (i - back) + 2 * j + 2, :]
                    else:
                        dst = actT[:, bass.ds(i * 4 + (2 * j - 4 * back), 2), :]
                    nc.scalar.copy(dst, ps[:, T0 + j, :].rearrange("p (k n) -> p k n", k=2))\
                        .then_inc(sem("hidden_ready"), 1)

            product_steps(act, split_hi, B_GU, 8, 0, {3: sig})
            with act.Fori(1, 11) as i:
                product_steps(act, split_hi, B_GU, 8, i, {3: lambda i: (hidden_back(i), sig(i))})
            hidden_back(11)

            def stage_hi(i, k):
                if isinstance(i, int):
                    src = actT[:, 4 * i + k, :]
                else:
                    src = actT[:, bass.ds(i * 4 + k, 1), :].rearrange("p a n -> p (a n)")
                nc.scalar.copy(aT_hi[:, k % 2, :], src).then_inc(sem("hidden_hi"), 1)

            act.wait_ge(sem("hidden_ready"), 22)
            stage_hi(0, 0)
            stage_hi(0, 1)
            with act.Fori(0, 10) as i:
                for k in range(4):
                    split_hi(act, B_DOWN, 4, i, k + 2)
                    stage_hi(i, k + 2)
            for k in range(4):
                split_hi(act, B_DOWN, 4, 10, k + 2)
                if k < 2:
                    stage_hi(10, k + 2)

            for tok in range(TT):
                act.wait_ge(drained[tok], 2 + Q_WIN2)
            act.wait_ge(sem("down_added"), 4)
            rms_act(act, resid, scaled, 2)
            turned_to_hi(act, 2 * KT, 2)
            act.wait_ge(sem("final_normed"), 4)
            rms_act(act, resid, scaled, 3)
            act.wait_ge(sem("rinv_ready"), 4)

            def store2(bank, col, width=CC):
                def f(i):
                    dst = z2[:, 0, col:col + width] if isinstance(i, int) else \
                        z2[:, 0, bass.ds(i * 2 * CC + col, width)]
                    nc.scalar.activation(dst, ps[:, bank, 0:width], ACT.Copy, scale=rinv[:, 1, 0:1])\
                        .then_inc(drained[0], 1)
                return f

            with act.Fori(0, 7) as i:
                product_steps(act, split_hi, B_WIN2, 8, i, {3: store2(0, 0), 7: store2(2, CC)})
            product_steps(act, split_hi, B_WIN2 + 56, 8, 0,
                          {3: store2(0, 14 * CC), 7: store2(2, 15 * CC, N2 - 15 * CC)})

            for j in range(2):
                act.wait_ge(sem("keys_turned"), j + 1)
                nc.scalar.copy(KTs[:, j, :, :], ps[:, T0 + j, :].rearrange("p (g n) -> p g n", g=2))\
                    .then_inc(sem("keysT_ready"), 1)
            act.wait_ge(drained[0], 2 + 68 - 0)
            act.wait_ge(drained[1], 2 + 68 - 0)
            nc.scalar.activation(gsig[:, :, 0:16], z2[:, :, C_GATE + 8:C_GATE + 24], ACT.Exp, scale=-1.0)\
                .then_inc(sem("gate_exp"), 1)
            nc.scalar.activation(gsig[:, :, 16:24], z2[:, :, C_GATE:C_GATE + 8], ACT.Exp, scale=-1.0)\
                .then_inc(sem("gate_exp"), 1)
            for k in range(4):
                split_hi(act, B_CMP, 4, 0, k + 2)
            chunk_done(act, B_CMP, 4, 0, 3)
            nc.scalar.activation(hexp[:, :, 0:30], ps[:, 0:2, 0:30], ACT.Exp, scale=-1.0)\
                .then_inc(sem("hid_exp"), 1)
            act.wait_ge(sem("compressed"), 1)
            nc.scalar.copy(kcT[:, 0:30], ps[:, 2, 0:30]).then_inc(sem("kcT_ready"), 1)

            with act.Fori(0, 2) as g:
                for hh in range(4):
                    n = g * 4 + hh
                    act.wait_ge(sem("q2_turned"), n + 1)
                    nc.scalar.copy(q2T[:], ps[:, T0, 0:S]).then_inc(sem("q2T_ready"), 1)
                    act.wait_ge(sem("nsa_max"), n + 1)
                    for b in range(3):
                        for qt in range(TT):
                            if b == 2:
                                seg = prc[:, qt, 0:NCMP]
                            else:
                                seg = pr[:, b, 0:P] if qt == 0 else pr[:, b, P:384]
                            nc.scalar.activation(seg, seg, ACT.Exp, bias=mx2[:, b, qt:qt + 1],
                                                 accum_out=sm2[:, b, qt:qt + 1]).then_inc(sem("nsa_exp"), 1)
                    act.wait_ge(sem("probs2_turned"), n + 1)
                    nc.scalar.copy(pT2[:, 0, :], ps[:, T1, 0:384]).then_inc(sem("pT2_ready_0"), 1)
                    nc.scalar.copy(pcT[0:NCMP, :], ps[0:NCMP, T3, 0:S]).then_inc(sem("pT2_ready_0"), 1)
                    act.wait_ge(sem("pv2_done"), n + 1)
                    nc.scalar.copy(oy[:, :, bass.ds(n * P, P)],
                                   ps[:, 3, 0:S].rearrange("p (t n) -> p t n", t=TT))\
                        .then_inc(sem("nsa_out_ready"), 1)

            rwkv_act(act, link)

            act.wait_ge(sem("rwkv_done"), 1)
            for c in (C_ZA, C_ZB):
                nc.scalar.activation(ysc[:, :, 0:1024] if c == C_ZA else ysc[:, :, 1024:D],
                                     z2[:, :, c:c + 1024], ACT.Sigmoid).then_inc(sem("z_sig"), 1)
            turned_to_hi(act, 3 * KT, None)

            def store3(bank, col):
                def f(i):
                    nc.scalar.copy(y2[:, 0, bass.ds(i * 2 * CC + col, CC)], ps[:, bank, :])\
                        .then_inc(drained[0], 1)
                return f

            with act.Fori(0, 1) as i:
                product_steps(act, split_hi, B_WOUT2, 8, i, {3: store3(0, 0), 7: store3(2, CC)})
            for k in range(8):
                if k < 6:
                    split_hi(act, B_WOUT2 + 8, 8, 0, k + 2)
                if k % 4 == 3:
                    chunk_done(act, B_WOUT2 + 8, 8, 0, k)
                    nc.scalar.copy(y2[:, 0, (2 + k // 4) * CC:(3 + k // 4) * CC], ps[:, 2 * (k // 4), :])\
                        .then_inc(drained[0], 1)
            act.wait_ge(drained[1], 2 + 72)
            act.wait_ge(drained[0], 2 + 72)
            rms_act(act, y2, ysc, 4)

        @block.vector
        def _(dve):
            link = Chain(dve, "dve_chain")
            dve.sem_inc(block_split, RAW_SLOTS)
            dve.sem_inc(block_used, SPLIT_SLOTS)
            dve.sem_inc(drained[0], 2)
            dve.sem_inc(drained[1], 2)
            dve.sem_inc(sem("relb_used"), 1)
            dve.sem_inc(sem("pool_mixed"), 1)
            dve.sem_inc(sem("pool_stored"), 2)
            dve.sem_inc(sem("att_stored"), 1)

            dve.wait_ge(sem("params_turned"), 1)
            nc.vector.tensor_copy(per_feature[:, 0:KT], ps[:, 0, 0:KT]).then_inc(sem("params_ready"), 1)
            dve.wait_ge(sem("params_ready"), 1)
            turned_to_lo(dve, 0, 0, range(8))
            split_lo(dve, B_WIN, 0, 0, 0)
            turned_to_lo(dve, 0, 0, range(8, KT))
            split_lo(dve, B_WIN, 0, 0, 1)
            dve.wait_ge(sem("params_turned"), 2)
            nc.vector.tensor_copy(per_feature[:, KT:121], ps[:, 1, 0:121 - KT]).then_inc(sem("params_ready"), 1)
            dve.wait_ge(sem("params_ready"), 2)
            dve.wait_ge(sem("rel_turned"), 1)
            nc.vector.tensor_copy(relT[:, 0:2, :], ps[:, 2, 0:32].rearrange("p (k n) -> p k n", k=2))\
                .then_inc(sem("relT_ready"), 1)
            nc.vector.tensor_copy(relT[0:1, 2, :], ps[0:1, 2, 32:48]).then_inc(sem("relT_ready"), 1)
            dve.wait_ge(sem("rows_made"), 1)
            nc.vector.tensor_copy(rel_row[:], ps[0:16, T0, 0:384]).then_inc(sem("rel_row_ready"), 1)
            dve.wait_ge(sem("bucket_loaded"), 48)
            nc.vector.tensor_tensor(buck_row[:], ps[0:HN, T1, :], future[:], ALU.add).then_inc(sem("buck_row_ready"), 1)
            rms_dve(dve, link, 0)

            def store(bank, col):
                def f(i):
                    nc.vector.tensor_scalar(qkvu[:, 1, bass.ds(i * 2 * CC + col, CC)], ps[:, bank + 1, :],
                                            rinv[:, 0, 1:2], None, ALU.mult).then_inc(drained[1], 1)
                return f

            with dve.Fori(0, 4) as i:
                product_steps(dve, split_lo, B_WIN, 8, i, {3: store(0, 0), 7: store(2, CC)})
            for tok in range(TT):
                dve.wait_ge(drained[tok], 2 + 8)

            def stage_q(n):
                nc.vector.tensor_scalar(qst[:], qkvu[:, :, bass.ds(n * P, P)], 0.125, None, ALU.mult)\
                    .then_inc(sem("q_staged"), 1)

            def softmax(c, last):
                def f(i):
                    n = i * 2 + (c - 8)
                    dve.wait_ge(sem("scores_ready"), n + 1)
                    dve.wait_ge(sem("relb_loaded"), i * 32 + 16 * (c - 7))
                    link(nc.vector.memset(relb[0:64, :, 192:256], NEG))
                    link(nc.vector.tensor_tensor(prob[:, :, 0:P], ps[:, T2:T2 + 2, 0:P], relb[:, :, P:256], ALU.add))
                    nc.vector.tensor_tensor(prob[:, :, P:384], ps[:, T2:T2 + 2, P:384], relb[:], ALU.add)\
                        .then_inc(sem("relb_used"), 1)
                    dve.wait_ge(sem("relb_used"), n + 2)
                    link(nc.vector.tensor_reduce(smax[:, 0:2], prob[:, :, 0:P], AX, ALU.max))
                    link(nc.vector.tensor_reduce(smax[:, 2:4], prob[:, :, P:384], AX, ALU.max))
                    nc.vector.tensor_scalar(smax[:], smax[:], -1.0, None, ALU.mult).then_inc(sem("att_max"), 1)
                    if not last:
                        stage_q(n + 1)
                    dve.wait_ge(sem("att_exp"), i * 8 + 4 * (c - 7))
                    link(nc.vector.reciprocal(ssum[:], ssum[:]))
                    for hd in range(2):
                        for qt in range(TT):
                            seg = prob[:, hd, 0:P] if qt == 0 else prob[:, hd, P:384]
                            e = 2 * qt + hd
                            nc.vector.tensor_scalar(seg, seg, ssum[:, e:e + 1], None, ALU.mult)\
                                .then_inc(sem("probs_ready"), 1)
                return f

            def pool_means(i):
                dve.wait_ge(sem("pool_mean"), i - 3)
                nc.vector.tensor_copy(dT[:].rearrange("p x n -> p (x n)"), ps[:, T0, :]).then_inc(sem("dT_ready"), 1)

            def probs_back(c):
                def f(i):
                    dve.wait_ge(sem("probs_turned"), i * 2 + (c - 7))
                    nc.vector.tensor_copy(probT[:, 1, :], ps[:, T3, 0:384]).then_inc(sem("pT_ready_1"), 1)
                return f

            def with_attention(i, last):
                product_steps(dve, split_lo, B_WIN, 8, i, {},
                              {1: [softmax(0, False)], 2: [pool_means], 3: [probs_back(0)],
                               5: [softmax(1, last)], 7: [probs_back(1)]})

            stage_q(0)
            with link.loop(4, 7, 10) as i:
                with_attention(i, False)
            with_attention(7, True)

            for j in range(4):
                dve.wait_ge(sem("inputs_hi"), j + 1)
                dst, src = branch_inputs(xT_lo, j)
                hi, _ = branch_inputs(xT_hi, j)
                nc.vector.tensor_tensor(dst, src, hi.bitcast(F32), ALU.subtract).then_inc(sem("inputs_lo"), 1)

            def branch(i, which):
                buf = g_act if which == 0 else h_act
                if which == 0 and not isinstance(i, int):
                    dve.wait_ge(sem("merged_ready"), i)
                for tok in range(TT):
                    col = i * CC + which * D
                    src = gate[:, tok, col:col + CC] if isinstance(i, int) else gate[:, tok, bass.ds(col, CC)]
                    nc.vector.tensor_tensor(buf[:, tok, :], ps[:, 2 * which + tok, :], src, ALU.mult)\
                        .then_inc(drained[tok], 1)
                if which == 1:
                    for tok in range(TT):
                        dve.wait_ge(drained[tok], i * 2 + (Q_MERGE + 2 + 2))
                    nc.vector.tensor_tensor(m_tmp[:], g_act[:], h_act[:], ALU.add)\
                        .then_inc(sem("merged_ready"), 1)

            def merged_lo(i):
                for j in range(4):
                    dve.wait_ge(sem("merged_hi"), i * 4 + (j + 1 - 4))
                    if isinstance(i, int):
                        lo, hi = mT_lo[:, 4 * (i - 1) + j, :], mT_hi[:, 4 * (i - 1) + j, :]
                    else:
                        kt = bass.ds(i * 4 + (j - 4), 1)
                        lo, hi = (m[:, kt, :].rearrange("p a n -> p (a n)") for m in (mT_lo, mT_hi))
                    nc.vector.tensor_tensor(lo, ps[:, T0 + j, 0:S], hi.bitcast(F32), ALU.subtract)\
                        .then_inc(sem("merged_lo"), 1)

            product_steps(dve, split_lo, B_MERGE, 4, 0,
                          {1: lambda i: branch(i, 0), 3: lambda i: branch(i, 1)})
            with dve.Fori(1, 4) as i:
                product_steps(dve, split_lo, B_MERGE, 4, i,
                              {1: lambda i: (branch(i, 0), merged_lo(i)), 3: lambda i: branch(i, 1)})
            merged_lo(4)

            def add(i):
                for tok in range(TT):
                    x = resid[:, tok, i * CC:(i + 1) * CC]
                    nc.vector.tensor_tensor(x, x, ps[:, 2 * (i % 2) + tok, :], ALU.add).then_inc(drained[tok], 1)

            def turned_back(i):
                turned_to_lo(dve, KT, 1, range(4 * i - 4, 4 * i))

            for c in range(4):
                product_steps(dve, split_lo, B_WOUT, 4, c, {3: add}, {3: [turned_back]} if c else {})

            turned_back(4)
            rms_dve(dve, link, 1)

            def gated(i):
                for tok in range(TT):
                    dve.wait_ge(sem("sig_ready"), i * 2 + (tok + 1))
                    nc.vector.scalar_tensor_tensor(g_act[:, tok, :], ps[:, tok, :], rinv[:, 1, tok:tok + 1],
                                                   g_act[:, tok, :], ALU.mult, ALU.mult)\
                        .then_inc(drained[tok], 1)

            def hidden(i):
                for tok in range(TT):
                    dve.wait_ge(drained[tok], i * 2 + (Q_GU + 2 + 1))
                    nc.vector.scalar_tensor_tensor(h_act[:, tok, :], ps[:, 2 + tok, :], rinv[:, 1, tok:tok + 1],
                                                   g_act[:, tok, :], ALU.mult, ALU.mult)\
                        .then_inc(drained[tok], 1)

            with dve.Fori(0, 11) as i:
                product_steps(dve, split_lo, B_GU, 8, i, {3: gated, 7: hidden})

            def stage_lo(i, k):
                dve.wait_ge(sem("hidden_hi"), i * 4 + (k + 1))
                if isinstance(i, int):
                    src = actT[:, 4 * i + k, :]
                else:
                    src = actT[:, bass.ds(i * 4 + k, 1), :].rearrange("p a n -> p (a n)")
                nc.vector.tensor_tensor(aT_lo[:, k % 2, :], src, aT_hi[:, k % 2, :].bitcast(F32), ALU.subtract)\
                    .then_inc(sem("hidden_staged"), 1)

            stage_lo(0, 0)
            stage_lo(0, 1)
            with dve.Fori(0, 10) as i:
                for k in range(4):
                    split_lo(dve, B_DOWN, 4, i, k + 2)
                    stage_lo(i, k + 2)
            for k in range(4):
                split_lo(dve, B_DOWN, 4, 10, k + 2)
                if k < 2:
                    stage_lo(10, k + 2)
            chunk_done(dve, B_DOWN, 4, 10, 3)
            for n in range(4):
                for tok in range(TT):
                    x = resid[:, tok, n * CC:(n + 1) * CC]
                    ins = nc.vector.tensor_tensor(x, x, ps[:, 2 * n + tok, :], ALU.add)
                    ins.then_inc(drained[tok] if n < 2 else sem("down_added"), 1)
            dve.wait_ge(sem("down_added"), 4)

            rms_dve(dve, link, 2)
            dve.wait_ge(sem("fin_gain_loaded"), 16)
            for half in (slice(0, 1024), slice(1024, D)):
                for tok in range(TT):
                    x = resid[:, tok, half]
                    nc.vector.scalar_tensor_tensor(x, x, rinv[:, 0, tok:tok + 1], fin_gain[:, half], ALU.mult,
                                                   ALU.mult).then_inc(sem("final_normed"), 1)
            turned_to_lo(dve, 2 * KT, 2)
            rms_dve(dve, link, 3)

            def store2(bank, col, width=CC):
                def f(i):
                    dst = z2[:, 1, col:col + width] if isinstance(i, int) else \
                        z2[:, 1, bass.ds(i * 2 * CC + col, width)]
                    nc.vector.tensor_scalar(dst, ps[:, bank + 1, 0:width], rinv[:, 1, 1:2], None, ALU.mult)\
                        .then_inc(drained[1], 1)
                return f

            with dve.Fori(0, 7) as i:
                product_steps(dve, split_lo, B_WIN2, 8, i, {3: store2(0, 0), 7: store2(2, CC)})
            product_steps(dve, split_lo, B_WIN2 + 56, 8, 0,
                          {3: store2(0, 14 * CC), 7: store2(2, 15 * CC, N2 - 15 * CC)})

            for j in range(2):
                dve.wait_ge(sem("keys_turned"), j + 3)
                link(nc.vector.tensor_copy(kvcT[:, j, :, :], ps[:, T2 + j, :].rearrange("p (g n) -> p g n", g=2)))
            dve.wait_ge(sem("nsa_loaded"), 80)
            for kv, (hi, lo) in enumerate(((A_hi, A_lo), (A_hi2, A_lo2))):
                for g in range(2):
                    pos = posT[:, kv, :].unsqueeze(2).broadcast_to([P, 32, NCMP])
                    link(nc.vector.tensor_tensor(blkA[:, :, g * NCMP:(g + 1) * NCMP], windows(kv, g), pos, ALU.add))
                link(nc.vector.tensor_copy(hi[:], blkA[:]))
                link(nc.vector.tensor_tensor(lo[:], blkA[:], hi[:].bitcast(F32), ALU.subtract))
            dve.sem_inc(sem("windows_ready"), 1)
            for qt in range(TT):
                c = 159 - P * qt
                link(nc.vector.tensor_copy(biasc[:, :, qt, 0:NCMP], bias2[:, :, c:c + 16 * NCMP - 15:16]))
            dve.wait_ge(sem("gate_exp"), 2)
            link(nc.vector.tensor_scalar(gsig[:], gsig[:], 1.0, None, ALU.add))
            link(nc.vector.reciprocal(gsig[:], gsig[:]))
            for k in range(4):
                split_lo(dve, B_CMP, 4, 0, k + 2)
            dve.wait_ge(sem("hid_exp"), 1)
            link(nc.vector.tensor_scalar(hexp[:, :, 0:30], hexp[:, :, 0:30], 1.0, None, ALU.add))
            link(nc.vector.reciprocal(hexp[:, :, 0:30], hexp[:, :, 0:30]))
            nc.vector.tensor_tensor(hid[:, :, 0:30], ps[:, 0:2, 0:30], hexp[:, :, 0:30], ALU.mult)\
                .then_inc(sem("hid_ready"), 1)
            dve.wait_ge(sem("compressed"), 1)
            link(nc.vector.tensor_copy(vc[0:NCMP, :, :], ps[0:NCMP, 3, 0:256].rearrange("p (g n) -> p g n", g=2)))
            dve.sem_inc(sem("vc_ready"), 1)

            with link.loop(0, 2, 4 * 9) as g:
                for hh in range(4):
                    n = g * 4 + hh
                    nc.vector.tensor_scalar(q2[:], z2[:, :, bass.ds(n * P, P)], float(P) ** -0.5, None, ALU.mult)\
                        .then_inc(sem("q2_staged"), 1)
                    dve.wait_ge(sem("scores2_ready"), n + 1)
                    hb = bias2[:, bass.ds(n, 1), :]
                    for b in range(2):
                        link(nc.vector.tensor_tensor(pr[:, b, 0:P], ps[:, b, 0:P],
                                                     hb[:, :, P:256].rearrange("p a n -> p (a n)"), ALU.add))
                        link(nc.vector.tensor_tensor(pr[:, b, P:384], ps[:, b, P:384],
                                                     hb[:, :, 0:256].rearrange("p a n -> p (a n)"), ALU.add))
                    nc.vector.tensor_tensor(
                        prc[:, :, 0:NCMP], ps[:, 2, 0:32].rearrange("p (t n) -> p t n", t=TT)[:, :, 0:NCMP],
                        biasc[:, bass.ds(n, 1), :, 0:NCMP].rearrange("p a t n -> p (a t) n"), ALU.add)\
                        .then_inc(sem("prc_biased"), 1)
                    dve.wait_ge(sem("prc_biased"), n + 1)
                    link(nc.vector.tensor_reduce(mx2[:, 0:2, 0], pr[:, :, 0:P], AX, ALU.max))
                    link(nc.vector.tensor_reduce(mx2[:, 0:2, 1], pr[:, :, P:384], AX, ALU.max))
                    link(nc.vector.tensor_reduce(mx2[:, 2, :], prc[:, :, 0:NCMP], AX, ALU.max))
                    nc.vector.tensor_scalar(mx2[:], mx2[:], 0.9 * NEG, -1.0, ALU.max, ALU.mult)\
                        .then_inc(sem("nsa_max"), 1)
                    dve.wait_ge(sem("nsa_exp"), n * 6 + 6)
                    nc.vector.tensor_scalar(sm2[:], sm2[:], 1e-30, None, ALU.max).then_inc(sem("sums_kept"), 1)
                    dve.wait_ge(sem("sums_kept"), n + 1)
                    link(nc.vector.reciprocal(sm2[:], sm2[:]))
                    gs = gsig[:].rearrange("p t (b h) -> p b t h", b=3)[:, :, :, bass.ds(n, 1)]
                    link(nc.vector.tensor_tensor(sm2[:], sm2[:], gs.rearrange("p b t a -> p b (t a)"), ALU.mult))
                    for b in range(3):
                        for qt in range(TT):
                            if b == 2:
                                seg = prc[:, qt, 0:NCMP]
                            else:
                                seg = pr[:, b, 0:P] if qt == 0 else pr[:, b, P:384]
                            nc.vector.tensor_scalar(seg, seg, sm2[:, b, qt:qt + 1], None, ALU.mult)\
                                .then_inc(sem("probs2_ready"), 1)
                    dve.wait_ge(sem("probs2_turned"), n + 1)
                    nc.vector.tensor_copy(pT2[:, 1, :], ps[:, T2, 0:384]).then_inc(sem("pT2_ready_1"), 1)

            rwkv_dve(dve, link)

            for j, c in enumerate((C_ZA, C_ZB)):
                dve.wait_ge(sem("z_sig"), j + 1)
                part = slice(1024 * j, 1024 * j + 1024)
                link(nc.vector.tensor_tensor(ysc[:, :, part], ysc[:, :, part], z2[:, :, c:c + 1024], ALU.mult))
                link(nc.vector.tensor_tensor(oy[:, :, part], oy[:, :, part], ysc[:, :, part], ALU.mult))
            dve.sem_inc(sem("mix_ready"), 1)
            turned_to_lo(dve, 3 * KT, None)

            def store3(bank, col):
                def f(i):
                    nc.vector.tensor_copy(y2[:, 1, bass.ds(i * 2 * CC + col, CC)], ps[:, bank + 1, :])\
                        .then_inc(drained[1], 1)
                return f

            with dve.Fori(0, 1) as i:
                product_steps(dve, split_lo, B_WOUT2, 8, i, {3: store3(0, 0), 7: store3(2, CC)})
            for k in range(8):
                if k < 6:
                    split_lo(dve, B_WOUT2 + 8, 8, 0, k + 2)
                if k % 4 == 3:
                    chunk_done(dve, B_WOUT2 + 8, 8, 0, k)
                    nc.vector.tensor_copy(y2[:, 1, (2 + k // 4) * CC:(3 + k // 4) * CC], ps[:, 2 * (k // 4) + 1, :])\
                        .then_inc(drained[1], 1)
            rms_dve(dve, link, 4)
            dve.wait_ge(sem("post_gain_loaded"), 16)
            for tok in range(TT):
                link(nc.vector.scalar_tensor_tensor(y2[:, tok, :], y2[:, tok, :], rinv[:, 0, tok:tok + 1],
                                                    post_gain[:], ALU.mult, ALU.mult))
                nc.vector.tensor_tensor(y2[:, tok, :], y2[:, tok, :], resid[:, tok, :], ALU.add)\
                    .then_inc(sem("out_ready"), 1)

        @block.tensor
        def _(pe):
            pe.wait_ge(sem("ident_loaded"), 16)
            pe.wait_ge(sem("norm_mix_loaded"), 16)
            nc.tensor.transpose(ps[:, 0, 0:KT], mix_rows[:], ident[0:KT, 0:KT]).then_inc(sem("params_turned"), 1)
            for j in range(4):
                pe.wait_ge(sem(f"x_loaded_{j}"), 16)
                turn_rows(pe, resid, 0, range(4 * j, 4 * j + 4))
            pe.wait_ge(sem("params_loaded"), 144)
            n = 121 - KT
            nc.tensor.transpose(ps[:, 1, 0:n], par_rows[:], ident[0:n, 0:n]).then_inc(sem("params_turned"), 1)
            pe.wait_ge(sem("rel_bias_loaded"), 16)
            for j in range(3):
                n = min(P, 2 * REL + 1 - j * P)
                tr = nc.tensor.transpose(ps[0:n, 2, 16 * j:16 * j + 16], rel_in[:, j * P:j * P + n], ident[0:16, 0:16])
            tr.then_inc(sem("rel_turned"), 1)
            pe.wait_ge(sem("rel_loaded"), 16)
            pe.wait_ge(sem("relT_ready"), 2)
            pe.wait_ge(turned_lo, KT)
            for j in range(3):
                n = min(P, 2 * REL + 1 - j * P)
                nc.tensor.matmul(ps[0:16, T0, 0:384], relT[0:n, j, :], pick_rel[0:n, j, :], start=j == 0, stop=j == 2)
            pe.wait_ge(sem("bucket_loaded"), 48)
            nc.tensor.matmul(ps[0:HN, T1, :], tableT[:], pick_b[:], start=True, stop=True).then_inc(sem("rows_made"), 1)

            pe.wait_ge(sem("relT_ready"), 2)
            plain_product(pe, B_WIN, Q_WIN, 4, xT_hi, xT_lo)

            def turn_qk(i, c):
                n = i * 2 + (c - 8)
                pe.wait_ge(sem("q_staged"), n + 1)
                pe.wait_ge(sem("k_staged"), n + 1)
                if c == 0:
                    pe.wait_ge(sem("pool_stored"), i * 2 - 6)
                else:
                    pe.wait_ge(sem("dT_ready"), i - 3)
                for x, src in enumerate((qst, kst)):
                    for tok in range(TT):
                        o = x * S + tok * P
                        tr = nc.tensor.transpose(ps[:, T0, o:o + P], src[:, tok, :], ident[:])
                tr.then_inc(sem("qk_turned"), 1)

            def scores(i, c):
                pe.wait_ge(sem("qkT_ready"), i * 2 + (c - 7))
                for hd in range(2):
                    h = slice(64 * hd, 64 * hd + 64)
                    nc.tensor.matmul(ps[:, T2 + hd, 0:P], qkT[h, 0, 0:P], qkT[h, 1, 0:P], start=True, stop=True)
                    mm = nc.tensor.matmul(ps[:, T2 + hd, P:384], qkT[h, 0, P:S], qkT[h, 1, :], start=True, stop=True)
                mm.then_inc(sem("scores_ready"), 1)

            def turn_probs(i, c):
                pe.wait_ge(sem("probs_ready"), i * 8 + 4 * (c - 7))
                for hd in range(2):
                    for j in range(3):
                        tr = nc.tensor.transpose(ps[:, T2 + hd, j * P:(j + 1) * P],
                                                 prob[:, hd, j * P:(j + 1) * P], ident[:])
                tr.then_inc(sem("probs_turned"), 1)

            def values(i, c):
                n = i * 2 + (c - 8)
                pe.wait_ge(sem("pT_ready_0"), n + 1)
                pe.wait_ge(sem("pT_ready_1"), n + 1)
                pe.wait_ge(sem("v_staged"), n + 1)
                pe.wait_ge(sem("att_stored"), n + 1)
                for hd in range(2):
                    h = slice(64 * hd, 64 * hd + 64)
                    nc.tensor.matmul(ps[h, T1, 0:S], vst[:, 0, h], probT[:, hd, 0:S], start=True, stop=False)
                    mm = nc.tensor.matmul(ps[h, T1, P:S], vst[:, 1, h], probT[:, hd, S:384], start=False, stop=True)
                mm.then_inc(sem("pv_done"), 1)

            def pool_mean(i):
                pe.wait_ge(sem("u_staged"), i - 3)
                pe.wait_ge(sem("pool_loaded"), i * 32 - 96)
                for x in range(2):
                    for t in range(TT):
                        mm = nc.tensor.matmul(ps[:, T0, x * S:(x + 1) * S], ust[:, t, x * P:(x + 1) * P], rowp[:, t, :],
                                              start=t == 0, stop=t == 1)
                mm.then_inc(sem("pool_mean"), 1)

            def pool_mix(i):
                for e in range(2):
                    for x in range(2):
                        mm = nc.tensor.matmul(ps[:, T0, e * S:(e + 1) * S], pwg[:, x, e * P:(e + 1) * P], dT[:, x, :],
                                              start=x == 0, stop=x == 1)
                mm.then_inc(sem("pool_mixed"), 1)

            def between(i, c, k):
                if k == 0:
                    turn_qk(i, c)
                elif k == 1:
                    scores(i, c)
                elif k == 2:
                    (pool_mean, pool_mix)[c](i)
                elif k == 3:
                    turn_probs(i, c)
                else:
                    values(i, c)

            plain_product(pe, B_WIN, Q_WIN, 8, xT_hi, xT_lo, 4, between)

            def branches(i, ks, lead=0):
                for k in ks:
                    if k % 2 == 0:
                        acc_free(pe, Q_MERGE + k // 2, i, 2)
                    mm_block(pe, B_MERGE, 4, i, k, xT_hi, xT_lo, 4 * (k % 4), k % 4 // 2 * 2,
                             k % 2 == 0, k % 2 == 1)

            def turn_merged(i):
                pe.wait_ge(sem("merged_ready"), i + 1)
                for j in range(4):
                    for tok in range(TT):
                        tr = nc.tensor.transpose(ps[:, T0 + j, tok * P:(tok + 1) * P],
                                                 m_tmp[:, tok, j * P:(j + 1) * P], ident[:])
                    tr.then_inc(sem("merged_turned"), 1)

            pe.wait_ge(sem("inputs_lo"), 2)
            branches(0, (0, 1))
            pe.wait_ge(sem("inputs_lo"), 4)
            with pe.Fori(0, 3) as i:
                branches(i, (2, 3, 4, 5))
                turn_merged(i)
            branches(3, (2, 3))
            turn_merged(3)

            def turn_sums(c):
                for tok in range(TT):
                    pe.wait_ge(drained[tok], 2 + Q_WOUT + c + 1)
                turn_rows(pe, resid, KT, range(4 * c, 4 * c + 4))

            pe.wait_ge(sem("merged_lo"), KT)
            for c in range(4):
                acc_free(pe, Q_WOUT + c)
                for k in range(4):
                    if c and k == 2:
                        turn_sums(c - 1)
                    mm_block(pe, B_WOUT, 4, c, k, mT_hi, mT_lo, 4 * k, c % 2 * 2, k == 0, k == 3)

            turn_sums(3)

            def up_gate(i, ks):
                for k in ks:
                    if k % 4 == 0:
                        acc_free(pe, Q_GU + k // 4, i, 2)
                    mm_block(pe, B_GU, 8, i, k, xT_hi, xT_lo, 4 * (k % 4), k % 8 // 4 * 2,
                             k % 4 == 0, k % 4 == 3)

            def turn_hidden(i):
                for tok in range(TT):
                    pe.wait_ge(drained[tok], i * 2 + (Q_GU + 2 + 2))
                for j in range(4):
                    for tok in range(TT):
                        c = j % 2 * S + tok * P
                        tr = nc.tensor.transpose(ps[:, T0 + j // 2, c:c + P],
                                                 h_act[:, tok, j * P:(j + 1) * P], ident[:])
                tr.then_inc(sem("hidden_turned"), 1)

            pe.wait_ge(turned_lo, 2 * KT)
            up_gate(0, (0, 1))
            with pe.Fori(0, 10) as i:
                up_gate(i, range(2, 10))
                turn_hidden(i)
            up_gate(10, range(2, 8))
            turn_hidden(10)

            def down_block(i, k, start, stop):
                pe.wait_ge(sem("hidden_staged"), i * 4 + (k + 1))
                pe.wait_ge(block_split, i * 4 + (B_DOWN + k + 1 + RAW_SLOTS))
                for tok in range(TT):
                    xh = aT_hi[:, k % 2, tok * P:(tok + 1) * P]
                    xl = aT_lo[:, k % 2, tok * P:(tok + 1) * P]
                    for n in range(4):
                        wh = w_hi[:, k % 2, n * CC:(n + 1) * CC]
                        wl = w_lo[:, k % 2, n * CC:(n + 1) * CC]
                        o = ps[:, 2 * n + tok, :]
                        nc.tensor.matmul(o, xh, wh, start=start, stop=False)
                        nc.tensor.matmul(o, xh, wl, start=False, stop=False)
                        mm = nc.tensor.matmul(o, xl, wh, start=False, stop=stop)
                mm.then_inc(block_used, 1)

            acc_free(pe, Q_DOWN + 1)
            for k in range(4):
                down_block(0, k, k == 0, False)
            with pe.Fori(1, 10) as i:
                for k in range(4):
                    down_block(i, k, False, False)
            for k in range(4):
                down_block(10, k, False, k == 3)

            pe.wait_ge(sem("down_added"), 4)
            for half in range(2):
                pe.wait_ge(sem("final_normed"), 2 * half + 2)
                turn_rows(pe, resid, 2 * KT, range(8 * half, 8 * half + 8))

            pe.wait_ge(turned_lo, 3 * KT)
            plain_product(pe, B_WIN2, Q_WIN2, 7, xT_hi, xT_lo)
            for c, width in ((14, CC), (15, N2 - 15 * CC)):
                acc_free(pe, Q_WIN2 + c)
                for k in range(4):
                    mm_block(pe, B_WIN2 + 4 * c, 4, 0, k, xT_hi, xT_lo, 4 * k, 2 * (c % 2), k == 0, k == 3, width)

            for tok in range(TT):
                pe.wait_ge(drained[tok], 2 + 68)
            for j, cols_ in enumerate((C_KS, C_KW, C_KC, C_VC)):
                for g in range(2):
                    for tok in range(TT):
                        tr = nc.tensor.transpose(ps[:, T0 + j, g * S + tok * P:g * S + (tok + 1) * P],
                                                 z2[:, tok, cols_ + g * P:cols_ + (g + 1) * P], ident[:])
                tr.then_inc(sem("keys_turned"), 1)
            pe.wait_ge(sem("windows_ready"), 1)
            for k in range(4):
                kv = k // 2
                hi, lo = ((A_hi, A_lo), (A_hi2, A_lo2))[kv]
                pe.wait_ge(block_split, B_CMP + k + 1 + RAW_SLOTS)
                for t in range(16):
                    wh = w_hi[:, k % 2, t * P:(t + 1) * P]
                    wl = w_lo[:, k % 2, t * P:(t + 1) * P]
                    p = 16 * (k % 2) + t
                    o = ps[:, kv, 0:30]
                    nc.tensor.matmul(o, wh, hi[:, p, :], start=p == 0, stop=False)
                    nc.tensor.matmul(o, wh, lo[:, p, :], start=False, stop=False)
                    mm = nc.tensor.matmul(o, wl, hi[:, p, :], start=False, stop=p == 31)
                mm.then_inc(block_used, 1)
            pe.wait_ge(sem("hid_ready"), 1)
            nc.tensor.matmul(ps[:, 2, 0:30], cw2[:, 0, :], hid[:, 0, 0:30], start=True, stop=True)
            for g in range(2):
                mm = nc.tensor.matmul(ps[0:NCMP, 3, g * P:(g + 1) * P], hid[:, 1, g * NCMP:(g + 1) * NCMP],
                                      cw2[:, 1, :], start=True, stop=True)
            mm.then_inc(sem("compressed"), 1)

            pe.wait_ge(sem("kcT_ready"), 1)
            pe.wait_ge(sem("vc_ready"), 1)
            with pe.Fori(0, 2) as g:
                def keysT(b):
                    return KTs[:, b, bass.ds(g, 1), :].rearrange("p a n -> p (a n)")

                for hh in range(4):
                    n = g * 4 + hh
                    pe.wait_ge(sem("q2_staged"), n + 1)
                    for tok in range(TT):
                        tr = nc.tensor.transpose(ps[:, T0, tok * P:(tok + 1) * P], q2[:, tok, :], ident[:])
                    tr.then_inc(sem("q2_turned"), 1)
                    pe.wait_ge(sem("q2T_ready"), n + 1)
                    for qt in range(TT):
                        q = q2T[:, qt * P:(qt + 1) * P]
                        for b in range(2):
                            o = ps[:, b, 0:P] if qt == 0 else ps[:, b, P:384]
                            nc.tensor.matmul(o, q, keysT(b)[:, 0:P] if qt == 0 else keysT(b), start=True, stop=True)
                        mm = nc.tensor.matmul(ps[:, 2, 16 * qt:16 * qt + NCMP], q,
                                              kcT[:, bass.ds(g * NCMP, NCMP)], start=True, stop=True)
                    mm.then_inc(sem("scores2_ready"), 1)
                    pe.wait_ge(sem("probs2_ready"), n * 6 + 6)
                    for b in range(2):
                        for j in range(3):
                            nc.tensor.transpose(ps[:, T1 + b, j * P:(j + 1) * P], pr[:, b, j * P:(j + 1) * P], ident[:])
                    for qt in range(TT):
                        tr = nc.tensor.transpose(ps[0:NCMP, T3, qt * P:(qt + 1) * P], prc[:, qt, 0:NCMP], ident[:])
                    tr.then_inc(sem("probs2_turned"), 1)
                    pe.wait_ge(sem("pT2_ready_0"), n * 2 + 2)
                    pe.wait_ge(sem("pT2_ready_1"), n + 1)
                    for qt in range(TT):
                        o = ps[:, 3, qt * P:(qt + 1) * P]
                        for b, c in enumerate((C_VS, C_VW)):
                            for j in range(qt + 1):
                                seg = (0, P, 2 * P)[qt + j]
                                nc.tensor.matmul(o, pT2[:, b, seg:seg + P], z2[:, j, bass.ds(g * P + c, P)],
                                                 start=b == 0 and j == 0, stop=False)
                        mm = nc.tensor.matmul(o, pcT[0:NCMP, qt * P:(qt + 1) * P],
                                              vc[0:NCMP, bass.ds(g, 1), :].rearrange("p a n -> p (a n)"),
                                              start=False, stop=True)
                    mm.then_inc(sem("pv2_done"), 1)

            rwkv_pe(pe)

            pe.wait_ge(sem("mix_ready"), 1)
            turn_rows(pe, oy, 3 * KT)

            pe.wait_ge(turned_lo, 4 * KT)
            plain_product(pe, B_WOUT2, Q_WOUT2, 2, xT_hi, xT_lo)


INPUTS = ("x", "norm_mix", "w_in", "rel_bias", "pool_w", "pool_scale", "w_branch_a", "w_branch_b", "w_out",
          "norm_ffn", "w_gate_up", "w_down", "norm_final", "pre_norm_g_2", "w_in_2", "rel_bias_table_2",
          "cmp_pos_k_2", "cmp_pos_v_2", "cmp_k_w1_2", "cmp_k_w2_2", "cmp_v_w1_2", "cmp_v_w2_2", "rwkv_mu_2",
          "rwkv_w0_2", "rwkv_w2_2", "rwkv_a0_2", "rwkv_a2_2", "rwkv_k_k_2", "rwkv_k_a_2", "rwkv_r_k_2",
          "rwkv_ln_w_2", "rwkv_ln_b_2", "w_out_2", "post_norm_g_2")


def kernel(**inputs):
    import numpy as _np
    import concourse.bacc as _bacc
    from concourse.bass_utils import run_bass_kernel_spmd as _run

    nc = _bacc.Bacc("TRN2", target_bir_lowering=False, num_devices=1)
    arrays, aps = {}, {}
    given = {name: _np.ascontiguousarray(inputs[name]) for name in INPUTS}
    for name, value in list(given.items()) + list(shape_constants().items()):
        arrays[f"in_{name}"] = value
        aps[name] = nc.dram_tensor(f"in_{name}", value.shape, F32, kind="ExternalInput").ap()
    out = nc.dram_tensor("out", (1, S, D), F32, kind="ExternalOutput").ap()
    program(nc, aps, out)
    r = _run(nc, [arrays], core_ids=[0])
    return r.results[0]["out"]
```

```python
import math
from contextlib import ExitStack

import numpy as np

import concourse.bass as bass
from concourse import mybir

ALU = mybir.AluOpType
ACT = mybir.ActivationFunctionType
AX = mybir.AxisListType.X
F32 = mybir.dt.float32
F32R = mybir.dt.float32r

P = 128
S = 256
TT = S // P
D = 2048
KT = D // P
CC = 512
BT = 4
BLK = BT * CC
RAW_SLOTS = 4
SPLIT_SLOTS = 2
EPS = 1e-6
NEG = -1e30

AW = 1024
PW = 1024
FF = 5632
FKT = FF // P
REL = 128
HN = 8
NB = 32
NCMP = 15
C_KC, C_VC, C_KS, C_VS, C_KW, C_VW = (1024 + 256 * n for n in range(6))
C_GATE = 2560
C_ZA = 2584
C_R = 3608
C_LORA = C_R + 3072
C_ZB = 6808
N2 = 7832

B_WIN, B_MERGE, B_WOUT, B_GU, B_DOWN, B_WIN2, B_CMP, B_REST2, B_WOUT2 = 0, 64, 80, 96, 184, 228, 252, 256, 296
LEAD2 = 6
N_BLOCKS = 312
Q_WIN, Q_MERGE, Q_WOUT, Q_GU, Q_DOWN, Q_WIN2, Q_WOUT2 = 0, 16, 24, 28, 50, 52, 68


def relative_buckets(dist):
    n = np.maximum(dist, 0)
    large = 16 + (np.log(np.maximum(n, 1).astype(np.float32) / np.float32(16))
                  / np.float32(math.log(1024 / 16)) * np.float32(16)).astype(np.int32)
    return np.where(n < 16, n, np.minimum(large, 31))


def shape_constants():
    c = {"ident": np.eye(P, dtype=np.float32)}
    z = np.arange(384)
    dist = 255 - z
    pick = np.zeros((384, 384), np.float32)
    pick[np.clip(dist, -REL, REL) + REL, z] = 1.0
    c["pick_rel"] = pick
    z = np.arange(512)
    dist = 255 - z
    pick = np.zeros((NB, 512), np.float32)
    pick[relative_buckets(dist), z] = 1.0
    c["pick_bucket"] = pick
    c["future"] = np.tile(np.where(dist < 0, NEG, 0.0).astype(np.float32), (HN, 1))
    t = np.arange(S)
    pool = np.zeros((4, S, S), np.float32)
    for g, w in enumerate((2, 4, 8, 16)):
        for tok in range(S):
            lo = max(tok + 1 - w, 0)
            pool[g, lo:tok + 1, tok] = np.float32(1.0) / np.float32(tok + 1 - lo)
            pool[g, tok, tok] -= 1.0
    c["pool_rows"] = pool
    s, q = np.arange(P)[:, None], np.arange(P)[None, :]
    chunk = s // 64 == q // 64
    strict, inclusive = (chunk & (s < q)), (chunk & (s <= q))
    masks = [strict, inclusive, strict, inclusive]
    for level in range(6):
        h = 1 << level
        masks.append((s // (2 * h) == q // (2 * h)) & (s % (2 * h) < h) & (q % (2 * h) >= h))
    masks.append(chunk)
    c["masks"] = np.stack(masks).astype(np.float32)
    return c


def program(nc, a, out):
    with ExitStack() as ctx:
        sems = {}

        def sem(name):
            if name not in sems:
                sems[name] = ctx.enter_context(nc.semaphore(name))
            return sems[name]

        BASE = 16640
        cursor = [BASE]

        def at(name, shape, dt=F32, offset=None):
            if offset is None:
                offset = cursor[0]
                size = 4 * int(np.prod(shape[1:]))
                cursor[0] += -(-size // 32) * 32
                assert cursor[0] <= 229368, (name, cursor[0])
            return nc.alloc_sbuf_tensor_at(name, shape, dt, offset=offset)

        class Region:
            def __init__(self, start, size):
                self.start, self.at, self.end = start, start, start + size

            def __call__(self, name, shape, dt=F32):
                size = -(-4 * int(np.prod(shape[1:])) // 32) * 32
                assert self.at + size <= self.end, (name, self.at + size - self.end)
                t = at(name, shape, dt, self.at)
                self.at += size
                return t

        resid = at("resid", [P, TT, D])
        XT0 = cursor[0]
        xT_hi = at("xT_hi", [P, KT, S], F32R)
        xT_lo = at("xT_lo", [P, KT, S], F32R)
        raw = at("raw", [P, RAW_SLOTS, BLK])
        w_hi = at("w_hi", [P, SPLIT_SLOTS, BLK], F32R)
        w_lo = at("w_lo", [P, SPLIT_SLOTS, BLK], F32R)
        Z0 = cursor[0]
        cursor[0] += 65536
        OY0 = cursor[0]
        cursor[0] += 16384
        ident = at("ident", [P, P])
        per_feature = at("per_feature", [P, 125])
        gains = per_feature[:, 0:48].rearrange("p (g k) -> p g k", g=3)
        pool_scale = per_feature[:, 48:56]
        par = per_feature[:, 56:96].rearrange("p (x k) -> p x k", x=5)
        mu = per_feature[:, 96:121]
        Pend = per_feature[:, 121:125]
        nw0a0 = at("nw0a0", [P, 2, 8])
        stats = at("stats", [P, 4 + 2 * TT])
        rinv = stats[:, 4:8].rearrange("p (x t) -> p x t", x=2)
        F0 = cursor[0]
        FSZ = 229368 - F0
        qkvu = at("qkvu", [P, TT, 4096], F32, Z0)
        gate = at("gate", [P, TT, 2 * D], F32, Z0 + 32768)
        mT_hi = at("mT_hi", [P, KT, S], F32R, Z0)
        mT_lo = at("mT_lo", [P, KT, S], F32R, Z0 + 16384)
        actT = at("actT", [P, FKT, S], F32, Z0)
        z2 = at("z2", [P, TT, N2], F32, Z0)
        scaled = at("scaled", [P, TT, D], F32, OY0)
        oy = at("oy", [P, TT, D], F32, OY0)
        r = Region(OY0, 16384)
        relb = r("relb", [P, 2, 256])
        qst = r("qst", [P, TT, P])
        kst = r("kst", [P, TT, P])
        vst = r("vst", [P, TT, P])
        qkT = r("qkT", [P, 2, S])
        prob = r("prob", [P, 2, 384])
        probT = r("probT", [P, 2, 384])
        r = Region(OY0, 16384)
        g_act = r("g_act", [P, TT, CC])
        h_act = r("h_act", [P, TT, CC])
        m_tmp = r("m_tmp", [P, TT, CC])
        r = Region(F0, FSZ)
        smax = r("smax", [P, 4])
        ssum = r("ssum", [P, 4])
        rowp = r("rowp", [P, 2, S])
        pwg = r("pwg", [P, 2, S])
        ust = r("ust", [P, TT, S])
        dT = r("dT", [P, 2, S])
        r = Region(Z0 + 32768, 32768)
        mix_rows = r("mix_rows", [KT, P])
        par_rows = r("par_rows", [121 - KT, P])
        rel_in = r("rel_in", [16, 2 * REL + 1])
        relT = r("relT", [P, 3, 16])
        pick_rel = r("pick_rel", [P, 3, 384])
        rel_row = r("rel_row", [16, 384])
        pick_b = r("pick_b", [NB, 512])
        future = r("future", [HN, 512])
        buck_row = r("buck_row", [HN, 512])
        tableT = r("tableT", [NB, HN])
        r = Region(F0, FSZ)
        aT_hi = r("aT_hi", [P, 2, S], F32R)
        aT_lo = r("aT_lo", [P, 2, S], F32R)
        fin_gain = at("fin_gain", [P, D], F32, XT0)
        r = Region(OY0 + 4096, 4096)
        KTs = r("KTs", [P, 2, 2, S])
        r = Region(OY0 + 12288, 4096)
        hbias = r("hbias", [P, 384])
        posT = r("posT", [P, 2, 32])
        r = Region(Z0 + 4 * LEAD2 * CC, 4 * (N2 - LEAD2 * CC))
        blkA = r("blkA", [P, 32, 30])
        A_hi = r("A_hi", [P, 32, 30], F32R)
        A_lo = r("A_lo", [P, 32, 30], F32R)
        A_hi2 = r("A_hi2", [P, 32, 30], F32R)
        r = Region(Z0 + 4 * (N2 + LEAD2 * CC), 4 * (N2 - LEAD2 * CC))
        kvcT = r("kvcT", [P, 2, 2, S])
        r = Region(F0, FSZ)
        pT2 = at("pT2", [P, 2, 384], F32, r.at)
        A_lo2 = r("A_lo2", [P, 32, 30], F32R)
        cw2 = r("cw2", [P, 2, P])
        hid = r("hid", [P, 2, 32])
        hexp = r("hexp", [P, 2, 32])
        kcT = r("kcT", [P, 32])
        vc = r("vc", [16, 2, P])
        gsig = r("gsig", [P, TT, 24])
        q2 = r("q2", [P, TT, P])
        q2T = r("q2T", [P, S])
        pr = r("pr", [P, 2, 384])
        prc = r("prc", [P, TT, 16])
        mx2 = r("mx2", [P, 3, TT])
        sm2 = r("sm2", [P, 3, TT])
        pcT = r("pcT", [16, S])
        r = Region(XT0, 32768)
        bv = r("bv", [P, TT, 1024])
        masks = r("masks", [P, 11, P])
        l2 = r("l2", [P, 1024])
        l2s = r("l2s", [P, P])
        lora = r("lora", [P, S])
        ar = r("ar", [P, TT, 2, P])
        bT = r("bT", [P, TT, P])
        kTt = r("kTt", [P, TT, P])
        tokm = r("tokm", [P, TT, 4, P])
        snap = r("snap", [P, 4, P])
        AtT = r("AtT", [P, TT, P])
        Ml1 = r("Ml1", [P, 4, P])
        r = Region(Z0, 10240)
        Mm = r("Mm", [P, 4, 4, P])
        Ml0 = r("Ml0", [P, 4, P])
        r = Region(Z0 + 4 * N2, 10240)
        TX = r("TX", [P, 2, 4, P])
        Tm, Xm = TX[:, 0, :, :], TX[:, 1, :, :]
        Ym = r("Ym", [P, 4, P])
        stg = r("stg", [P, TT, 3, P])
        rT = r("rT", [P, TT, P])
        r = Region(F0, FSZ)
        fT = r("fT", [P, 3, S + 1])
        pf = r("pf", [P, 3, S])
        wa = r("wa", [P, 2, S])
        Pc = r("Pc", [P, 4, 65])
        iP = r("iP", [P, S])
        kkn = r("kkn", [P, S])
        tmpf = r("tmpf", [P, S])
        zero64 = r("zero64", [P, 64])
        W1 = r("W1", [P, TT, 2, 64])
        Uu = r("Uu", [P, TT, 2, 64])
        bon = r("bon", [P, TT, 2])
        st16 = r("st16", [P, 2, TT, 16])
        free = z2[:, :, C_R:C_R + 3072].rearrange("p t (x n) -> p t x n", x=3)
        shift_gated, gain_gated, ysq = free[:, :, 0, :], free[:, :, 1, :], free[:, :, 2, :]
        sig_a, sig_b = shift_gated, gain_gated
        lnw, lnb = free[:, 0, 2, :], free[:, 1, 2, :]
        y2 = at("y2", [P, TT, D], F32, Z0)
        post_gain = at("post_gain", [P, D], F32, Z0 + 16384)
        y2_sq = at("y2_sq", [P, TT, CC], F32, OY0)
        y2_sums = at("y2_sums", [P, TT, 4], F32, OY0 + 8192)
        sum_sq = at("sum_sq", [P, TT, 4], F32, F0 + 8192)

        ps = ctx.enter_context(nc.psum_tensor("ps", [P, 8, 512], F32))

        rel_dram = nc.dram_tensor("rel_row_dram", (16, 384), F32, kind="Internal").ap()
        rel_rows = nc.dram_tensor("rel_rows_dram", (P, 16, 384), F32, kind="Internal").ap()
        buck_rows = nc.dram_tensor("buck_rows_dram", (P, HN, 512), F32, kind="Internal").ap()
        buck_dram = nc.dram_tensor("buck_row_dram", (HN, 512), F32, kind="Internal").ap()

        landed = [sem(f"block_landed_{s}") for s in range(RAW_SLOTS)]
        hi_ready, block_split, block_used = sem("hi_ready"), sem("block_split"), sem("block_used")
        drained = [sem("acc_drained_0"), sem("acc_drained_1")]
        class Chain:
            def __init__(self, eng, name):
                self.eng, self.sem, self.base, self.n = eng, sem(name), 0, 0

            def __call__(self, ins):
                ins.then_inc(self.sem, 1)
                self.n += 1
                self.eng.wait_ge(self.sem, self.base + self.n)

            def loop(self, start, end, n):
                return ChainLoop(self, start, end, n)

        class ChainLoop:
            def __init__(self, chain, start, end, n):
                self.c, self.start, self.end, self.per = chain, start, end, n

            def __enter__(self):
                self.f = self.c.eng.Fori(self.start, self.end)
                i = self.f.__enter__()
                self.b0 = self.c.base + self.c.n
                self.c.base, self.c.n = (i - self.start) * self.per + self.b0 if self.start else i * self.per + self.b0, 0
                return i

            def __exit__(self, *e):
                r = self.f.__exit__(*e)
                if e[0] is None:
                    assert self.c.n == self.per, (self.c.n, self.per)
                    self.c.base, self.c.n = self.b0 + self.per * (self.end - self.start), 0
                return r

        def blocks_of(w, col0=0, width=CC):
            return w.rearrange("(t p) n -> p t n", p=P)

        W = {k: blocks_of(a[k][0]) for k in ("w_in", "w_branch_a", "w_branch_b", "w_out", "w_gate_up",
                                            "w_in_2", "w_out_2", "cmp_k_w1_2", "cmp_v_w1_2")}
        w_down = a["w_down"][0].rearrange("(t p) n -> t p n", p=P)

        def load(sp, k, dst, src, b_const, b_reg=None, group=4):
            sp.wait_ge(block_split, b_const + 1 if b_reg is None else b_reg + (b_const + 1))
            sp.dma_start(dst, src).then_inc(landed[k % 4], 16)

        def slot(k, width=CC):
            return raw[:, k % 4, 0:BT * width].rearrange("p (t n) -> p t n", t=BT)

        def cols(w, kb, c0, width=CC):
            return w[:, kb * BT:(kb + 1) * BT, c0:c0 + width]

        def dcols(w, kb, creg, width=CC):
            return w[:, kb * BT:(kb + 1) * BT, bass.ds(creg, width)]

        def stream(sp, i, phase, k):
            if phase == "w_in":
                load(sp, k, slot(k), dcols(W["w_in"], k, i * CC), B_WIN + k, i * 4)
            elif phase == "merge":
                w = W["w_branch_a"] if k < 2 else W["w_branch_b"]
                load(sp, k, slot(k), dcols(w, k % 2, i * CC), B_MERGE + k, i * 4)
            elif phase == "w_out":
                load(sp, k, slot(k), dcols(W["w_out"], k, i * CC), B_WOUT + k, i * 4)
            elif phase == "gate_up":
                c = i * CC if k < 4 else i * CC + FF
                load(sp, k, slot(k), dcols(W["w_gate_up"], k % 4, c), B_GU + k, i * 8)
            elif phase == "down":
                load(sp, k, raw[:, k % 4, :],
                     w_down[bass.ds(i * 4 + k, 1)].rearrange("a p n -> (a p) n"), B_DOWN + k, i * 4)
            elif phase == "w_in2":
                load(sp, k, slot(k), dcols(W["w_in_2"], k, i * CC), B_WIN2 + k, i * 4)
            elif phase == "w_in2_rest":
                load(sp, k, slot(k), dcols(W["w_in_2"], k, i * CC + LEAD2 * CC), B_REST2 + k, i * 4)
            elif phase == "w_in2_tail":
                load(sp, k, slot(k, N2 - 15 * CC), cols(W["w_in_2"], k, 15 * CC, N2 - 15 * CC), B_REST2 + 36 + k)
            elif phase == "compress":
                w = W["cmp_k_w1_2"] if k < 2 else W["cmp_v_w1_2"]
                load(sp, k, raw[:, k % 4, :].rearrange("p (t n) -> p t n", t=16),
                     w[:, (k % 2) * 16:(k % 2) * 16 + 16, :], B_CMP + k)
            elif phase == "w_out2":
                load(sp, k, slot(k), dcols(W["w_out_2"], k, i * CC), B_WOUT2 + k, i * 4)

        STREAMS = [("w_in", 16, 4), ("merge", 4, 4), ("w_out", 4, 4), ("gate_up", 11, 8), ("down", 11, 4),
                   ("w_in2", LEAD2, 4), ("compress", 0, 4), ("w_in2_rest", 15 - LEAD2, 4), ("w_in2_tail", 0, 4),
                   ("w_out2", 4, 4)]

        def split_hi(act, b0, per, i, k):
            assert b0 % 4 == 0 and per % 4 == 0
            act.wait_ge(landed[k % 4], i * (4 * per) + 16 * ((b0 + k) // 4 + 1))
            act.wait_ge(block_used, i * per + (b0 + k + 1))
            nc.scalar.copy(w_hi[:, k % 2, :], raw[:, k % 4, :]).then_inc(hi_ready, 1)

        def split_lo(dve, b0, per, i, k):
            dve.wait_ge(hi_ready, i * per + (b0 + k + 1))
            nc.vector.tensor_tensor(w_lo[:, k % 2, :], raw[:, k % 4, :], w_hi[:, k % 2, :].bitcast(F32),
                                    ALU.subtract).then_inc(block_split, 1)

        def chunk_done(eng, b0, per, i, k):
            eng.wait_ge(block_used, i * per + (b0 + k + 1 + SPLIT_SLOTS))

        def product_steps(eng, split, b0, per, i, ends, before={}):
            for k in range(per):
                for step in before.get(k, ()):
                    step(i)
                split(eng, b0, per, i, k + 2)
                if k in ends:
                    chunk_done(eng, b0, per, i, k)
                    ends[k](i)

        def mm_block(pe, b0, per, i, k, hi, lo, kt0, bank, start, stop, width=CC):
            pe.wait_ge(block_split, i * per + (b0 + k + 1 + RAW_SLOTS))
            for t in range(BT):
                for tok in range(TT):
                    xh = hi[:, kt0 + t, tok * P:(tok + 1) * P]
                    xl = lo[:, kt0 + t, tok * P:(tok + 1) * P]
                    wh = w_hi[:, k % 2, t * width:(t + 1) * width]
                    wl = w_lo[:, k % 2, t * width:(t + 1) * width]
                    o = ps[:, bank + tok, 0:width]
                    nc.tensor.matmul(o, xh, wh, start=start and t == 0, stop=False)
                    nc.tensor.matmul(o, xh, wl, start=False, stop=False)
                    mm = nc.tensor.matmul(o, xl, wh, start=False, stop=stop and t == BT - 1)
            mm.then_inc(block_used, 1)

        def acc_free(pe, q, i=0, per=0):
            for tok in range(TT):
                pe.wait_ge(drained[tok], i * per + (q + 1))

        def plain_product(pe, b0, q0, n2, hi, lo, first=0, between=None):
            with pe.Fori(first, n2) as i:
                for c in range(2):
                    if between:
                        between(i, c, 0)
                    acc_free(pe, q0 + c, i, 2)
                    for k in range(4):
                        if between and k:
                            between(i, c, k)
                        mm_block(pe, b0, 8, i, 4 * c + k, hi, lo, 4 * k, 2 * c, k == 0, k == 3)
                    if between:
                        between(i, c, 4)

        def branch_inputs(x, j):
            n = P if j < 2 else S
            return (x[:, 4 * j:4 * j + 4, :].rearrange("p i (t n) -> p t i n", t=TT) if j < 2 else
                    x[:, 4 * j:4 * j + 4, :].rearrange("p (i t) n -> p t i n", t=TT),
                    qkvu[:, :, (0, CC, 3072, 3072 + CC)[j]:(CC, 2 * CC, 3072 + CC, 4096)[j]]
                    .rearrange("p t (i n) -> p t i n", n=n))

        turned, turned_hi, turned_lo = sem("tile_turned"), sem("turned_hi"), sem("turned_lo")

        def turn_rows(pe, src, base, kts=range(KT)):
            for kt in kts:
                n = base + kt
                if n >= 4:
                    pe.wait_ge(turned_lo, n - 3)
                for tok in range(TT):
                    tr = nc.tensor.transpose(ps[:, 4 + n % 4, tok * P:(tok + 1) * P],
                                             src[:, tok, kt * P:(kt + 1) * P], ident[:])
                tr.then_inc(turned, 1)

        def turned_to_hi(act, base, g, kts=range(KT)):
            for kt in kts:
                n = base + kt
                act.wait_ge(turned, n + 1)
                scale = gains[:, g, kt:kt + 1] if g is not None else 1.0
                nc.scalar.activation(xT_hi[:, kt, :], ps[:, 4 + n % 4, 0:S], ACT.Copy,
                                     scale=scale).then_inc(turned_hi, 1)

        def turned_to_lo(dve, base, g, kts=range(KT)):
            for kt in kts:
                n = base + kt
                dve.wait_ge(turned_hi, n + 1)
                src, hi = ps[:, 4 + n % 4, 0:S], xT_hi[:, kt, :].bitcast(F32)
                if g is None:
                    ins = nc.vector.tensor_tensor(xT_lo[:, kt, :], src, hi, ALU.subtract)
                else:
                    ins = nc.vector.scalar_tensor_tensor(xT_lo[:, kt, :], src, gains[:, g, kt:kt + 1],
                                                         hi, ALU.mult, ALU.subtract)
                ins.then_inc(turned_lo, 1)

        def rms_act(act, x, scratch, n):
            for tok in range(TT):
                nc.scalar.activation(scratch[:, tok, :], x[:, tok, :], ACT.Square,
                                     accum_out=stats[:, tok:tok + 1]).then_inc(sem("square_sums"), 1)
            act.wait_ge(sem("mean_squares"), n + 1)
            nc.scalar.activation(stats[:, 2:4], stats[:, 0:2], ACT.Sqrt).then_inc(sem("rms_roots"), 1)

        def root_act(act, n):
            act.wait_ge(sem("mean_squares"), n + 1)
            nc.scalar.activation(stats[:, 2:4], stats[:, 0:2], ACT.Sqrt).then_inc(sem("rms_roots"), 1)

        def rms_dve(dve, link, n, parts=None):
            dve.wait_ge(sem("square_sums"), TT * (n + 1))
            if parts is not None:
                link(nc.vector.tensor_reduce(stats[:, 0:2], parts[:], AX, ALU.add))
            nc.vector.tensor_scalar(stats[:, 0:2], stats[:, 0:2], 1.0 / D, EPS, ALU.mult, ALU.add)\
                .then_inc(sem("mean_squares"), 1)
            dve.wait_ge(sem("rms_roots"), n + 1)
            nc.vector.reciprocal(rinv[:, n % 2, :], stats[:, 2:4]).then_inc(sem("rinv_ready"), 1)
            dve.wait_ge(sem("rinv_ready"), n + 1)


        T0, T1, T2, T3 = 4, 5, 6, 7

        def shifted(rows, width):
            _, heads, pitch = rows.shape
            return bass.AP(tensor=rows.tensor, offset=P - 1, ap=[[heads * pitch - 1, P], [pitch, heads], [1, width]])

        def windows(kv, g):
            v = kvcT[:, kv, g, :]
            return bass.AP(tensor=v.tensor, offset=v.offset, ap=[list(v.ap[0]), [1, 32], [16, NCMP]])

        LEVELS = 5
        HALF = float(np.float32(math.exp(-0.5)))

        def rwkv_act(act, link):
            for tok in range(TT):
                act.wait_ge(drained[tok], 2 + Q_WOUT2)
            act.wait_ge(sem("lora_turned"), 1)
            act.wait_ge(sem("edges_set"), 1)
            nc.scalar.copy(fT[:, 0, 1:S + 1], ps[:, T0, 0:S]).then_inc(sem("lora_copied"), 1)
            act.wait_ge(sem("lora_mixed"), 1)
            nc.scalar.activation(lora[0:64, :], lora[0:64, :], ACT.Tanh).then_inc(sem("lora_ready"), 1)
            act.wait_ge(sem("rwkv_loaded"), 48)

            def stage(i):
                for x in range(3):
                    nc.scalar.copy(stg[:, :, x, :], z2[:, :, bass.ds(i * P + (C_R + 1024 * x), P)])\
                        .then_inc(sem("feat_staged"), 1)
                nc.scalar.copy(l2s[:], l2[:, bass.ds(i * P, P)]).then_inc(sem("l2_staged"), 1)

            def features(i):
                act.wait_ge(sem("feat_turned"), i + 1)
                nc.scalar.copy(fT[:, 0:2, 1:S + 1], ps[:, T0, :].rearrange("p (x n) -> p x n", x=2))\
                    .then_inc(sem("fT_ready"), 1)
                nc.scalar.copy(fT[:, 2, 1:S + 1], ps[:, T1, 0:S]).then_inc(sem("fT_ready"), 1)

            def exps(i):
                act.wait_ge(sem("lora_done"), i + 1)
                for x in range(2):
                    nc.scalar.activation(wa[:, x, :], ps[:, T2 + x, 0:S], ACT.Exp, scale=-1.0,
                                         bias=nw0a0[:, x, bass.ds(i, 1)]).then_inc(sem("wa_exp"), 1)

            def decay(i):
                act.wait_ge(sem("wa_sigmoid"), i + 1)
                nc.scalar.activation(wa[:, 0, :], wa[:, 0, :], ACT.Exp, scale=-HALF).then_inc(sem("decay_ready"), 1)

            def norm(i):
                act.wait_ge(sem("kk_summed"), i + 1)
                nc.scalar.activation(tmpf[:], ps[:, T0, 0:S], ACT.Sqrt).then_inc(sem("kk_norm"), 1)

            def pair(i, ahead):
                act.wait_ge(sem("tok_turned"), i + 1)
                nc.scalar.copy(tokm[:, 0, :, :], ps[:, T1, :].rearrange("p (x n) -> p x n", x=4))\
                    .then_inc(sem("tokm_ready_0"), 1)
                nc.scalar.copy(rT[:], ar[:, :, 1, :]).then_inc(sem("rT_ready"), 1)
                if ahead:
                    stage(i + 1)
                for h in range(2):
                    act.wait_ge(sem("x1_turned"), i * 2 + (h + 1))
                    nc.scalar.copy(Tm[:, 2 * h:2 * h + 2, :], ps[:, h, 0:S].rearrange("p (m n) -> p m n", m=2))\
                        .then_inc(sem("t1_ready"), 1)
                for lev in range(LEVELS):
                    for h in range(2):
                        act.wait_ge(sem("y_made"), i * (2 * LEVELS) + (2 * lev + h + 1))
                        nc.scalar.copy(Ym[:, 2 * h:2 * h + 2, :], ps[:, h, 0:S].rearrange("p (m n) -> p m n", m=2))\
                            .then_inc(sem("y_copied"), 1)
                    if ahead and lev < 4:
                        (features, exps, decay, norm)[lev](i + 1)
                    elif lev < 4:
                        if lev == 0:
                            act.wait_ge(sem("feat_staged"), 24)
                        c, t = ((C_ZA, sig_a), (C_ZB, sig_b))[lev // 2], lev % 2
                        nc.scalar.activation(c[1][:, t, :], z2[:, t, c[0]:c[0] + 1024], ACT.Sigmoid)\
                            .then_inc(sem("z_sig"), 1)
                act.wait_ge(sem("at_made"), i + 1)
                nc.scalar.copy(AtT[:], ps[:, 1, 0:S].rearrange("p (t n) -> p t n", t=TT)).then_inc(sem("at_ready"), 1)

            stage(0)
            for step in (features, exps, decay, norm):
                step(0)
            with act.Fori(0, 7) as i:
                pair(i, True)
            pair(7, False)

        def rwkv_dve(dve, link):
            dve.wait_ge(sem("nsa_out_ready"), HN + 1)
            dve.wait_ge(block_used, B_WOUT2 + SPLIT_SLOTS)
            link(nc.vector.memset(fT[:, :, 0:1], 0.0))
            link(nc.vector.memset(zero64[:], 0.0))
            link(nc.vector.memset(Pc[:, :, 0:1], 1.0))
            link(nc.vector.memset(snap[:, 0, :], 0.0))
            link(nc.vector.tensor_scalar(nw0a0[:], par[:, 0:2, :], -1.0, None, ALU.mult))
            dve.sem_inc(sem("edges_set"), 1)
            dve.wait_ge(sem("lora_copied"), 1)
            link(nc.vector.tensor_tensor(lora[:], fT[:, 0, 0:S], fT[:, 0, 1:S + 1], ALU.subtract))
            link(nc.vector.scalar_tensor_tensor(lora[:], lora[:], mu[:, 24:25], fT[:, 0, 1:S + 1], ALU.mult, ALU.add))
            dve.sem_inc(sem("lora_mixed"), 1)
            dve.wait_ge(sem("rwkv_loaded"), 48)


            def shift(i):
                dve.wait_ge(sem("fT_ready"), i * 2 + 2)
                link(nc.vector.tensor_tensor(pf[:], fT[:, :, 0:S], fT[:, :, 1:S + 1], ALU.subtract))
                for x in range(3):
                    link(nc.vector.scalar_tensor_tensor(pf[:, x, :], pf[:, x, :], mu[:, bass.ds(i + 8 * x, 1)],
                                                        fT[:, x, 1:S + 1], ALU.mult, ALU.add))
                link(nc.vector.tensor_scalar(kkn[:], pf[:, 1, :], par[:, 2, bass.ds(i, 1)], None, ALU.mult))
                link(nc.vector.tensor_tensor(tmpf[:], kkn[:], kkn[:], ALU.mult))
                dve.sem_inc(sem("kk_squared"), 1)

            def sigmoids(i):
                dve.wait_ge(sem("wa_exp"), i * 2 + 2)
                link(nc.vector.tensor_scalar(wa[:], wa[:], 1.0, None, ALU.add))
                link(nc.vector.reciprocal(wa[:], wa[:]))
                dve.sem_inc(sem("wa_sigmoid"), 1)

            def normed(i):
                dve.wait_ge(sem("kk_norm"), i + 1)
                link(nc.vector.tensor_scalar(tmpf[:], tmpf[:], 1e-12, None, ALU.max))
                link(nc.vector.reciprocal(tmpf[:], tmpf[:]))
                link(nc.vector.tensor_tensor(kkn[:], kkn[:], tmpf[:], ALU.mult))

            def decays(i):
                dve.wait_ge(sem("decay_ready"), i + 1)
                for c in range(4):
                    link(nc.vector.tensor_tensor_scan(Pc[:, c, 1:65], wa[:, 0, 64 * c:64 * c + 64], zero64[:], 1.0,
                                                      ALU.mult, ALU.add))

            def scaled_ar(i):
                for t in range(TT):
                    kv = kkn[:, t * P:(t + 1) * P].rearrange("p (c n) -> p c n", c=2)
                    rv = pf[:, 0, t * P:(t + 1) * P].rearrange("p (c n) -> p c n", c=2)
                    link(nc.vector.scalar_tensor_tensor(ar[:, t, 0, :].rearrange("p (c n) -> p c n", c=2), kv, -1.0,
                                                        Pc[:, 2 * t:2 * t + 2, 0:64], ALU.mult, ALU.mult))
                    link(nc.vector.tensor_tensor(ar[:, t, 1, :].rearrange("p (c n) -> p c n", c=2), rv,
                                                 Pc[:, 2 * t:2 * t + 2, 1:65], ALU.mult))

            def scaled_b(i):
                link(nc.vector.reciprocal(iP[:].rearrange("p (c n) -> p c n", c=4), Pc[:, :, 1:65]))
                link(nc.vector.tensor_tensor(kkn[:], kkn[:], wa[:, 1, :], ALU.mult))
                link(nc.vector.tensor_tensor(bT[:].rearrange("p t n -> p (t n)"), kkn[:], iP[:], ALU.mult))

            def scaled_k(i):
                link(nc.vector.tensor_scalar(wa[:, 0, :], wa[:, 1, :], 1.0, par[:, 3, bass.ds(i, 1)],
                                             ALU.subtract, ALU.mult))
                link(nc.vector.scalar_tensor_tensor(wa[:, 0, :], wa[:, 0, :], 1.0, pf[:, 1, :], ALU.add, ALU.mult))
                link(nc.vector.tensor_tensor(kTt[:].rearrange("p t n -> p (t n)"), wa[:, 0, :], iP[:], ALU.mult))
                link(nc.vector.scalar_tensor_tensor(tmpf[:], pf[:, 0, :], par[:, 4, bass.ds(i, 1)], wa[:, 0, :],
                                                    ALU.mult, ALU.mult))
                dve.sem_inc(sem("features_ready"), 1)

            def pair(i, ahead):
                link(nc.vector.tensor_copy(Pend, Pc[:, :, 64]))
                dve.wait_ge(sem("m_made"), i + 1)
                for m in range(4):
                    link(nc.vector.tensor_tensor(Mm[:, m, :, :], ps[:, m, :].rearrange("p (x n) -> p x n", x=4),
                                                 masks[:, 0:4, :], ALU.mult))
                dve.sem_inc(sem("m_masked"), 1)
                for h in range(2):
                    x = Xm[:, 2 * h:2 * h + 2, :]
                    link(nc.vector.tensor_tensor(x, Mm[:, 2 * h:2 * h + 2, 0, :],
                                                 masks[:, 4:5, :].broadcast_to([P, 2, P]), ALU.mult))
                    link(nc.vector.tensor_tensor(x, x, ident[:].unsqueeze(1).broadcast_to([P, 2, P]), ALU.add))
                    dve.sem_inc(sem("x1_ready"), 1)
                dve.wait_ge(sem("tok_turned"), i + 1)
                link(nc.vector.tensor_copy(tokm[:, 1, :, :], ps[:, T2, :].rearrange("p (x n) -> p x n", x=4)))
                dve.sem_inc(sem("tokm_ready_1"), 1)
                link(nc.vector.tensor_copy(bon[:], ps[:, T3, 0:4].rearrange("p (t h) -> p t h", t=TT)))
                dve.sem_inc(sem("bonus_read"), 1)
                for lev in range(LEVELS):
                    for h in range(2):
                        dve.wait_ge(sem("level_made"), i * (2 * LEVELS) + (2 * lev + h + 1))
                        if lev < LEVELS - 1:
                            x = TX[:, :, 2 * h:2 * h + 2, :].rearrange("p x m n -> p x (m n)")
                            d = ps[:, 2 + h, :].rearrange("p (x n) -> p x n", x=2)
                        else:
                            x = Xm[:, 2 * h:2 * h + 2, :].rearrange("p m n -> p (m n)")
                            d = ps[:, 2 + h, S:2 * S]
                        nc.vector.tensor_tensor(x, x, d, ALU.add).then_inc(sem("level_added"), 1)
                    if lev == 0:
                        dve.wait_ge(sem("tokm_ready_0"), i + 1)
                        for t in range(TT):
                            for hd in range(2):
                                nc.vector.tensor_scalar(bv[:, t, bass.ds(i * P + 64 * hd, 64)],
                                                        tokm[:, t, 3, 64 * hd:64 * hd + 64], bon[:, t, hd:hd + 1],
                                                        None, ALU.mult).then_inc(sem("bonus_ready"), 1)
                    if ahead and 1 <= lev <= 2:
                        (shift, sigmoids)[lev - 1](i + 1)
                if ahead:
                    normed(i + 1)
                    decays(i + 1)
                dve.wait_ge(sem("w0_made"), i + 1)
                link(nc.vector.tensor_copy(Uu[:].rearrange("p t h n -> p (t h n)"), ps[:, 0, 0:S]))
                dve.sem_inc(sem("w0_ready"), 1)
                dve.wait_ge(sem("w1_made"), i + 1)
                link(nc.vector.tensor_copy(W1[:].rearrange("p t h n -> p (t h n)"), ps[:, 2, 0:S]))
                for c in range(4):
                    t, rows = c // 2, slice(64 * (c % 2), 64 * (c % 2) + 64)
                    dve.wait_ge(sem("u_made"), i * 4 + (c + 1))
                    nc.vector.tensor_tensor(Uu[rows, t, :, :].rearrange("p h n -> p (h n)"), ps[rows, 0, 0:P],
                                            W1[rows, t, :, :].rearrange("p h n -> p (h n)"), ALU.add)\
                        .then_inc(sem("u_ready"), 1)
                    if ahead and c == 1:
                        dve.wait_ge(sem("rT_ready"), i + 1)
                        scaled_ar(i + 1)
                    if ahead and c == 3:
                        scaled_b(i + 1)
                        scaled_k(i + 1)
                    if c < 3:
                        link(nc.vector.tensor_scalar(snap[:, c + 1, :], snap[:, c, :], Pend[:, c:c + 1], None, ALU.mult))
                        dve.wait_ge(sem("s_made"), i * 3 + (c + 1))
                        for hd in range(2):
                            h = slice(64 * hd, 64 * hd + 64)
                            nc.vector.scalar_tensor_tensor(snap[h, c + 1, h], ps[h, 3, h], Pend[h, c:c + 1],
                                                           snap[h, c + 1, h], ALU.mult, ALU.add)\
                                .then_inc(sem("s_ready"), 1)
                        dve.wait_ge(sem("s_ready"), i * 6 + (2 * c + 2))
                dve.wait_ge(sem("y_out_made"), i + 1)
                nc.vector.tensor_copy(oy[:, :, bass.ds(i * P + 1024, P)],
                                      ps[:, 1, 0:S].rearrange("p (t n) -> p t n", t=TT)).then_inc(sem("pair_done"), 1)

            shift(0)
            sigmoids(0)
            normed(0)
            decays(0)
            scaled_ar(0)
            scaled_b(0)
            scaled_k(0)
            with link.loop(0, 7, 42) as i:
                pair(i, True)
            pair(7, False)

        def group_norm(dve, link, half):
            c = slice(512 * half, 512 * half + 512)
            y = oy[:, :, 1024 + 512 * half:1536 + 512 * half]
            yh = y.rearrange("p t (h n) -> p t h n", h=8)
            yq = ysq[:, :, c].rearrange("p t (h n) -> p t h n", h=8)
            mean, var = (st16[:, x, :, 8 * half:8 * half + 8] for x in range(2))
            wide = [P, TT, 8, 64]
            link(nc.vector.tensor_reduce(mean, yh, AX, ALU.add))
            link(nc.vector.tensor_scalar(mean, mean, 1.0 / 64, None, ALU.mult))
            link(nc.vector.tensor_tensor(yh, yh, mean.unsqueeze(3).broadcast_to(wide), ALU.subtract))
            link(nc.vector.tensor_tensor(yq, yh, yh, ALU.mult))
            link(nc.vector.tensor_reduce(var, yq, AX, ALU.add))
            link(nc.vector.tensor_scalar(var, var, 1.0 / 64, 64e-5, ALU.mult, ALU.add))
            dve.sem_inc(sem("gn_var"), 1)
            dve.wait_ge(sem("gn_root"), half + 1)
            link(nc.vector.reciprocal(var, var))
            link(nc.vector.tensor_tensor(yh, yh, var.unsqueeze(3).broadcast_to(wide), ALU.mult))
            link(nc.vector.tensor_tensor(y, y, gain_gated[:, :, c], ALU.mult))
            nc.vector.tensor_tensor(y, y, shift_gated[:, :, c], ALU.add).then_inc(sem("gn_done"), 1)

        def rwkv_pe(pe):
            for tok in range(TT):
                pe.wait_ge(drained[tok], 2 + Q_WOUT2)
            for tok in range(TT):
                tr = nc.tensor.transpose(ps[:, T0, tok * P:(tok + 1) * P], z2[:, tok, C_LORA:C_LORA + P], ident[:])
            tr.then_inc(sem("lora_turned"), 1)
            pe.wait_ge(sem("lora_ready"), 1)

            def turn_features(i):
                pe.wait_ge(sem("feat_staged"), i * 3 + 3)
                for x in range(3):
                    for tok in range(TT):
                        c = (x % 2) * S + tok * P
                        tr = nc.tensor.transpose(ps[:, T0 + x // 2, c:c + P], stg[:, tok, x, :], ident[:])
                tr.then_inc(sem("feat_turned"), 1)

            def low_rank(i):
                pe.wait_ge(sem("l2_staged"), i + 1)
                nc.tensor.matmul(ps[:, T2, 0:S], l2s[0:64, :], lora[0:64, :], start=True, stop=True)
                nc.tensor.matmul(ps[:, T3, 0:S], l2s[64:128, :], lora[64:128, :], start=True, stop=True)\
                    .then_inc(sem("lora_done"), 1)

            def kk_sums(i):
                pe.wait_ge(sem("kk_squared"), i + 1)
                nc.tensor.matmul(ps[:, T0, 0:S], masks[:, 10, :], tmpf[:], start=True, stop=True)\
                    .then_inc(sem("kk_summed"), 1)

            def pair(i, ahead):
                pe.wait_ge(sem("features_ready"), i + 1)
                for tok in range(TT):
                    for x, src in enumerate((ar[:, tok, 0, :], bT[:, tok, :], kTt[:, tok, :],
                                             pf[:, 2, tok * P:(tok + 1) * P])):
                        nc.tensor.transpose(ps[:, T1 + tok, x * P:(x + 1) * P], src, ident[:])
                for tok in range(TT):
                    mm = nc.tensor.matmul(ps[:, T3, 2 * tok:2 * tok + 2], tmpf[:, tok * P:(tok + 1) * P],
                                          masks[:, 10, 0:P:64], start=True, stop=True)
                mm.then_inc(sem("tok_turned"), 1)
                pe.wait_ge(sem("pair_done"), i + 1)
                for tok in range(TT):
                    for src, c in ((bT, 0), (kTt, S)):
                        for hd in range(2):
                            h = slice(64 * hd, 64 * hd + 64)
                            mm = nc.tensor.matmul(ps[:, 2 * tok + hd, c:c + S], src[h, tok, :],
                                                  ar[h, tok, :, :].rearrange("p x n -> p (x n)"), start=True, stop=True)
                mm.then_inc(sem("m_made"), 1)
                for h in range(2):
                    pe.wait_ge(sem("x1_ready"), i * 2 + (h + 1))
                    for m in range(2):
                        tr = nc.tensor.transpose(ps[:, h, m * P:(m + 1) * P], Xm[:, 2 * h + m, :], ident[:])
                    tr.then_inc(sem("x1_turned"), 1)
                if ahead:
                    pe.wait_ge(sem("tokm_ready_0"), i + 1)
                    pe.wait_ge(sem("bonus_read"), i + 1)
                    turn_features(i + 1)
                    low_rank(i + 1)
                for lev in range(LEVELS):
                    Ml = (Ml0, Ml1)[lev % 2]
                    pe.wait_ge(sem("level_ready"), i * LEVELS + (lev + 1))
                    for h in range(2):
                        if lev:
                            pe.wait_ge(sem("level_added"), i * (2 * LEVELS) + (2 * lev + h - 1))
                        else:
                            pe.wait_ge(sem("t1_ready"), i * 2 + (h + 1))
                        for m in range(2):
                            mm = nc.tensor.matmul(ps[:, h, m * P:(m + 1) * P], Ml[:, 2 * h + m, :],
                                                  Tm[:, 2 * h + m, :], start=True, stop=True)
                        mm.then_inc(sem("y_made"), 1)
                    for h in range(2):
                        pe.wait_ge(sem("y_copied"), i * (2 * LEVELS) + (2 * lev + h + 1))
                        for m in range(2):
                            x, y = Xm[:, 2 * h + m, :], Ym[:, 2 * h + m, :]
                            if lev < LEVELS - 1:
                                nc.tensor.matmul(ps[:, 2 + h, m * P:(m + 1) * P], x, y, start=True, stop=True)
                            mm = nc.tensor.matmul(ps[:, 2 + h, S + m * P:S + (m + 1) * P], y, x, start=True, stop=True)
                        mm.then_inc(sem("level_made"), 1)
                    if ahead and lev == 2:
                        kk_sums(i + 1)
                for m in range(4):
                    h = slice(64 * (m % 2), 64 * (m % 2) + 64)
                    mm = nc.tensor.matmul(ps[:, 0, m * 64:(m + 1) * 64], Mm[:, m, 2, :], tokm[:, m // 2, 3, h],
                                          start=True, stop=True)
                mm.then_inc(sem("w0_made"), 1)
                pe.wait_ge(sem("level_added"), i * (2 * LEVELS) + 2 * LEVELS)
                for m in range(4):
                    h = slice(64 * (m % 2), 64 * (m % 2) + 64)
                    mm = nc.tensor.matmul(ps[h, 1, (m // 2) * P:(m // 2 + 1) * P], tokm[:, m // 2, 0, h], Xm[:, m, :],
                                          start=True, stop=True)
                mm.then_inc(sem("at_made"), 1)
                pe.wait_ge(sem("w0_ready"), i + 1)
                for m in range(4):
                    mm = nc.tensor.matmul(ps[:, 2, m * 64:(m + 1) * 64], Xm[:, m, :], Uu[:, m // 2, m % 2, :],
                                          start=True, stop=True)
                mm.then_inc(sem("w1_made"), 1)
                pe.wait_ge(sem("at_ready"), i + 1)
                for c in range(4):
                    t, rows = c // 2, slice(64 * (c % 2), 64 * (c % 2) + 64)
                    if c:
                        pe.wait_ge(sem("s_ready"), i * 6 + 2 * c)
                    nc.tensor.matmul(ps[:, 0, 0:P], AtT[:, t, :], snap[:, c, :], start=True, stop=True)\
                        .then_inc(sem("u_made"), 1)
                    pe.wait_ge(sem("u_ready"), i * 4 + (c + 1))
                    if c < 3:
                        nc.tensor.matmul(ps[:, 3, 0:P], tokm[rows, t, 1, :],
                                         Uu[rows, t, :, :].rearrange("p h n -> p (h n)"), start=True, stop=False)
                        nc.tensor.matmul(ps[:, 3, 0:P], tokm[rows, t, 2, :], tokm[rows, t, 3, :],
                                         start=False, stop=True).then_inc(sem("s_made"), 1)
                pe.wait_ge(sem("rT_ready"), i + 1)
                for t in range(TT):
                    for c in (2 * t, 2 * t + 1):
                        rows = slice(64 * (c % 2), 64 * (c % 2) + 64)
                        nc.tensor.matmul(ps[rows, 1, t * P:(t + 1) * P], rT[:, t, rows], snap[:, c, :],
                                         start=True, stop=False, skip_group_check=True)
                    for hd in range(2):
                        h = slice(64 * hd, 64 * hd + 64)
                        o = ps[:, 1, t * P + 64 * hd:t * P + 64 * hd + 64]
                        nc.tensor.matmul(o, Mm[:, 2 * t + hd, 1, :], Uu[:, t, hd, :], start=False, stop=False,
                                         skip_group_check=True)
                        mm = nc.tensor.matmul(o, Mm[:, 2 * t + hd, 3, :], tokm[:, t, 3, h], start=False, stop=True,
                                              skip_group_check=True)
                mm.then_inc(sem("y_out_made"), 1)

            turn_features(0)
            low_rank(0)
            kk_sums(0)
            with pe.Fori(0, 7) as i:
                pair(i, True)
            pair(7, False)

        block = ctx.enter_context(nc.Block())

        @block.sync
        def _(sp):
            for j in range(4):
                sp.dma_start(resid[:, :, j * CC:(j + 1) * CC], a["x"][0].rearrange("(t p) n -> p t n", p=P)
                             [:, :, j * CC:(j + 1) * CC]).then_inc(sem(f"x_loaded_{j}"), 16)
            for phase, n, per in STREAMS:
                if n:
                    with sp.Fori(0, n) as i:
                        for k in range(per):
                            stream(sp, i, phase, k)
                else:
                    for k in range(per):
                        stream(sp, 0, phase, k)
            for j in range(4):
                half, tok = j // 2, j % 2
                sp.wait_ge(sem("out_ready"), j + 1)
                sp.dma_start(out[0][tok * P:(tok + 1) * P, half * 1024:half * 1024 + 1024],
                             y2[:, tok, half * 1024:half * 1024 + 1024]).then_inc(sem("out_stored"), 16)
            sp.wait_ge(sem("out_stored"), 64)

        @block.gpsimd
        def _(pool):
            rel, buck = sem("rel_loaded"), sem("bucket_loaded")
            pool.dma_start(ident[:], a["ident"]).then_inc(sem("ident_loaded"), 16)
            pool.wait_ge(sem("x_loaded_3"), 16)
            pool.dma_start(pick_rel[:], a["pick_rel"].rearrange("(k p) n -> p k n", p=P)).then_inc(rel, 16)
            pool.dma_start(tableT[:], a["rel_bias_table_2"]).then_inc(buck, 16)
            pool.dma_start(pick_b[:], a["pick_bucket"]).then_inc(buck, 16)
            pool.dma_start(future[:], a["future"]).then_inc(buck, 16)
            pool.wait_ge(sem("rel_row_ready"), 1)
            pool.dma_start(rel_dram, rel_row[:]).then_inc(sem("rel_row_stored"), 16)
            pool.wait_ge(sem("buck_row_ready"), 1)
            pool.dma_start(buck_dram, buck_row[:]).then_inc(sem("buck_row_stored"), 16)
            pool.wait_ge(sem("rel_row_stored"), 16)
            pool.dma_start(rel_rows, rel_dram.partition_broadcast(P)).then_inc(sem("rel_rows_stored"), 16)
            pool.wait_ge(sem("buck_row_stored"), 16)
            pool.dma_start(buck_rows, buck_dram.partition_broadcast(P)).then_inc(sem("buck_rows_stored"), 16)
            pool.wait_ge(sem("rel_rows_stored"), 16)
            pool.wait_ge(sem("buck_rows_stored"), 16)
            pool.wait_ge(block_used, B_DOWN + SPLIT_SLOTS)
            pool.dma_start(fin_gain[:], a["norm_final"].partition_broadcast(P)).then_inc(sem("fin_gain_loaded"), 16)
            nsa = sem("nsa_loaded")
            pool.wait_ge(sem("square_sums"), 4 * TT)
            with nc.allow_non_contiguous_dma("positions, transposed"):
                for j, name in enumerate(("cmp_pos_k_2", "cmp_pos_v_2")):
                    pool.dma_start(posT[:, j, :], a[name][0].rearrange("t d -> d t")).then_inc(nsa, 16)
            for j, name in enumerate(("cmp_k_w2_2", "cmp_v_w2_2")):
                pool.dma_start(cw2[:, j, :], a[name][0]).then_inc(nsa, 16)
            rw = sem("rwkv_loaded")
            pool.wait_ge(sem("nsa_out_ready"), HN + 1)
            pool.wait_ge(block_used, B_WOUT2 + SPLIT_SLOTS)
            pool.dma_start(masks[:], a["masks"].rearrange("m p n -> p m n")).then_inc(rw, 16)
            pool.dma_start(l2[0:64, :], a["rwkv_w2_2"][0]).then_inc(rw, 16)
            pool.dma_start(l2[64:128, :], a["rwkv_a2_2"][0]).then_inc(rw, 16)
            def level(i, lev):
                if lev < 2:
                    pool.wait_ge(sem("m_masked"), i + 1)
                else:
                    pool.wait_ge(sem("level_made"), i * (2 * LEVELS) + 2 * (lev - 1))
                pool.tensor_tensor((Ml0, Ml1)[lev % 2][:], Mm[:, :, 0, :],
                                   masks[:, 5 + lev:6 + lev, :].broadcast_to([P, 4, P]), ALU.mult)\
                    .then_inc(sem("level_ready"), 1)

            pool.wait_ge(rw, 48)
            with pool.Fori(0, 8) as i:
                for lev in range(LEVELS):
                    level(i, lev)
            link = Chain(pool, "pool_chain")
            pool.wait_ge(sem("feat_staged"), 24)
            pool.dma_start(lnw, a["rwkv_ln_w_2"][0].partition_broadcast(P)).then_inc(sem("ln_loaded"), 16)
            pool.dma_start(lnb, a["rwkv_ln_b_2"][0].partition_broadcast(P)).then_inc(sem("ln_loaded"), 16)
            z_a, z_b = z2[:, :, C_ZA:C_ZA + 1024], z2[:, :, C_ZB:C_ZB + 1024]
            pool.wait_ge(sem("z_sig"), 2)
            link(pool.tensor_tensor(z_a, z_a, sig_a, ALU.mult))
            link(pool.tensor_tensor(oy[:, :, 0:1024], oy[:, :, 0:1024], z_a, ALU.mult))
            pool.wait_ge(sem("z_sig"), 4)
            link(pool.tensor_tensor(z_b, z_b, sig_b, ALU.mult))
            pool.wait_ge(sem("ln_loaded"), 32)
            link(pool.tensor_tensor(gain_gated, z_b, lnw.unsqueeze(1).broadcast_to([P, TT, 1024]), ALU.mult))
            pool.wait_ge(sem("bonus_ready"), 32)
            link(pool.tensor_tensor(shift_gated, bv[:], lnb.unsqueeze(1).broadcast_to([P, TT, 1024]), ALU.add))
            pool.tensor_tensor(shift_gated, shift_gated, z_b, ALU.mult).then_inc(sem("gates_applied"), 1)
            pool.wait_ge(turned_lo, 4 * KT)
            pool.dma_start(post_gain[:], a["post_norm_g_2"][0].partition_broadcast(P))\
                .then_inc(sem("post_gain_loaded"), 16)

        @block.scalar
        def _(act):
            link = Chain(act, "act_chain")

            act.dma_start(mix_rows[:], a["norm_mix"][0].rearrange("(k p) -> k p", p=P)).then_inc(sem("norm_mix_loaded"), 16)
            row = 0
            for name in ("norm_ffn", "pre_norm_g_2", "pool_scale", "rwkv_w0_2", "rwkv_a0_2",
                         "rwkv_k_k_2", "rwkv_k_a_2", "rwkv_r_k_2", "rwkv_mu_2"):
                v = a[name][0]
                if len(v.shape) == 2:
                    v = v.rearrange("h n -> (h n)")
                rows = v.shape[0] // P
                act.dma_start(par_rows[row:row + rows, :], v.rearrange("(k p) -> k p", p=P))\
                    .then_inc(sem("params_loaded"), 16)
                row += rows
            act.dma_start(rel_in[:], a["rel_bias"][0]).then_inc(sem("rel_bias_loaded"), 16)
            act.wait_ge(sem("params_ready"), 1)
            turned_to_hi(act, 0, 0, range(8))
            split_hi(act, B_WIN, 0, 0, 0)
            turned_to_hi(act, 0, 0, range(8, KT))
            split_hi(act, B_WIN, 0, 0, 1)
            for j in range(4):
                act.wait_ge(sem(f"x_loaded_{j}"), 16)
            rms_act(act, resid, scaled, 0)
            act.wait_ge(sem("rinv_ready"), 1)
            act.wait_ge(sem("params_ready"), 2)

            def store(dst, bank, col):
                def f(i):
                    nc.scalar.activation(dst[:, 0, bass.ds(i * 2 * CC + col, CC)], ps[:, bank, :], ACT.Copy,
                                         scale=rinv[:, 0, 0:1]).then_inc(drained[0], 1)
                return f

            def gates(bank, col):
                def f(i):
                    for tok in range(TT):
                        nc.scalar.activation(gate[:, tok, bass.ds(i * 2 * CC + (col - 4096), CC)],
                                             ps[:, bank + tok, :], ACT.Sigmoid, scale=rinv[:, 0, tok:tok + 1])\
                            .then_inc(drained[tok], 1)
                return f

            with act.Fori(0, 4) as i:
                product_steps(act, split_hi, B_WIN, 8, i, {3: store(qkvu, 0, 0), 7: store(qkvu, 2, CC)})
            act.wait_ge(sem("rel_row_stored"), 16)
            act.wait_ge(sem("buck_row_stored"), 16)
            for tok in range(TT):
                act.wait_ge(drained[tok], 2 + 8)
            act.wait_ge(sem("square_sums"), TT)
            act.wait_ge(sem("rel_rows_stored"), 16)

            def stage_k(n):
                nc.scalar.copy(kst[:], qkvu[:, :, bass.ds(n * P + 1024, P)]).then_inc(sem("k_staged"), 1)

            def begin(c):
                def f(i):
                    n = i * 2 + (c - 8)
                    act.wait_ge(sem("relb_used"), n + 1)
                    act.dma_start(relb[:], shifted(rel_rows, 256)[:, bass.ds(n * 2, 2), :])\
                        .then_inc(sem("relb_loaded"), 16)
                    if c == 0:
                        g = i - 4
                        act.wait_ge(sem("pool_mixed"), g + 1)
                        act.dma_start(rowp[:], a["pool_rows"][bass.ds(g, 1)]
                                      .rearrange("a (k p) n -> p (a k) n", p=P)).then_inc(sem("pool_loaded"), 16)
                        act.dma_start(pwg[:], a["pool_w"][0][bass.ds(g, 1)]
                                      .rearrange("a (k p) n -> p (a k) n", p=P)).then_inc(sem("pool_loaded"), 16)
                    act.wait_ge(sem("qk_turned"), n + 1)
                    nc.scalar.copy(qkT[:].rearrange("p x n -> p (x n)"), ps[:, T0, :]).then_inc(sem("qkT_ready"), 1)
                    nc.scalar.copy(vst[:], qkvu[:, :, bass.ds(n * P + 2048, P)]).then_inc(sem("v_staged"), 1)
                    if c == 0:
                        nc.scalar.copy(ust[:], qkvu[:, :, bass.ds(i * S + (3072 - 4 * S), S)])\
                            .then_inc(sem("u_staged"), 1)
                return f

            def exps(c, last):
                def f(i):
                    n = i * 2 + (c - 8)
                    if not last:
                        stage_k(n + 1)
                    act.wait_ge(sem("att_max"), n + 1)
                    for hd in range(2):
                        for qt in range(TT):
                            seg = prob[:, hd, 0:P] if qt == 0 else prob[:, hd, P:384]
                            e = 2 * qt + hd
                            nc.scalar.activation(seg, seg, ACT.Exp, bias=smax[:, e:e + 1],
                                                 accum_out=ssum[:, e:e + 1]).then_inc(sem("att_exp"), 1)
                return f

            def pooled(i):
                act.wait_ge(sem("pool_mixed"), i - 2)
                for e in range(2):
                    nc.scalar.activation(qkvu[:, e, bass.ds(i * S + (3072 - 4 * S), S)], ps[:, T0, e * S:(e + 1) * S],
                                         ACT.Copy, scale=pool_scale[:, bass.ds(i * 2 + (e - 8), 1)])\
                        .then_inc(sem("pool_stored"), 1)

            def probs_back(c):
                def f(i):
                    act.wait_ge(sem("probs_turned"), i * 2 + (c - 7))
                    nc.scalar.copy(probT[:, 0, :], ps[:, T2, 0:384]).then_inc(sem("pT_ready_0"), 1)
                return f

            def finish(c, bank):
                def f(i):
                    gates(bank, c * CC)(i)
                    act.wait_ge(sem("pv_done"), i * 2 + (c - 7))
                    nc.scalar.copy(qkvu[:, :, bass.ds(i * S + (c * P - 8 * P), P)],
                                   ps[:, T1, 0:S].rearrange("p (t n) -> p t n", t=TT)).then_inc(sem("att_stored"), 1)
                return f

            def with_attention(i, last):
                product_steps(act, split_hi, B_WIN, 8, i, {3: finish(0, 0), 7: finish(1, 2)},
                              {0: [begin(0)], 1: [exps(0, False)], 3: [probs_back(0)],
                               4: [begin(1)], 5: [exps(1, last)], 6: [pooled], 7: [probs_back(1)]})

            stage_k(0)
            with act.Fori(4, 7) as i:
                with_attention(i, False)
            with_attention(7, True)

            act.wait_ge(block_used, B_MERGE + SPLIT_SLOTS)
            act.wait_ge(sem("att_stored"), 9)
            act.wait_ge(sem("pool_stored"), 10)
            for j in range(4):
                dst, src = branch_inputs(xT_hi, j)
                nc.scalar.copy(dst, src).then_inc(sem("inputs_hi"), 1)

            def merged_hi(i, back):
                for j in range(4):
                    act.wait_ge(sem("merged_turned"), i * 4 + (j + 1 - 4 * back))
                    nc.scalar.copy(mT_hi[:, bass.ds(i * 4 + (j - 4 * back), 1), :].rearrange("p a n -> p (a n)")
                                   if not isinstance(i, int) else mT_hi[:, 4 * (i - back) + j, :],
                                   ps[:, T0 + j, 0:S]).then_inc(sem("merged_hi"), 1)

            product_steps(act, split_hi, B_MERGE, 4, 0, {})
            with act.Fori(1, 4) as i:
                product_steps(act, split_hi, B_MERGE, 4, i, {1: lambda i: merged_hi(i, 1)})
            merged_hi(4, 1)

            def turned_back(i):
                turned_to_hi(act, KT, 1, range(4 * i - 4, 4 * i))

            for c in range(4):
                product_steps(act, split_hi, B_WOUT, 4, c, {}, {3: [turned_back]} if c else {})

            turned_back(4)
            for tok in range(TT):
                act.wait_ge(drained[tok], 2 + Q_GU)
            rms_act(act, resid, scaled, 1)
            act.wait_ge(sem("rinv_ready"), 2)

            def sig(i):
                for tok in range(TT):
                    nc.scalar.activation(g_act[:, tok, :], ps[:, tok, :], ACT.Sigmoid, scale=rinv[:, 1, tok:tok + 1])\
                        .then_inc(sem("sig_ready"), 1)

            def hidden_back(i, back=1):
                act.wait_ge(sem("hidden_turned"), i + (1 - back))
                for j in range(2):
                    if isinstance(i, int):
                        dst = actT[:, 4 * (i - back) + 2 * j:4 * (i - back) + 2 * j + 2, :]
                    else:
                        dst = actT[:, bass.ds(i * 4 + (2 * j - 4 * back), 2), :]
                    nc.scalar.copy(dst, ps[:, T0 + j, :].rearrange("p (k n) -> p k n", k=2))\
                        .then_inc(sem("hidden_ready"), 1)

            product_steps(act, split_hi, B_GU, 8, 0, {3: sig})
            with act.Fori(1, 11) as i:
                product_steps(act, split_hi, B_GU, 8, i, {3: lambda i: (hidden_back(i), sig(i))})
            hidden_back(11)

            def stage_hi(i, k):
                if isinstance(i, int):
                    src = actT[:, 4 * i + k, :]
                else:
                    src = actT[:, bass.ds(i * 4 + k, 1), :].rearrange("p a n -> p (a n)")
                nc.scalar.copy(aT_hi[:, k % 2, :], src).then_inc(sem("hidden_hi"), 1)

            act.wait_ge(sem("hidden_ready"), 22)
            stage_hi(0, 0)
            stage_hi(0, 1)
            with act.Fori(0, 10) as i:
                for k in range(4):
                    split_hi(act, B_DOWN, 4, i, k + 2)
                    stage_hi(i, k + 2)
            for k in range(4):
                split_hi(act, B_DOWN, 4, 10, k + 2)
                if k < 2:
                    stage_hi(10, k + 2)

            for n in range(4):
                for tok in range(TT):
                    act.wait_ge(sem("down_added"), TT * n + tok + 1)
                    part = slice(n * CC, (n + 1) * CC)
                    sq = nc.scalar.activation(scaled[:, tok, part], resid[:, tok, part], ACT.Square,
                                              accum_out=sum_sq[:, tok, n:n + 1])
                    if n == 3:
                        sq.then_inc(sem("square_sums"), 1)
            root_act(act, 2)
            turned_to_hi(act, 2 * KT, 2)
            act.wait_ge(sem("final_normed"), 4)
            rms_act(act, resid, scaled, 3)
            act.wait_ge(sem("rinv_ready"), 4)

            def store2(bank, col, width=CC):
                def f(i):
                    dst = z2[:, 0, bass.ds(i * 2 * CC + col, width)]
                    nc.scalar.activation(dst, ps[:, bank, 0:width], ACT.Copy, scale=rinv[:, 1, 0:1])\
                        .then_inc(drained[0], 1)
                return f

            with act.Fori(0, LEAD2 // 2) as i:
                product_steps(act, split_hi, B_WIN2, 8, i, {3: store2(0, 0), 7: store2(2, CC)})

            for j in range(2):
                act.wait_ge(sem("keys_turned"), j + 1)
                nc.scalar.copy(KTs[:, j, :, :], ps[:, T0 + j, :].rearrange("p (g n) -> p g n", g=2))\
                    .then_inc(sem("keysT_ready"), 1)
            act.wait_ge(drained[0], 2 + Q_WIN2 + LEAD2)
            act.wait_ge(drained[1], 2 + Q_WIN2 + LEAD2)
            nc.scalar.activation(gsig[:, :, 0:16], z2[:, :, C_GATE + 8:C_GATE + 24], ACT.Exp, scale=-1.0)\
                .then_inc(sem("gate_exp"), 1)
            nc.scalar.activation(gsig[:, :, 16:24], z2[:, :, C_GATE:C_GATE + 8], ACT.Exp, scale=-1.0)\
                .then_inc(sem("gate_exp"), 1)
            for k in range(4):
                split_hi(act, B_CMP, 4, 0, k + 2)
            chunk_done(act, B_CMP, 4, 0, 3)
            nc.scalar.activation(hexp[:, :, 0:30], ps[:, 0:2, 0:30], ACT.Exp, scale=-1.0)\
                .then_inc(sem("hid_exp"), 1)
            act.wait_ge(sem("compressed"), 1)
            nc.scalar.copy(kcT[:, 0:30], ps[:, 2, 0:30]).then_inc(sem("kcT_ready"), 1)

            def begin(c):
                def f(i):
                    n = i * 2 + (c - LEAD2)
                    act.wait_ge(sem("nsa_bias_used"), n + 1)
                    act.dma_start(hbias[:].unsqueeze(1), shifted(buck_rows, 384)[:, bass.ds(n, 1), :])\
                        .then_inc(sem("nsa_bias_loaded"), 16)
                    act.wait_ge(sem("q2_turned"), n + 1)
                    nc.scalar.copy(q2T[:], ps[:, T0, 0:S]).then_inc(sem("q2T_ready"), 1)
                return f

            def exps(c):
                def f(i):
                    act.wait_ge(sem("nsa_max"), i * 2 + (c - LEAD2 + 1))
                    for b in range(3):
                        for qt in range(TT):
                            if b == 2:
                                seg = prc[:, qt, 0:NCMP]
                            else:
                                seg = pr[:, b, 0:P] if qt == 0 else pr[:, b, P:384]
                            nc.scalar.activation(seg, seg, ACT.Exp, bias=mx2[:, b, qt:qt + 1],
                                                 accum_out=sm2[:, b, qt:qt + 1]).then_inc(sem("nsa_exp"), 1)
                return f

            def probs_back(c):
                def f(i):
                    act.wait_ge(sem("probs2_turned"), i * 2 + (c - LEAD2 + 1))
                    nc.scalar.copy(pT2[:, 0, :], ps[:, T1, 0:384]).then_inc(sem("pT2_ready_0"), 1)
                    nc.scalar.copy(pcT[0:NCMP, :], ps[0:NCMP, T3, 0:S]).then_inc(sem("pT2_ready_0"), 1)
                return f

            def finish(c):
                def f(i):
                    n = i * 2 + (c - LEAD2)
                    store2(2 * c, c * CC)(i)
                    act.wait_ge(sem("pv2_done"), n + 1)
                    nc.scalar.copy(oy[:, :, bass.ds(n * P, P)],
                                   ps[:, T0, 0:S].rearrange("p (t n) -> p t n", t=TT))\
                        .then_inc(sem("nsa_out_ready"), 1)
                return f

            def with_nsa(i):
                product_steps(act, split_hi, B_WIN2 + 4, 8, i, {3: finish(0), 7: finish(1)},
                              {0: [begin(0)], 1: [exps(0)], 3: [probs_back(0)],
                               4: [begin(1)], 5: [exps(1)], 7: [probs_back(1)]})

            with act.Fori(3, 5) as i:
                with_nsa(i)
            with_nsa(5)
            with_nsa(6)
            product_steps(act, split_hi, B_WIN2 + 4, 8, 7, {3: store2(0, 0), 7: store2(2, CC, N2 - 15 * CC)})

            rwkv_act(act, link)

            def root(half):
                act.wait_ge(sem("gn_var"), half + 1)
                v = st16[:, 1, :, 8 * half:8 * half + 8]
                nc.scalar.activation(v, v, ACT.Sqrt).then_inc(sem("gn_root"), 1)

            act.wait_ge(sem("gates_applied"), 1)
            turned_to_hi(act, 3 * KT, None, range(8))
            root(0)
            for c in range(4):
                for k in range(4):
                    if 4 * c + k + 2 < 16:
                        split_hi(act, B_WOUT2, 4, c, k + 2)
                    if c == 0 and k == 0:
                        turned_to_hi(act, 3 * KT, None, range(8, 12))
                    if c == 0 and k == 1:
                        root(1)
                        turned_to_hi(act, 3 * KT, None, range(12, KT))
                chunk_done(act, B_WOUT2, 4, c, 3)
                for tok in range(TT):
                    if c:
                        act.wait_ge(sem("y2_squared"), TT * (c - 1) + tok + 1)
                    nc.scalar.activation(y2_sq[:, tok, :], ps[:, 2 * (c % 2) + tok, :], ACT.Square,
                                         accum_out=y2_sums[:, tok, c:c + 1]).then_inc(sem("y2_squared"), 1)
            root_act(act, 4)

        @block.vector
        def _(dve):
            link = Chain(dve, "dve_chain")
            dve.sem_inc(block_split, RAW_SLOTS)
            dve.sem_inc(block_used, SPLIT_SLOTS)
            dve.sem_inc(drained[0], 2)
            dve.sem_inc(drained[1], 2)
            dve.sem_inc(sem("relb_used"), 1)
            dve.sem_inc(sem("pool_mixed"), 1)
            dve.sem_inc(sem("pool_stored"), 2)
            dve.sem_inc(sem("att_stored"), 1)
            dve.sem_inc(sem("nsa_bias_used"), 1)
            dve.sem_inc(sem("pair_done"), 1)
            dve.sem_inc(sem("nsa_out_ready"), 1)

            dve.wait_ge(sem("params_turned"), 1)
            nc.vector.tensor_copy(per_feature[:, 0:KT], ps[:, 0, 0:KT]).then_inc(sem("params_ready"), 1)
            dve.wait_ge(sem("params_ready"), 1)
            turned_to_lo(dve, 0, 0, range(8))
            split_lo(dve, B_WIN, 0, 0, 0)
            turned_to_lo(dve, 0, 0, range(8, KT))
            split_lo(dve, B_WIN, 0, 0, 1)
            dve.wait_ge(sem("params_turned"), 2)
            nc.vector.tensor_copy(per_feature[:, KT:121], ps[:, 1, 0:121 - KT]).then_inc(sem("params_ready"), 1)
            dve.wait_ge(sem("params_ready"), 2)
            dve.wait_ge(sem("rel_turned"), 1)
            nc.vector.tensor_copy(relT[:, 0:2, :], ps[:, 2, 0:32].rearrange("p (k n) -> p k n", k=2))\
                .then_inc(sem("relT_ready"), 1)
            nc.vector.tensor_copy(relT[0:1, 2, :], ps[0:1, 2, 32:48]).then_inc(sem("relT_ready"), 1)
            dve.wait_ge(sem("rows_made"), 1)
            nc.vector.tensor_copy(rel_row[:], ps[0:16, T0, 0:384]).then_inc(sem("rel_row_ready"), 1)
            dve.wait_ge(sem("bucket_loaded"), 48)
            nc.vector.tensor_tensor(buck_row[:], ps[0:HN, T1, :], future[:], ALU.add).then_inc(sem("buck_row_ready"), 1)
            rms_dve(dve, link, 0)

            def store(bank, col):
                def f(i):
                    nc.vector.tensor_scalar(qkvu[:, 1, bass.ds(i * 2 * CC + col, CC)], ps[:, bank + 1, :],
                                            rinv[:, 0, 1:2], None, ALU.mult).then_inc(drained[1], 1)
                return f

            with dve.Fori(0, 4) as i:
                product_steps(dve, split_lo, B_WIN, 8, i, {3: store(0, 0), 7: store(2, CC)})
            for tok in range(TT):
                dve.wait_ge(drained[tok], 2 + 8)

            def stage_q(n):
                nc.vector.tensor_scalar(qst[:], qkvu[:, :, bass.ds(n * P, P)], 0.125, None, ALU.mult)\
                    .then_inc(sem("q_staged"), 1)

            def softmax(c, last):
                def f(i):
                    n = i * 2 + (c - 8)
                    dve.wait_ge(sem("scores_ready"), n + 1)
                    dve.wait_ge(sem("relb_loaded"), i * 32 + 16 * (c - 7))
                    link(nc.vector.memset(relb[0:64, :, 192:256], NEG))
                    link(nc.vector.tensor_tensor(prob[:, :, 0:P], ps[:, T2:T2 + 2, 0:P], relb[:, :, P:256], ALU.add))
                    nc.vector.tensor_tensor(prob[:, :, P:384], ps[:, T2:T2 + 2, P:384], relb[:], ALU.add)\
                        .then_inc(sem("relb_used"), 1)
                    dve.wait_ge(sem("relb_used"), n + 2)
                    link(nc.vector.tensor_reduce(smax[:, 0:2], prob[:, :, 0:P], AX, ALU.max))
                    link(nc.vector.tensor_reduce(smax[:, 2:4], prob[:, :, P:384], AX, ALU.max))
                    nc.vector.tensor_scalar(smax[:], smax[:], -1.0, None, ALU.mult).then_inc(sem("att_max"), 1)
                    if not last:
                        stage_q(n + 1)
                    dve.wait_ge(sem("att_exp"), i * 8 + 4 * (c - 7))
                    link(nc.vector.reciprocal(ssum[:], ssum[:]))
                    for hd in range(2):
                        for qt in range(TT):
                            seg = prob[:, hd, 0:P] if qt == 0 else prob[:, hd, P:384]
                            e = 2 * qt + hd
                            nc.vector.tensor_scalar(seg, seg, ssum[:, e:e + 1], None, ALU.mult)\
                                .then_inc(sem("probs_ready"), 1)
                return f

            def pool_means(i):
                dve.wait_ge(sem("pool_mean"), i - 3)
                nc.vector.tensor_copy(dT[:].rearrange("p x n -> p (x n)"), ps[:, T0, :]).then_inc(sem("dT_ready"), 1)

            def probs_back(c):
                def f(i):
                    dve.wait_ge(sem("probs_turned"), i * 2 + (c - 7))
                    nc.vector.tensor_copy(probT[:, 1, :], ps[:, T3, 0:384]).then_inc(sem("pT_ready_1"), 1)
                return f

            def with_attention(i, last):
                product_steps(dve, split_lo, B_WIN, 8, i, {},
                              {1: [softmax(0, False)], 2: [pool_means], 3: [probs_back(0)],
                               5: [softmax(1, last)], 7: [probs_back(1)]})

            stage_q(0)
            with link.loop(4, 7, 10) as i:
                with_attention(i, False)
            with_attention(7, True)

            for j in range(4):
                dve.wait_ge(sem("inputs_hi"), j + 1)
                dst, src = branch_inputs(xT_lo, j)
                hi, _ = branch_inputs(xT_hi, j)
                nc.vector.tensor_tensor(dst, src, hi.bitcast(F32), ALU.subtract).then_inc(sem("inputs_lo"), 1)

            def branch(i, which):
                buf = g_act if which == 0 else h_act
                if which == 0 and not isinstance(i, int):
                    dve.wait_ge(sem("merged_ready"), i)
                for tok in range(TT):
                    col = i * CC + which * D
                    src = gate[:, tok, col:col + CC] if isinstance(i, int) else gate[:, tok, bass.ds(col, CC)]
                    nc.vector.tensor_tensor(buf[:, tok, :], ps[:, 2 * which + tok, :], src, ALU.mult)\
                        .then_inc(drained[tok], 1)
                if which == 1:
                    for tok in range(TT):
                        dve.wait_ge(drained[tok], i * 2 + (Q_MERGE + 2 + 2))
                    nc.vector.tensor_tensor(m_tmp[:], g_act[:], h_act[:], ALU.add)\
                        .then_inc(sem("merged_ready"), 1)

            def merged_lo(i):
                for j in range(4):
                    dve.wait_ge(sem("merged_hi"), i * 4 + (j + 1 - 4))
                    if isinstance(i, int):
                        lo, hi = mT_lo[:, 4 * (i - 1) + j, :], mT_hi[:, 4 * (i - 1) + j, :]
                    else:
                        kt = bass.ds(i * 4 + (j - 4), 1)
                        lo, hi = (m[:, kt, :].rearrange("p a n -> p (a n)") for m in (mT_lo, mT_hi))
                    nc.vector.tensor_tensor(lo, ps[:, T0 + j, 0:S], hi.bitcast(F32), ALU.subtract)\
                        .then_inc(sem("merged_lo"), 1)

            product_steps(dve, split_lo, B_MERGE, 4, 0,
                          {1: lambda i: branch(i, 0), 3: lambda i: branch(i, 1)})
            with dve.Fori(1, 4) as i:
                product_steps(dve, split_lo, B_MERGE, 4, i,
                              {1: lambda i: (branch(i, 0), merged_lo(i)), 3: lambda i: branch(i, 1)})
            merged_lo(4)

            def add(i):
                for tok in range(TT):
                    x = resid[:, tok, i * CC:(i + 1) * CC]
                    nc.vector.tensor_tensor(x, x, ps[:, 2 * (i % 2) + tok, :], ALU.add).then_inc(drained[tok], 1)

            def turned_back(i):
                turned_to_lo(dve, KT, 1, range(4 * i - 4, 4 * i))

            for c in range(4):
                product_steps(dve, split_lo, B_WOUT, 4, c, {3: add}, {3: [turned_back]} if c else {})

            turned_back(4)
            rms_dve(dve, link, 1)

            def gated(i):
                for tok in range(TT):
                    dve.wait_ge(sem("sig_ready"), i * 2 + (tok + 1))
                    nc.vector.scalar_tensor_tensor(g_act[:, tok, :], ps[:, tok, :], rinv[:, 1, tok:tok + 1],
                                                   g_act[:, tok, :], ALU.mult, ALU.mult)\
                        .then_inc(drained[tok], 1)

            def hidden(i):
                for tok in range(TT):
                    dve.wait_ge(drained[tok], i * 2 + (Q_GU + 2 + 1))
                    nc.vector.scalar_tensor_tensor(h_act[:, tok, :], ps[:, 2 + tok, :], rinv[:, 1, tok:tok + 1],
                                                   g_act[:, tok, :], ALU.mult, ALU.mult)\
                        .then_inc(drained[tok], 1)

            with dve.Fori(0, 11) as i:
                product_steps(dve, split_lo, B_GU, 8, i, {3: gated, 7: hidden})

            def stage_lo(i, k):
                dve.wait_ge(sem("hidden_hi"), i * 4 + (k + 1))
                if isinstance(i, int):
                    src = actT[:, 4 * i + k, :]
                else:
                    src = actT[:, bass.ds(i * 4 + k, 1), :].rearrange("p a n -> p (a n)")
                nc.vector.tensor_tensor(aT_lo[:, k % 2, :], src, aT_hi[:, k % 2, :].bitcast(F32), ALU.subtract)\
                    .then_inc(sem("hidden_staged"), 1)

            stage_lo(0, 0)
            stage_lo(0, 1)
            with dve.Fori(0, 10) as i:
                for k in range(4):
                    split_lo(dve, B_DOWN, 4, i, k + 2)
                    stage_lo(i, k + 2)
            for k in range(4):
                split_lo(dve, B_DOWN, 4, 10, k + 2)
                if k < 2:
                    stage_lo(10, k + 2)
            chunk_done(dve, B_DOWN, 4, 10, 3)
            for n in range(4):
                for tok in range(TT):
                    x = resid[:, tok, n * CC:(n + 1) * CC]
                    nc.vector.tensor_tensor(x, x, ps[:, 2 * n + tok, :], ALU.add).then_inc(sem("down_added"), 1)
            dve.wait_ge(sem("down_added"), 8)
            for tok in range(TT):
                dve.sem_inc(drained[tok], 2)

            rms_dve(dve, link, 2, sum_sq)
            dve.wait_ge(sem("fin_gain_loaded"), 16)
            for half in (slice(0, 1024), slice(1024, D)):
                for tok in range(TT):
                    x = resid[:, tok, half]
                    nc.vector.scalar_tensor_tensor(x, x, rinv[:, 0, tok:tok + 1], fin_gain[:, half], ALU.mult,
                                                   ALU.mult).then_inc(sem("final_normed"), 1)
            turned_to_lo(dve, 2 * KT, 2)
            rms_dve(dve, link, 3)

            def store2(bank, col, width=CC):
                def f(i):
                    dst = z2[:, 1, bass.ds(i * 2 * CC + col, width)]
                    nc.vector.tensor_scalar(dst, ps[:, bank + 1, 0:width], rinv[:, 1, 1:2], None, ALU.mult)\
                        .then_inc(drained[1], 1)
                return f

            with dve.Fori(0, LEAD2 // 2) as i:
                product_steps(dve, split_lo, B_WIN2, 8, i, {3: store2(0, 0), 7: store2(2, CC)})

            for j in range(2):
                dve.wait_ge(sem("keys_turned"), j + 3)
                link(nc.vector.tensor_copy(kvcT[:, j, :, :], ps[:, T2 + j, :].rearrange("p (g n) -> p g n", g=2)))
            dve.wait_ge(sem("nsa_loaded"), 64)
            for kv, (hi, lo) in enumerate(((A_hi, A_lo), (A_hi2, A_lo2))):
                for g in range(2):
                    pos = posT[:, kv, :].unsqueeze(2).broadcast_to([P, 32, NCMP])
                    link(nc.vector.tensor_tensor(blkA[:, :, g * NCMP:(g + 1) * NCMP], windows(kv, g), pos, ALU.add))
                link(nc.vector.tensor_copy(hi[:], blkA[:]))
                link(nc.vector.tensor_tensor(lo[:], blkA[:], hi[:].bitcast(F32), ALU.subtract))
            dve.sem_inc(sem("windows_ready"), 1)
            dve.wait_ge(sem("gate_exp"), 2)
            link(nc.vector.tensor_scalar(gsig[:], gsig[:], 1.0, None, ALU.add))
            link(nc.vector.reciprocal(gsig[:], gsig[:]))
            for k in range(4):
                split_lo(dve, B_CMP, 4, 0, k + 2)
            dve.wait_ge(sem("hid_exp"), 1)
            link(nc.vector.tensor_scalar(hexp[:, :, 0:30], hexp[:, :, 0:30], 1.0, None, ALU.add))
            link(nc.vector.reciprocal(hexp[:, :, 0:30], hexp[:, :, 0:30]))
            nc.vector.tensor_tensor(hid[:, :, 0:30], ps[:, 0:2, 0:30], hexp[:, :, 0:30], ALU.mult)\
                .then_inc(sem("hid_ready"), 1)
            dve.wait_ge(sem("compressed"), 1)
            link(nc.vector.tensor_copy(vc[0:NCMP, :, :], ps[0:NCMP, 3, 0:256].rearrange("p (g n) -> p g n", g=2)))
            dve.sem_inc(sem("vc_ready"), 1)

            def stage_q2(n):
                nc.vector.tensor_scalar(q2[:], z2[:, :, bass.ds(n * P, P)], float(P) ** -0.5, None, ALU.mult)\
                    .then_inc(sem("q2_staged"), 1)

            def softmaxes(c, last):
                def f(i):
                    n = i * 2 + (c - LEAD2)
                    dve.wait_ge(sem("scores2_ready"), n + 1)
                    dve.wait_ge(sem("nsa_bias_loaded"), n * 16 + 16)
                    for b in range(2):
                        link(nc.vector.tensor_tensor(pr[:, b, 0:P], ps[:, T1 + b, 0:P], hbias[:, P:256], ALU.add))
                        link(nc.vector.tensor_tensor(pr[:, b, P:384], ps[:, T1 + b, P:384], hbias[:, 0:256], ALU.add))
                    for qt in range(TT):
                        d = 159 - P * qt
                        ins = nc.vector.tensor_tensor(prc[:, qt, 0:NCMP], ps[:, T3, 16 * qt:16 * qt + NCMP],
                                                      hbias[:, d:d + 16 * NCMP - 15:16], ALU.add)
                        if qt == 0:
                            link(ins)
                    ins.then_inc(sem("nsa_bias_used"), 1)
                    dve.wait_ge(sem("nsa_bias_used"), n + 2)
                    link(nc.vector.tensor_reduce(mx2[:, 0:2, 0], pr[:, :, 0:P], AX, ALU.max))
                    link(nc.vector.tensor_reduce(mx2[:, 0:2, 1], pr[:, :, P:384], AX, ALU.max))
                    link(nc.vector.tensor_reduce(mx2[:, 2, :], prc[:, :, 0:NCMP], AX, ALU.max))
                    nc.vector.tensor_scalar(mx2[:], mx2[:], 0.9 * NEG, -1.0, ALU.max, ALU.mult)\
                        .then_inc(sem("nsa_max"), 1)
                    if not last:
                        stage_q2(n + 1)
                    dve.wait_ge(sem("nsa_exp"), n * 6 + 6)
                    nc.vector.tensor_scalar(sm2[:], sm2[:], 1e-30, None, ALU.max).then_inc(sem("sums_kept"), 1)
                    dve.wait_ge(sem("sums_kept"), n + 1)
                    link(nc.vector.reciprocal(sm2[:], sm2[:]))
                    gs = gsig[:].rearrange("p t (b h) -> p b t h", b=3)[:, :, :, bass.ds(n, 1)]
                    link(nc.vector.tensor_tensor(sm2[:], sm2[:], gs.rearrange("p b t a -> p b (t a)"), ALU.mult))
                    for b in range(3):
                        for qt in range(TT):
                            if b == 2:
                                seg = prc[:, qt, 0:NCMP]
                            else:
                                seg = pr[:, b, 0:P] if qt == 0 else pr[:, b, P:384]
                            nc.vector.tensor_scalar(seg, seg, sm2[:, b, qt:qt + 1], None, ALU.mult)\
                                .then_inc(sem("probs2_ready"), 1)
                return f

            def probs_back(c):
                def f(i):
                    dve.wait_ge(sem("probs2_turned"), i * 2 + (c - LEAD2 + 1))
                    nc.vector.tensor_copy(pT2[:, 1, :], ps[:, T2, 0:384]).then_inc(sem("pT2_ready_1"), 1)
                return f

            def with_nsa(i, last):
                product_steps(dve, split_lo, B_WIN2 + 4, 8, i, {3: store2(0, 0), 7: store2(2, CC)},
                              {1: [softmaxes(0, False)], 3: [probs_back(0)],
                               5: [softmaxes(1, last)], 7: [probs_back(1)]})

            stage_q2(0)
            with link.loop(3, 5, 20) as i:
                with_nsa(i, False)
            with_nsa(5, False)
            with_nsa(6, True)
            product_steps(dve, split_lo, B_WIN2 + 4, 8, 7, {3: store2(0, 0), 7: store2(2, CC, N2 - 15 * CC)})

            rwkv_dve(dve, link)

            dve.wait_ge(sem("pair_done"), 8 + 1)
            turned_to_lo(dve, 3 * KT, None, range(8))
            dve.wait_ge(sem("gates_applied"), 1)
            group_norm(dve, link, 0)
            for c in range(4):
                for k in range(4):
                    if 4 * c + k + 2 < 16:
                        split_lo(dve, B_WOUT2, 4, c, k + 2)
                    if c == 0 and k == 0:
                        turned_to_lo(dve, 3 * KT, None, range(8, 12))
                    if c == 0 and k == 1:
                        group_norm(dve, link, 1)
                        turned_to_lo(dve, 3 * KT, None, range(12, KT))
                if c == 0:
                    dve.wait_ge(sem("post_gain_loaded"), 16)
                for tok in range(TT):
                    dve.wait_ge(sem("y2_squared"), TT * c + tok + 1)
                    part = slice(c * CC, (c + 1) * CC)
                    nc.vector.tensor_tensor(y2[:, tok, part], ps[:, 2 * (c % 2) + tok, :], post_gain[:, part],
                                            ALU.mult).then_inc(drained[tok], 1)
            link(nc.vector.tensor_reduce(stats[:, 0:2], y2_sums[:], AX, ALU.add))
            nc.vector.tensor_scalar(stats[:, 0:2], stats[:, 0:2], 1.0 / D, EPS, ALU.mult, ALU.add)\
                .then_inc(sem("mean_squares"), 1)
            dve.wait_ge(sem("rms_roots"), 5)
            link(nc.vector.reciprocal(rinv[:, 0, :], stats[:, 2:4]))
            for tok in range(TT):
                dve.wait_ge(drained[tok], 2 + Q_WOUT2 + 4)
            for half in (slice(0, 1024), slice(1024, D)):
                for tok in range(TT):
                    nc.vector.scalar_tensor_tensor(y2[:, tok, half], y2[:, tok, half], rinv[:, 0, tok:tok + 1],
                                                   resid[:, tok, half], ALU.mult, ALU.add)\
                        .then_inc(sem("out_ready"), 1)

        @block.tensor
        def _(pe):
            pe.wait_ge(sem("ident_loaded"), 16)
            pe.wait_ge(sem("norm_mix_loaded"), 16)
            nc.tensor.transpose(ps[:, 0, 0:KT], mix_rows[:], ident[0:KT, 0:KT]).then_inc(sem("params_turned"), 1)
            for j in range(4):
                pe.wait_ge(sem(f"x_loaded_{j}"), 16)
                turn_rows(pe, resid, 0, range(4 * j, 4 * j + 4))
            pe.wait_ge(sem("params_loaded"), 144)
            n = 121 - KT
            nc.tensor.transpose(ps[:, 1, 0:n], par_rows[:], ident[0:n, 0:n]).then_inc(sem("params_turned"), 1)
            pe.wait_ge(sem("rel_bias_loaded"), 16)
            for j in range(3):
                n = min(P, 2 * REL + 1 - j * P)
                tr = nc.tensor.transpose(ps[0:n, 2, 16 * j:16 * j + 16], rel_in[:, j * P:j * P + n], ident[0:16, 0:16])
            tr.then_inc(sem("rel_turned"), 1)
            pe.wait_ge(sem("rel_loaded"), 16)
            pe.wait_ge(sem("relT_ready"), 2)
            pe.wait_ge(turned_lo, KT)
            for j in range(3):
                n = min(P, 2 * REL + 1 - j * P)
                nc.tensor.matmul(ps[0:16, T0, 0:384], relT[0:n, j, :], pick_rel[0:n, j, :], start=j == 0, stop=j == 2)
            pe.wait_ge(sem("bucket_loaded"), 48)
            nc.tensor.matmul(ps[0:HN, T1, :], tableT[:], pick_b[:], start=True, stop=True).then_inc(sem("rows_made"), 1)

            pe.wait_ge(sem("relT_ready"), 2)
            plain_product(pe, B_WIN, Q_WIN, 4, xT_hi, xT_lo)

            def turn_qk(i, c):
                n = i * 2 + (c - 8)
                pe.wait_ge(sem("q_staged"), n + 1)
                pe.wait_ge(sem("k_staged"), n + 1)
                if c == 0:
                    pe.wait_ge(sem("pool_stored"), i * 2 - 6)
                else:
                    pe.wait_ge(sem("dT_ready"), i - 3)
                for x, src in enumerate((qst, kst)):
                    for tok in range(TT):
                        o = x * S + tok * P
                        tr = nc.tensor.transpose(ps[:, T0, o:o + P], src[:, tok, :], ident[:])
                tr.then_inc(sem("qk_turned"), 1)

            def scores(i, c):
                pe.wait_ge(sem("qkT_ready"), i * 2 + (c - 7))
                for hd in range(2):
                    h = slice(64 * hd, 64 * hd + 64)
                    nc.tensor.matmul(ps[:, T2 + hd, 0:P], qkT[h, 0, 0:P], qkT[h, 1, 0:P], start=True, stop=True)
                    mm = nc.tensor.matmul(ps[:, T2 + hd, P:384], qkT[h, 0, P:S], qkT[h, 1, :], start=True, stop=True)
                mm.then_inc(sem("scores_ready"), 1)

            def turn_probs(i, c):
                pe.wait_ge(sem("probs_ready"), i * 8 + 4 * (c - 7))
                for hd in range(2):
                    for j in range(3):
                        tr = nc.tensor.transpose(ps[:, T2 + hd, j * P:(j + 1) * P],
                                                 prob[:, hd, j * P:(j + 1) * P], ident[:])
                tr.then_inc(sem("probs_turned"), 1)

            def values(i, c):
                n = i * 2 + (c - 8)
                pe.wait_ge(sem("pT_ready_0"), n + 1)
                pe.wait_ge(sem("pT_ready_1"), n + 1)
                pe.wait_ge(sem("v_staged"), n + 1)
                pe.wait_ge(sem("att_stored"), n + 1)
                for hd in range(2):
                    h = slice(64 * hd, 64 * hd + 64)
                    nc.tensor.matmul(ps[h, T1, 0:S], vst[:, 0, h], probT[:, hd, 0:S], start=True, stop=False)
                    mm = nc.tensor.matmul(ps[h, T1, P:S], vst[:, 1, h], probT[:, hd, S:384], start=False, stop=True)
                mm.then_inc(sem("pv_done"), 1)

            def pool_mean(i):
                pe.wait_ge(sem("u_staged"), i - 3)
                pe.wait_ge(sem("pool_loaded"), i * 32 - 96)
                for x in range(2):
                    for t in range(TT):
                        mm = nc.tensor.matmul(ps[:, T0, x * S:(x + 1) * S], ust[:, t, x * P:(x + 1) * P], rowp[:, t, :],
                                              start=t == 0, stop=t == 1)
                mm.then_inc(sem("pool_mean"), 1)

            def pool_mix(i):
                for e in range(2):
                    for x in range(2):
                        mm = nc.tensor.matmul(ps[:, T0, e * S:(e + 1) * S], pwg[:, x, e * P:(e + 1) * P], dT[:, x, :],
                                              start=x == 0, stop=x == 1)
                mm.then_inc(sem("pool_mixed"), 1)

            def between(i, c, k):
                if k == 0:
                    turn_qk(i, c)
                elif k == 1:
                    scores(i, c)
                elif k == 2:
                    (pool_mean, pool_mix)[c](i)
                elif k == 3:
                    turn_probs(i, c)
                else:
                    values(i, c)

            plain_product(pe, B_WIN, Q_WIN, 8, xT_hi, xT_lo, 4, between)

            def branches(i, ks, lead=0):
                for k in ks:
                    if k % 2 == 0:
                        acc_free(pe, Q_MERGE + k // 2, i, 2)
                    mm_block(pe, B_MERGE, 4, i, k, xT_hi, xT_lo, 4 * (k % 4), k % 4 // 2 * 2,
                             k % 2 == 0, k % 2 == 1)

            def turn_merged(i):
                pe.wait_ge(sem("merged_ready"), i + 1)
                for j in range(4):
                    for tok in range(TT):
                        tr = nc.tensor.transpose(ps[:, T0 + j, tok * P:(tok + 1) * P],
                                                 m_tmp[:, tok, j * P:(j + 1) * P], ident[:])
                    tr.then_inc(sem("merged_turned"), 1)

            pe.wait_ge(sem("inputs_lo"), 2)
            branches(0, (0, 1))
            pe.wait_ge(sem("inputs_lo"), 4)
            with pe.Fori(0, 3) as i:
                branches(i, (2, 3, 4, 5))
                turn_merged(i)
            branches(3, (2, 3))
            turn_merged(3)

            def turn_sums(c):
                for tok in range(TT):
                    pe.wait_ge(drained[tok], 2 + Q_WOUT + c + 1)
                turn_rows(pe, resid, KT, range(4 * c, 4 * c + 4))

            pe.wait_ge(sem("merged_lo"), KT)
            for c in range(4):
                acc_free(pe, Q_WOUT + c)
                for k in range(4):
                    if c and k == 2:
                        turn_sums(c - 1)
                    mm_block(pe, B_WOUT, 4, c, k, mT_hi, mT_lo, 4 * k, c % 2 * 2, k == 0, k == 3)

            turn_sums(3)

            def up_gate(i, ks):
                for k in ks:
                    if k % 4 == 0:
                        acc_free(pe, Q_GU + k // 4, i, 2)
                    mm_block(pe, B_GU, 8, i, k, xT_hi, xT_lo, 4 * (k % 4), k % 8 // 4 * 2,
                             k % 4 == 0, k % 4 == 3)

            def turn_hidden(i):
                for tok in range(TT):
                    pe.wait_ge(drained[tok], i * 2 + (Q_GU + 2 + 2))
                for j in range(4):
                    for tok in range(TT):
                        c = j % 2 * S + tok * P
                        tr = nc.tensor.transpose(ps[:, T0 + j // 2, c:c + P],
                                                 h_act[:, tok, j * P:(j + 1) * P], ident[:])
                tr.then_inc(sem("hidden_turned"), 1)

            pe.wait_ge(turned_lo, 2 * KT)
            up_gate(0, (0, 1))
            with pe.Fori(0, 10) as i:
                up_gate(i, range(2, 10))
                turn_hidden(i)
            up_gate(10, range(2, 8))
            turn_hidden(10)

            def down_block(i, k, start, stop):
                pe.wait_ge(sem("hidden_staged"), i * 4 + (k + 1))
                pe.wait_ge(block_split, i * 4 + (B_DOWN + k + 1 + RAW_SLOTS))
                for tok in range(TT):
                    xh = aT_hi[:, k % 2, tok * P:(tok + 1) * P]
                    xl = aT_lo[:, k % 2, tok * P:(tok + 1) * P]
                    for n in range(4):
                        wh = w_hi[:, k % 2, n * CC:(n + 1) * CC]
                        wl = w_lo[:, k % 2, n * CC:(n + 1) * CC]
                        o = ps[:, 2 * n + tok, :]
                        nc.tensor.matmul(o, xh, wh, start=start, stop=False)
                        nc.tensor.matmul(o, xh, wl, start=False, stop=False)
                        mm = nc.tensor.matmul(o, xl, wh, start=False, stop=stop)
                mm.then_inc(block_used, 1)

            acc_free(pe, Q_DOWN + 1)
            for k in range(4):
                down_block(0, k, k == 0, False)
            with pe.Fori(1, 10) as i:
                for k in range(4):
                    down_block(i, k, False, False)
            for k in range(4):
                down_block(10, k, False, k == 3)

            pe.wait_ge(sem("down_added"), 8)
            for half in range(2):
                pe.wait_ge(sem("final_normed"), 2 * half + 2)
                turn_rows(pe, resid, 2 * KT, range(8 * half, 8 * half + 8))

            pe.wait_ge(turned_lo, 3 * KT)
            plain_product(pe, B_WIN2, Q_WIN2, LEAD2 // 2, xT_hi, xT_lo)

            for tok in range(TT):
                pe.wait_ge(drained[tok], 2 + Q_WIN2 + LEAD2)
            for j, cols_ in enumerate((C_KS, C_KW, C_KC, C_VC)):
                for g in range(2):
                    for tok in range(TT):
                        tr = nc.tensor.transpose(ps[:, T0 + j, g * S + tok * P:g * S + (tok + 1) * P],
                                                 z2[:, tok, cols_ + g * P:cols_ + (g + 1) * P], ident[:])
                tr.then_inc(sem("keys_turned"), 1)
            pe.wait_ge(sem("windows_ready"), 1)
            for k in range(4):
                kv = k // 2
                hi, lo = ((A_hi, A_lo), (A_hi2, A_lo2))[kv]
                pe.wait_ge(block_split, B_CMP + k + 1 + RAW_SLOTS)
                for t in range(16):
                    wh = w_hi[:, k % 2, t * P:(t + 1) * P]
                    wl = w_lo[:, k % 2, t * P:(t + 1) * P]
                    p = 16 * (k % 2) + t
                    o = ps[:, kv, 0:30]
                    nc.tensor.matmul(o, wh, hi[:, p, :], start=p == 0, stop=False)
                    nc.tensor.matmul(o, wh, lo[:, p, :], start=False, stop=False)
                    mm = nc.tensor.matmul(o, wl, hi[:, p, :], start=False, stop=p == 31)
                mm.then_inc(block_used, 1)
            pe.wait_ge(sem("hid_ready"), 1)
            nc.tensor.matmul(ps[:, 2, 0:30], cw2[:, 0, :], hid[:, 0, 0:30], start=True, stop=True)
            for g in range(2):
                mm = nc.tensor.matmul(ps[0:NCMP, 3, g * P:(g + 1) * P], hid[:, 1, g * NCMP:(g + 1) * NCMP],
                                      cw2[:, 1, :], start=True, stop=True)
            mm.then_inc(sem("compressed"), 1)

            pe.wait_ge(sem("kcT_ready"), 1)
            pe.wait_ge(sem("vc_ready"), 1)
            pe.wait_ge(sem("keysT_ready"), 2)

            def turn_q2(n):
                pe.wait_ge(sem("q2_staged"), n + 1)
                pe.wait_ge(sem("nsa_out_ready"), n + 1)
                for tok in range(TT):
                    tr = nc.tensor.transpose(ps[:, T0, tok * P:(tok + 1) * P], q2[:, tok, :], ident[:])
                tr.then_inc(sem("q2_turned"), 1)

            def scores2(n, g):
                pe.wait_ge(sem("q2T_ready"), n + 1)
                for qt in range(TT):
                    q = q2T[:, qt * P:(qt + 1) * P]
                    for b in range(2):
                        o = ps[:, T1 + b, 0:P] if qt == 0 else ps[:, T1 + b, P:384]
                        nc.tensor.matmul(o, q, KTs[:, b, g, 0:P] if qt == 0 else KTs[:, b, g, :],
                                         start=True, stop=True)
                    mm = nc.tensor.matmul(ps[:, T3, 16 * qt:16 * qt + NCMP], q,
                                          kcT[:, g * NCMP:(g + 1) * NCMP], start=True, stop=True)
                mm.then_inc(sem("scores2_ready"), 1)

            def turn_probs2(n):
                pe.wait_ge(sem("probs2_ready"), n * 6 + 6)
                for b in range(2):
                    for j in range(3):
                        nc.tensor.transpose(ps[:, T1 + b, j * P:(j + 1) * P], pr[:, b, j * P:(j + 1) * P], ident[:])
                for qt in range(TT):
                    tr = nc.tensor.transpose(ps[0:NCMP, T3, qt * P:(qt + 1) * P], prc[:, qt, 0:NCMP], ident[:])
                tr.then_inc(sem("probs2_turned"), 1)

            def values2(n, g):
                pe.wait_ge(sem("pT2_ready_0"), n * 2 + 2)
                pe.wait_ge(sem("pT2_ready_1"), n + 1)
                for qt in range(TT):
                    o = ps[:, T0, qt * P:(qt + 1) * P]
                    for b, c in enumerate((C_VS, C_VW)):
                        for j in range(qt + 1):
                            seg = (0, P, 2 * P)[qt + j]
                            nc.tensor.matmul(o, pT2[:, b, seg:seg + P], z2[:, j, c + g * P:c + (g + 1) * P],
                                             start=b == 0 and j == 0, stop=False)
                    mm = nc.tensor.matmul(o, pcT[0:NCMP, qt * P:(qt + 1) * P], vc[0:NCMP, g, :],
                                          start=False, stop=True)
                mm.then_inc(sem("pv2_done"), 1)

            def between2(g):
                def f(i, c, k):
                    n = i * 2 + (c - LEAD2)
                    if k == 0:
                        turn_q2(n)
                    elif k == 1:
                        scores2(n, g)
                    elif k == 3:
                        turn_probs2(n)
                    elif k == 4:
                        values2(n, g)
                return f

            for g in range(2):
                plain_product(pe, B_WIN2 + 4, Q_WIN2, 5 + 2 * g, xT_hi, xT_lo, 3 + 2 * g, between2(g))
            for c, width in ((14, CC), (15, N2 - 15 * CC)):
                acc_free(pe, Q_WIN2 + c)
                for k in range(4):
                    mm_block(pe, B_WIN2 + 4 + 4 * c, 4, 0, k, xT_hi, xT_lo, 4 * k, 2 * (c % 2), k == 0, k == 3, width)

            rwkv_pe(pe)

            pe.wait_ge(sem("gates_applied"), 1)
            turn_rows(pe, oy, 3 * KT, range(8))
            pe.wait_ge(turned_lo, 3 * KT + 8)
            for c in range(4):
                acc_free(pe, Q_WOUT2 + c)
                for k in range(4):
                    if c == 0 and k >= 2:
                        pe.wait_ge(sem("gn_done"), k - 1)
                        turn_rows(pe, oy, 3 * KT, range(4 * k, 4 * k + 4))
                        pe.wait_ge(turned_lo, 3 * KT + 4 * k + 4)
                    mm_block(pe, B_WOUT2, 4, c, k, xT_hi, xT_lo, 4 * k, 2 * (c % 2), k == 0, k == 3)


INPUTS = ("x", "norm_mix", "w_in", "rel_bias", "pool_w", "pool_scale", "w_branch_a", "w_branch_b", "w_out",
          "norm_ffn", "w_gate_up", "w_down", "norm_final", "pre_norm_g_2", "w_in_2", "rel_bias_table_2",
          "cmp_pos_k_2", "cmp_pos_v_2", "cmp_k_w1_2", "cmp_k_w2_2", "cmp_v_w1_2", "cmp_v_w2_2", "rwkv_mu_2",
          "rwkv_w0_2", "rwkv_w2_2", "rwkv_a0_2", "rwkv_a2_2", "rwkv_k_k_2", "rwkv_k_a_2", "rwkv_r_k_2",
          "rwkv_ln_w_2", "rwkv_ln_b_2", "w_out_2", "post_norm_g_2")


def kernel(**inputs):
    import numpy as _np
    import concourse.bacc as _bacc
    from concourse.bass_utils import run_bass_kernel_spmd as _run

    nc = _bacc.Bacc("TRN2", target_bir_lowering=False, num_devices=1)
    arrays, aps = {}, {}
    given = {name: _np.ascontiguousarray(inputs[name]) for name in INPUTS}
    for name, value in list(given.items()) + list(shape_constants().items()):
        arrays[f"in_{name}"] = value
        aps[name] = nc.dram_tensor(f"in_{name}", value.shape, F32, kind="ExternalInput").ap()
    out = nc.dram_tensor("out", (1, S, D), F32, kind="ExternalOutput").ap()
    program(nc, aps, out)
    r = _run(nc, [arrays], core_ids=[0])
    return r.results[0]["out"]
```
